# Optimizing a Trainium2 kernel written in Bass

```python
import jax, jax.numpy as jnp
from jax import lax
import numpy as np

D_MODEL = 1024
BATCH = 1
SEQ = 512
DEPTH = 1
DEC_BATCH = 1
DEC_SEQ = 64
PAST_LEN = 256

CHUNK = 64
GLA_HEADS = 4
GLA_DK = 64
GLA_DV = 128
GLA_LOWRANK = 16
GLA_TAU = 16.0
GLA_BLOCK = 16
ATT_HEADS = 8
ATT_KV_HEADS = 2
ATT_HD = 64
IDX_HEADS = 4
IDX_DIM = 64
TOPK_MAX = 256
D_FF = 2816
EPS = 1e-6

GLA_QK = GLA_HEADS * GLA_DK
GLA_V = GLA_HEADS * GLA_DV
ATT_Q = ATT_HEADS * ATT_HD
ATT_KV = ATT_KV_HEADS * ATT_HD
MIX_WIDTH = GLA_V + ATT_Q
IN_WIDTH = 2 * GLA_QK + GLA_V + GLA_LOWRANK + GLA_V + ATT_Q + 2 * ATT_KV + IDX_HEADS * IDX_DIM + IDX_DIM + IDX_HEADS

kernel_name = 'hybrid_gla_dsa_macaron_stream_step'

def _split_points():
    sizes = (GLA_QK, GLA_QK, GLA_V, GLA_LOWRANK, GLA_V, ATT_Q, ATT_KV, ATT_KV, IDX_HEADS * IDX_DIM, IDX_DIM, IDX_HEADS)
    pts, acc = [], 0
    for s in sizes[:-1]:
        acc += s
        pts.append(acc)
    return pts

def _alibi_slopes():
    return jnp.asarray([2.0 ** (-8.0 * (h + 1) / ATT_HEADS) for h in range(ATT_HEADS)], jnp.float32)

def _rmsnorm(x, g):
    xf = x.astype(jnp.float32)
    y = xf * lax.rsqrt(jnp.mean(xf * xf, axis=-1, keepdims=True) + EPS)
    return (y * g.astype(jnp.float32)).astype(x.dtype)

def _swiglu(h, w_gate, w_up, w_down):
    return (jax.nn.silu(h @ w_gate) * (h @ w_up)) @ w_down

def _gla_recurrence(q, k, v, log_a, s0):
    B, L, H, _ = q.shape
    DV = v.shape[-1]
    C = GLA_BLOCK
    pad = (-L) % C
    f32 = jnp.float32
    padw = ((0, 0), (0, pad), (0, 0), (0, 0))
    q, k, v, log_a = (jnp.pad(t.astype(f32), padw) for t in (q, k, v, log_a))
    n = (L + pad) // C

    def to_blocks(t):
        return t.reshape(B, n, C, H, t.shape[-1]).transpose(1, 0, 3, 2, 4)

    qb, kb, vb, gb = (to_blocks(t) for t in (q, k, v, log_a))
    bb = jnp.cumsum(gb, axis=3)
    causal = jnp.tril(jnp.ones((C, C), dtype=bool))

    def step(S, blk):
        qc, kc, vc, bc = blk
        tot = bc[:, :, -1:, :]
        q_dec = qc * jnp.exp(bc)
        k_dec = kc * jnp.exp(-bc)
        k_end = kc * jnp.exp(tot - bc)
        A = jnp.where(causal, jnp.einsum('bhtk,bhsk->bhts', q_dec, k_dec), 0.0)
        o = jnp.einsum('bhtk,bhkv->bhtv', q_dec, S) + jnp.einsum('bhts,bhsv->bhtv', A, vc)
        S = S * jnp.exp(tot)[:, :, 0, :, None] + jnp.einsum('bhsk,bhsv->bhkv', k_end, vc)
        return S, o

    sT, ob = lax.scan(step, s0.astype(f32), (qb, kb, vb, bb))
    o = ob.transpose(1, 0, 3, 2, 4).reshape(B, n * C, H, DV)[:, :L]
    return o, sT

def _gla_mixer(gq, gk, gv, ga, gr, w_a2, b_a, g_gla, s0):
    B, L, _ = gq.shape
    q = gq.reshape(B, L, GLA_HEADS, GLA_DK) * (GLA_DK ** -0.5)
    k = gk.reshape(B, L, GLA_HEADS, GLA_DK)
    v = gv.reshape(B, L, GLA_HEADS, GLA_DV)
    log_a = jax.nn.log_sigmoid((ga @ w_a2 + b_a).astype(jnp.float32)) / GLA_TAU
    log_a = log_a.reshape(B, L, GLA_HEADS, GLA_DK)
    o, sT = _gla_recurrence(q, k, v, log_a, s0)
    o = _rmsnorm(o.astype(gv.dtype), g_gla).reshape(B, L, GLA_V)
    return o * jax.nn.silu(gr), sT.astype(s0.dtype)

def _dsa_block(q, iq, iw, q_pos, k_all, v_all, ik_all, topk):
    B, Q = q.shape[:2]
    Lk = k_all.shape[1]
    f32 = jnp.float32
    k_pos = jnp.arange(Lk, dtype=jnp.int32)
    limit = (q_pos // CHUNK + 1) * CHUNK
    logits = jnp.einsum('bqhd,bld->bqhl', iq.astype(f32), ik_all)
    score = jnp.einsum('bqh,bqhl->bql', iw.astype(f32), jax.nn.relu(logits))
    admissible = k_pos[None, :] < limit[:, None]
    score = jnp.where(admissible[None], score, -jnp.inf)
    _, idx = lax.top_k(score, topk)
    sel_pos = k_pos[idx]
    sel_ok = sel_pos < limit[None, :, None]
    gather = jax.vmap(lambda rows, i: rows[i])
    kg = gather(k_all, idx).astype(f32)
    vg = gather(v_all, idx).astype(f32)
    qg = q.astype(f32).reshape(B, Q, ATT_KV_HEADS, ATT_HEADS // ATT_KV_HEADS, ATT_HD)
    s = jnp.einsum('bqgrd,bqkgd->bqgrk', qg, kg) * (ATT_HD ** -0.5)
    dist = jnp.abs(q_pos[None, :, None] - sel_pos).astype(f32)
    slopes = _alibi_slopes().reshape(ATT_KV_HEADS, ATT_HEADS // ATT_KV_HEADS)
    s = s - slopes[None, None, :, :, None] * dist[:, :, None, None, :]
    s = jnp.where(sel_ok[:, :, None, None, :], s, -jnp.inf)
    p = jax.nn.softmax(s, axis=-1)
    o = jnp.einsum('bqgrk,bqkgd->bqgrd', p, vg)
    return o.reshape(B, Q, ATT_Q).astype(q.dtype)

def _layer(x, c, past_k, past_v, past_ik, s0,
           w_ada, b_ada, g_ffn1, w1_gate, w1_up, w1_down, g_mix, w_in, w_a2, b_a, g_gla,
           g_q, g_k, w_out, g_ffn2, w2_gate, w2_up, w2_down, g_out):
    B, L, _ = x.shape
    P = past_k.shape[1]
    mod = jax.nn.silu(c) @ w_ada + b_ada
    sh1, sc1, gt1, sh2, sc2, gt2, sh3, sc3, gt3 = jnp.split(mod[:, None, :], 9, axis=-1)

    h = _rmsnorm(x, g_ffn1) * (1 + sc1) + sh1
    x = x + 0.5 * gt1 * _swiglu(h, w1_gate, w1_up, w1_down)

    h = _rmsnorm(x, g_mix) * (1 + sc2) + sh2
    z = h @ w_in
    gq, gk, gv, ga, gr, aq, ak, av, iq, ik, iw = jnp.split(z, _split_points(), axis=-1)

    gla_out, sT = _gla_mixer(gq, gk, gv, ga, gr, w_a2, b_a, g_gla, s0)

    q = _rmsnorm(aq.reshape(B, L, ATT_HEADS, ATT_HD), g_q)
    k = _rmsnorm(ak.reshape(B, L, ATT_KV_HEADS, ATT_HD), g_k)
    v = av.reshape(B, L, ATT_KV_HEADS, ATT_HD)
    iq = iq.reshape(B, L, IDX_HEADS, IDX_DIM)
    iw = iw * ((IDX_HEADS * IDX_DIM) ** -0.5)
    k_all = jnp.concatenate([past_k.astype(k.dtype), k], axis=1)
    v_all = jnp.concatenate([past_v.astype(v.dtype), v], axis=1)
    ik_all = jnp.concatenate([past_ik.astype(ik.dtype), ik], axis=1).astype(jnp.float32)
    q_pos = P + jnp.arange(L, dtype=jnp.int32)
    topk = min(TOPK_MAX, (P + L) // 4)
    if L <= CHUNK:
        att = _dsa_block(q, iq, iw, q_pos, k_all, v_all, ik_all, topk)
    else:
        n = L // CHUNK

        def to_chunks(t):
            return t.reshape(B, n, CHUNK, *t.shape[2:]).swapaxes(0, 1)

        att = lax.map(lambda a: _dsa_block(a[0], a[1], a[2], a[3], k_all, v_all, ik_all, topk),
                      (to_chunks(q), to_chunks(iq), to_chunks(iw), q_pos.reshape(n, CHUNK)))
        att = att.swapaxes(0, 1).reshape(B, L, ATT_Q)

    x = x + gt2 * (jnp.concatenate([gla_out, att], axis=-1) @ w_out)

    h = _rmsnorm(x, g_ffn2) * (1 + sc3) + sh3
    x = x + 0.5 * gt3 * _swiglu(h, w2_gate, w2_up, w2_down)
    x = _rmsnorm(x, g_out)
    return x, k, v, ik, sT

def setup_inputs(seed: int = 0) -> dict:
    key = jax.random.key(seed)
    ks = iter(jax.random.split(key, 40))
    f32 = jnp.float32

    def nrm(shape, scale):
        return jax.random.normal(next(ks), shape, f32) * scale

    def gain(shape):
        return 1.0 + 0.02 * jax.random.normal(next(ks), shape, f32)

    D = D_MODEL
    return {
        'x_prompt': nrm((BATCH, SEQ, D), 1.0),
        'x_sample': nrm((DEC_BATCH, DEC_SEQ, D), 1.0),
        'c_prompt': nrm((BATCH, D), 1.0),
        'c_sample': nrm((DEC_BATCH, D), 1.0),
        'cache_k': nrm((DEPTH, DEC_BATCH, PAST_LEN, ATT_KV_HEADS, ATT_HD), 1.0),
        'cache_v': nrm((DEPTH, DEC_BATCH, PAST_LEN, ATT_KV_HEADS, ATT_HD), 1.0),
        'cache_idx_k': nrm((DEPTH, DEC_BATCH, PAST_LEN, IDX_DIM), 1.0),
        'state_gla': nrm((DEPTH, DEC_BATCH, GLA_HEADS, GLA_DK, GLA_DV), 0.5),
        'w_ada': nrm((DEPTH, D, 9 * D), 0.5 * D ** -0.5),
        'b_ada': nrm((DEPTH, 9 * D), 0.02),
        'g_ffn1': gain((DEPTH, D)),
        'w1_gate': nrm((DEPTH, D, D_FF), D ** -0.5),
        'w1_up': nrm((DEPTH, D, D_FF), D ** -0.5),
        'w1_down': nrm((DEPTH, D_FF, D), D_FF ** -0.5),
        'g_mix': gain((DEPTH, D)),
        'w_in': nrm((DEPTH, D, IN_WIDTH), D ** -0.5),
        'w_a2': nrm((DEPTH, GLA_LOWRANK, GLA_QK), GLA_LOWRANK ** -0.5),
        'b_a': nrm((DEPTH, GLA_QK), 0.1),
        'g_gla': gain((DEPTH, GLA_DV)),
        'g_q': gain((DEPTH, ATT_HD)),
        'g_k': gain((DEPTH, ATT_HD)),
        'w_out': nrm((DEPTH, MIX_WIDTH, D), MIX_WIDTH ** -0.5),
        'g_ffn2': gain((DEPTH, D)),
        'w2_gate': nrm((DEPTH, D, D_FF), D ** -0.5),
        'w2_up': nrm((DEPTH, D, D_FF), D ** -0.5),
        'w2_down': nrm((DEPTH, D_FF, D), D_FF ** -0.5),
        'g_out': gain((DEPTH, D)),
    }

def reference(x_prompt, x_sample, c_prompt, c_sample, cache_k, cache_v, cache_idx_k, state_gla,
              w_ada, b_ada, g_ffn1, w1_gate, w1_up, w1_down, g_mix, w_in, w_a2, b_a, g_gla,
              g_q, g_k, w_out, g_ffn2, w2_gate, w2_up, w2_down, g_out):
    yp, ys = x_prompt, x_sample
    Bp = x_prompt.shape[0]
    pk_l, pv_l, pik_l, ps_l = [], [], [], []
    sk_l, sv_l, sik_l, ss_l = [], [], [], []
    empty_k = jnp.zeros((Bp, 0, ATT_KV_HEADS, ATT_HD), x_prompt.dtype)
    empty_ik = jnp.zeros((Bp, 0, IDX_DIM), x_prompt.dtype)
    zero_s = jnp.zeros((Bp, GLA_HEADS, GLA_DK, GLA_DV), state_gla.dtype)
    for l in range(DEPTH):
        params = (w_ada[l], b_ada[l], g_ffn1[l], w1_gate[l], w1_up[l], w1_down[l], g_mix[l], w_in[l],
                  w_a2[l], b_a[l], g_gla[l], g_q[l], g_k[l], w_out[l], g_ffn2[l], w2_gate[l], w2_up[l],
                  w2_down[l], g_out[l])
        yp, k1, v1, i1, s1 = _layer(yp, c_prompt, empty_k, empty_k, empty_ik, zero_s, *params)
        ys, k2, v2, i2, s2 = _layer(ys, c_sample, cache_k[l], cache_v[l], cache_idx_k[l], state_gla[l], *params)
        pk_l.append(k1); pv_l.append(v1); pik_l.append(i1); ps_l.append(s1)
        sk_l.append(k2); sv_l.append(v2); sik_l.append(i2); ss_l.append(s2)
    return (yp, ys,
            jnp.stack(pk_l), jnp.stack(pv_l), jnp.stack(pik_l), jnp.stack(ps_l),
            jnp.stack(sk_l), jnp.stack(sv_l), jnp.stack(sik_l), jnp.stack(ss_l))


_drawn_inputs = setup_inputs


def setup_inputs(seed=0):
    import zlib

    import numpy as np

    out = dict(_drawn_inputs(seed))
    spreads = {}
    factors = {'cache_k': 23.844,
     'state_gla': 3.783,
     'g_ffn1': 8.0,
     'g_gla': 179.603,
     'g_q': 200.0,
     'g_k': 25.048,
     'g_ffn2': 22.531,
     'g_out': 21.742,
     'cache_v': 8.0,
     'cache_idx_k': 6.005}
    for name, (base, spread) in spreads.items():
        noise = np.random.default_rng([zlib.crc32(name.encode()), seed]).standard_normal(out[name].shape)
        drawn = base * np.exp(spread * noise) if base else spread * noise
        out[name] = __import__('jax').numpy.asarray(drawn.astype(out[name].dtype))
    for name, factor in factors.items():
        out[name] = (out[name] * factor).astype(out[name].dtype)
    return out
```

```python
from contextlib import ExitStack

import numpy as np

import concourse.bass as bass
from concourse import mybir

ALU = mybir.AluOpType
ACT = mybir.ActivationFunctionType
F32 = mybir.dt.float32
F32R = mybir.dt.float32r
I32 = mybir.dt.int32

P = 128
D = 1024
KD = D // P
DFF = 2816
NF = DFF // P
NPROMPT = 512
NSAMPLE = 64
T = NPROMPT + NSAMPLE
HALF = T // 2
PAST = 256
LSAMPLE = PAST + NSAMPLE
CREDIT = 2
SPARE = 2

GLA_HEADS, GLA_DK, GLA_DV, LOWRANK, GBLOCK = 4, 64, 128, 16, 16
TAU = 16.0
HEADS, KV_HEADS, HD = 8, 2, 64
PER_KV = HEADS // KV_HEADS
IDX_HEADS = 4
EPS = 1e-6
TOPK_PROMPT = min(256, NPROMPT // 4)
TOPK_SAMPLE = min(256, LSAMPLE // 4)
INADMISSIBLE = -3.0e38
TAKEN = -3.4e38
DROPPED = -1.0e30

IQ, IK, GA, AK, AV, AQ, GQ, GK, GV, GR = 0, 2, 3, 4, 5, 6, 10, 12, 14, 18
NZ = 22

START = 16
MIXER_LOADS = 16 * 7
NPAIR = (9 * KD - START) // 2
DOWN_PARTS = ((0, 6), (6, 5), (11, 6), (17, 5))

TILES = [(P * i, P, P * (i + 1), TOPK_PROMPT // 8) for i in range(4)] + [(NPROMPT, NSAMPLE, LSAMPLE, TOPK_SAMPLE // 8)]
SAMPLE = 4

CONST_AT = {}
for _name, _width in (("ident", P), ("causal", P), ("block", 8), ("carry", T), ("dist", 512), ("qk_sum", 50),
                      ("qk_spread", 5 * P), ("gla_sum", 16), ("gla_spread", 4 * P)):
    CONST_AT[_name] = (sum(w for _, w in CONST_AT.values()), _width)
NCONST = sum(w for _, w in CONST_AT.values())


def program(nc, I, O):
    with ExitStack() as ctx:
        at = [-(-nc.sbuf_base // 64) * 64]

        def place(name, shape, dt=F32, offset=None):
            size = 4 * int(np.prod(shape[1:]))
            if offset is None:
                offset = at[0]
                at[0] += -(-size // 32) * 32
            return nc.alloc_sbuf_tensor_at(name, list(shape), dt, offset=offset)

        x = place("x", [P, KD, T])
        mod = place("mod", [P, 9 * KD, 2])
        b_ada = place("b_ada", [P, 9 * KD])
        gains = place("gains", [P, 4, KD])
        cond = place("cond", [P, KD, 2])
        scond = place("scond", [P, KD, 2])
        scale = place("scale", [P, KD, 2])
        gate = place("gate", [P, KD, 2])
        eps = place("eps", [P, 1])
        ones = place("ones", [P, P])
        sumsq = place("sumsq", [P, T])
        rstd = place("rstd", [P, T])
        tmp_a = place("tmp_a", [P, 2, T])
        tmp_b = place("tmp_b", [P, 2, T])
        ada_acc = place("ada_acc", [P, 2, 2 * P])
        raw = place("raw", [P, 2, KD, P])
        w_hi = place("w_hi", [P, 2, KD, P], F32R)
        w_lo = place("w_lo", [P, 2, KD, P], F32R)
        ada_at = at[0]
        ada = place("ada", [P, KD, 2 * P])
        h_at = at[0]
        h_hi = place("h_hi", [P, KD, T], F32R)
        h_lo = place("h_lo", [P, KD, T], F32R)
        g_at = at[0]
        g_hi = place("g_hi", [P, NF, T], F32R)
        g_lo = place("g_lo", [P, NF, T], F32R)
        end = at[0]
        assert end <= nc.sbuf_usable_end
        ada_start = place("ada_start", [P, START, KD, P], F32, offset=g_at)
        assert START * D * 4 <= end - g_at
        at[0] = g_at
        z = place("z", [P, NZ, T])
        const = place("const", [P, NCONST])
        score = place("score", [P, 4, 512])
        bias0 = place("bias0", [P, P])
        v_prompt = place("v_prompt", [P, 4, P])
        v_sample = place("v_sample", [P, 3, P])
        kT_sample = place("kT_sample", [P, LSAMPLE])
        ikT_sample = place("ikT_sample", [P, LSAMPLE])
        iw = place("iw", [P, 4, 32])
        k_dec = place("k_dec", [P, 2, T])
        w_a2 = place("w_a2", [LOWRANK, 2 * P])
        small = place("small", [P, 8])
        etot = place("etot", [P, 2, T // GBLOCK])
        state = place("state", [P, 2, 9, 2 * GLA_DV])
        stats = place("stats", [P, 2, 4])
        top = place("top", [P, 4, 8])
        state_in = place("state_in", [P, 2, GLA_DV])
        assert at[0] <= nc.sbuf_usable_end
        at[0] = h_at
        soft_at = at[0]
        decay = place("decay", [P, 2, T])
        exp_q = place("exp_q", [P, 2, T])
        exp_k = place("exp_k", [P, 2, T])
        exp_end = place("exp_end", [P, 2, T])
        v_tok = place("v_tok", [P, 2, 4 * GLA_DV])
        k_tok = place("k_tok", [P, 2 * P])
        k_block = place("k_block", [P, 8, 2 * P])
        attn = place("attn", [P, 2, GLA_HEADS, P])
        assert at[0] <= g_at
        at[0] = soft_at
        soft = place("soft", [P, 2, 512])
        slant = place("slant", [P, 512])
        probs_t = place("probs_t", [P, 4, PER_KV, P], F32, offset=ada_at)

        def c(name, rows=P):
            a, w = CONST_AT[name]
            return const[0:rows, a:a + w]

        ident = c("ident")
        qk_sum = c("qk_sum").rearrange("p (j r) -> p j r", j=5)
        qk_spread = c("qk_spread").rearrange("p (j r) -> p j r", j=5)
        gla_sum = c("gla_sum").rearrange("p (j r) -> p j r", j=4)
        gla_spread = c("gla_spread").rearrange("p (j r) -> p j r", j=4)
        gain_q, gain_k, gain_gla, gain_q8 = (small[:, n:n + 1] for n in range(4))
        b_a = small[:, 4:6]

        acc = ctx.enter_context(nc.psum_tensor("acc", [P, 4, 512], F32))
        aux = ctx.enter_context(nc.psum_tensor("aux", [P, 4, 512], F32))

        def sem(name):
            return ctx.enter_context(nc.semaphore(name))

        def accumulator(b):
            return acc[:, 2 * b:2 * b + 2, 0:HALF]

        def halves(ap):
            return ap.rearrange("p (a n) -> p a n", a=2)

        small_in, x_in, mixer_in = sem("small_in"), sem("x_in"), sem("mixer_in")
        start_in = [sem(f"start_in{n}") for n in range(4)]
        raw_in = [sem(f"raw_in{n}") for n in range(2)]
        ada_in = sem("ada_in")
        rounded, split, used = sem("rounded"), sem("split"), sem("used")
        cond_ready, start_sum, ada_step, ada_used, ada_sum, ada_kept = (
            sem(n) for n in ("cond_ready", "start_sum", "ada_step", "ada_used", "ada_sum", "ada_kept"))
        mod_ready = sem("mod_ready")
        consts_ready, sq_ready, sumsq_ready, ss_ready, rms_ready, scaled, shifted, h_rounded, h_ready = (
            sem(n) for n in ("consts_ready", "sq_ready", "sumsq_ready", "ss_ready", "rms_ready", "scaled",
                             "shifted", "h_rounded", "h_ready"))
        silu_ready, g_full, g_rounded, g_ready, x_part, x_added, square_made = (
            sem(n) for n in ("silu_ready", "g_full", "g_rounded", "g_ready", "x_part", "x_added", "square_made"))
        z_ready, mix_ready = sem("z_ready"), sem("mix_ready")
        iw_made, iw_ready, logit_made, relu_ready, logit_used = (
            sem(n) for n in ("iw_made", "iw_ready", "logit_made", "relu_ready", "logit_used"))
        top_found, top_taken, tick = sem("top_found"), sem("top_taken"), sem("tick")
        za_made, log_ready, decay_ready, exp_ready, gla_in_ready = (
            sem(n) for n in ("za_made", "log_ready", "decay_ready", "exp_ready", "gla_in_ready"))
        qk_sq, qk_ss, qk_rms, qk_rstd, qk_wide, qk_ready = (
            sem(n) for n in ("qk_sq", "qk_ss", "qk_rms", "qk_rstd", "qk_wide", "qk_ready"))
        v_turned, v_ready = sem("v_turned"), sem("v_ready")
        tok_made, tok_ready, block_ready, attn_made, attn_ready, u_made, s_ready, o_made, o_ready, s_first = (
            sem(n) for n in ("tok_made", "tok_ready", "block_ready", "attn_made", "attn_ready", "u_made",
                             "s_ready", "o_made", "o_ready", "s_first"))
        o_within = sem("o_within")
        gla_sq, gla_ss, gla_rms, gla_rstd, gla_wide, gla_silu = (
            sem(n) for n in ("gla_sq", "gla_ss", "gla_rms", "gla_rstd", "gla_wide", "gla_silu"))
        s_made, s_biased, p_exp, p_ready, pT_made, pT_ready, pv_made, att_ready = (
            sem(n) for n in ("s_made", "s_biased", "p_exp", "p_ready", "pT_made", "pT_ready", "pv_made",
                             "att_ready"))
        y_ready = sem("y_ready")
        stored, y_stored = sem("stored"), [sem(f"y_stored{n}") for n in range(4)]
        act_step, vec_step = sem("act_step"), sem("vec_step")

        FFN1, DOWN1, Z0, WOUT, FFN2, DOWN2 = np.cumsum([0, 2 * NF, 4 * KD, NZ, KD, 2 * NF]).tolist()

        block = ctx.enter_context(nc.Block())

        @block.sync
        def _(sp):
            def load(u, slot, source, nk=KD):
                sp.wait_ge(split, u + 1)
                sp.dma_start(raw[:, slot, 0:nk, :], source.rearrange("p (k n) -> p k n", k=nk)).then_inc(raw_in[slot], 16)

            def load_pair(p):
                sp.wait_ge(ada_used, p + SPARE)
                sp.dma_start(ada[:, :, :], I["w_ada_pairs"][p].rearrange("p (k n) -> p k n", k=KD)).then_inc(ada_in, 16)

            def load_ffn(n, first, down_first):
                w_gate, w_up, w_down = I[f"w{n}_gate"], I[f"w{n}_up"], I[f"w{n}_down"]
                with sp.Fori(0, NF) as f:
                    load(f * 2 + first, 0, w_gate[f])
                    load(f * 2 + (first + 1), 1, w_up[f])
                    if n == 1:
                        load_pair(f)
                with sp.Fori(0, KD // 2) as i:
                    for j in range(2):
                        for q, (k0, nk) in enumerate(DOWN_PARTS):
                            load(i * 8 + (down_first + 4 * j + q), q % 2, w_down[i * 2 + j][:, k0 * P:(k0 + nk) * P], nk)
                    if n == 1:
                        load_pair(i + NF)

            sp.dma_start(cond[:, :, :], I["cond"]).then_inc(small_in, 16)
            sp.dma_start(b_ada[:, :], I["b_ada"]).then_inc(small_in, 16)
            sp.dma_start(gains[:, :, :], I["gains"]).then_inc(small_in, 16)
            sp.dma_start(x[:, :, :], I["x"]).then_inc(x_in, 16)
            for n in range(4):
                m = START // 4
                sp.dma_start(ada_start[:, m * n:m * n + m, :, :],
                             I["w_ada_start"][:, m * n:m * n + m, :].rearrange("p m (k n) -> p m k n", k=KD)
                             ).then_inc(start_in[n], 16)
            load_ffn(1, FFN1, DOWN1)
            with sp.Fori(0, 2) as i:
                for j in range(2):
                    load(i * 2 + (Z0 + j), j, I["w_in"][i * 2 + j])
                load_pair(i + (NF + KD // 2))
            sp.wait_ge(used, Z0 + CREDIT)
            for dst, name in ((const[:, :], "const"), (small[:, 0:6], "small"), (w_a2[:, :], "w_a2"),
                              (kT_sample[:, 0:PAST], "cache_kT"), (ikT_sample[:, 0:PAST], "cache_ikT"),
                              (v_sample[:, 0:2, :], "cache_v"), (state_in[:, :, :], "state")):
                sp.dma_start(dst, I[name]).then_inc(mixer_in, 16)
            with sp.Fori(2, NZ // 2) as i:
                for j in range(2):
                    load(i * 2 + (Z0 + j), j, I["w_in"][i * 2 + j])
            sp.wait_ge(v_ready, 2)
            sp.dma_start(O["ikT"], z[0:HD, IK, :]).then_inc(stored, 16)
            sp.dma_start(O["vT"], z[:, AV, :]).then_inc(stored, 16)
            sp.wait_ge(qk_ready, 5)
            sp.dma_start(O["kT"], z[:, AK, :]).then_inc(stored, 16)
            sp.wait_ge(s_ready, 4 * 8)
            for r in range(2):
                rows = slice(GLA_DK * r, GLA_DK * (r + 1))
                sp.dma_start(O["state_prompt"][rows], state[rows, :, 8, GLA_DV * r:GLA_DV * (r + 1)]).then_inc(stored, 16)
            sp.wait_ge(s_ready, 4 * 8 + 4)
            for r in range(2):
                rows = slice(GLA_DK * r, GLA_DK * (r + 1))
                sp.dma_start(O["state_sample"][rows], state[rows, :, 4, GLA_DV * r:GLA_DV * (r + 1)]).then_inc(stored, 16)
            with sp.Fori(0, KD // 2) as i:
                for j in range(2):
                    load(i * 2 + (WOUT + j), j, I["w_out"][i * 2 + j])
            load_ffn(2, FFN2, DOWN2)
            for k in range(KD):
                sp.wait_ge(y_ready, k + 1)
                sp.dma_start(O["yT"][:, k, :], tmp_a[:, k % 2, :] if k % 4 < 2 else tmp_b[:, k % 2, :]).then_inc(y_stored[k % 4], 16)
            for n in range(4):
                sp.wait_ge(y_stored[n], 16 * KD // 4)
            sp.wait_ge(stored, 16 * 7)

        @block.gpsimd
        def _(pool):
            pool.sem_inc(split, CREDIT)
            pool.memset(ones[:, :], 1.0).then_inc(consts_ready, 1)
            pool.memset(eps[:, :], EPS).then_inc(consts_ready, 1)

            def low_half(u, slot, nk=KD):
                pool.wait_ge(rounded, u + 1)
                pool.tensor_tensor(w_lo[:, slot, 0:nk, :], raw[:, slot, 0:nk, :], w_hi[:, slot, 0:nk, :].bitcast(F32),
                                   ALU.subtract).then_inc(split, 1)

            def ffn(first, down_first):
                with pool.Fori(0, NF) as f:
                    for s in range(2):
                        low_half(f * 2 + (first + s), s)
                with pool.Fori(0, KD // 2) as i:
                    for q in range(8):
                        low_half(i * 8 + (down_first + q), q % 2, DOWN_PARTS[q % 4][1])

            def paired(first, start, stop):
                with pool.Fori(start, stop) as i:
                    for s in range(2):
                        low_half(i * 2 + (first + s), s)

            def round_h(n):
                for k in range(KD):
                    pool.wait_ge(shifted, KD * n + k + 1)
                    pool.tensor_copy(h_hi[:, k, :], tmp_b[:, k % 2, :]).then_inc(h_rounded, 1)

            round_h(0)
            ffn(FFN1, DOWN1)
            round_h(1)
            paired(Z0, 0, NZ // 2)
            pool.wait_ge(mixer_in, MIXER_LOADS)
            for i, (t0, nt, _, _) in enumerate(TILES):
                nb = nt // GBLOCK
                pool.wait_ge(tok_ready, i + 1)
                if i:
                    pool.wait_ge(u_made, 8 * i)
                pool.tensor_tensor(
                    k_block[0:nt, 0:nb, :],
                    k_tok[0:nt, :].rearrange("p (o n) -> p o n", o=1).to_broadcast([nt, nb, 2 * P]),
                    c("block", nt)[:, 0:nb].rearrange("p (n o) -> p n o", o=1).to_broadcast([nt, nb, 2 * P]),
                    ALU.mult).then_inc(block_ready, 1)
            paired(WOUT, 0, KD // 2)
            round_h(2)
            ffn(FFN2, DOWN2)

        @block.scalar
        def _(act):
            steps = [0]
            for s in (z_ready, silu_ready):
                act.sem_inc(s, SPARE)

            def settle(ins):
                steps[0] += 1
                ins.then_inc(act_step, 1)
                act.wait_ge(act_step, steps[0])

            def round_unit(n, u, slot, nk=KD):
                act.wait_ge(raw_in[slot], n)
                act.wait_ge(used, u + 1)
                act.activation(w_hi[:, slot, 0:nk, :], raw[:, slot, 0:nk, :], ACT.Copy).then_inc(rounded, 1)

            def paired(first, start, stop):
                with act.Fori(start, stop) as i:
                    for s in range(2):
                        round_unit(i * 16 + (8 * first + 16), i * 2 + (first + s), s)

            def norm(n, shift_at):
                act.wait_ge(ss_ready, n + 1)
                act.activation(halves(rstd[:, :]), aux[:, 0:2, 0:HALF], ACT.Sqrt, bias=eps[:, :], scale=1.0 / D).then_inc(rms_ready, 1)
                act.wait_ge(mod_ready, 1 + n)
                for k in range(KD):
                    act.wait_ge(scaled, KD * n + k + 1)
                    if KD * n + k >= 2:
                        act.wait_ge(h_ready, KD * n + k - 1)
                    for s, cols in enumerate((slice(0, NPROMPT), slice(NPROMPT, T))):
                        ins = act.activation(tmp_b[:, k % 2, cols], tmp_a[:, k % 2, cols], ACT.Identity,
                                       bias=mod[:, shift_at + k, s:s + 1], scale=scale[:, k, s:s + 1])
                    ins.then_inc(shifted, 1)

            def ffn(first, down_first, done):
                with act.Fori(0, NF) as f:
                    round_unit(f * 16 + (8 * first + 16), f * 2 + first, 0)
                    round_unit(f * 16 + (8 * first + 16), f * 2 + (first + 1), 1)
                    act.wait_ge(used, f * 2 + (first + 1 + CREDIT))
                    act.wait_ge(g_full, f + done + SPARE)
                    act.activation(halves(tmp_a[:, 0, :]), accumulator(0), ACT.Silu).then_inc(silu_ready, 1)
                with act.Fori(0, KD // 2) as i:
                    for q in range(8):
                        round_unit(i * 64 + (8 * down_first + 16 * (q // 2) + 16), i * 8 + (down_first + q), q % 2,
                                   DOWN_PARTS[q % 4][1])

            act.wait_ge(small_in, 48)
            act.activation(scond[:, :, :], cond[:, :, :], ACT.Silu).then_inc(cond_ready, 1)
            act.wait_ge(consts_ready, 2)
            for k in range(KD):
                act.wait_ge(x_in, 16)
                if k >= 2:
                    act.wait_ge(sumsq_ready, k - 1)
                act.activation(tmp_b[:, k % 2, :], x[:, k, :], ACT.Square).then_inc(sq_ready, 1)
            norm(0, 0)
            ffn(FFN1, DOWN1, 0)
            norm(1, 3 * KD)

            def z_copy(b, n):
                act.wait_ge(used, n + (Z0 + 1 + CREDIT))
                act.activation(halves(z[:, bass.ds(n, 1), :].rearrange("p o n -> p (o n)")), accumulator(b), ACT.Copy).then_inc(z_ready, 1)

            def z_blocks(start, stop):
                round_unit(8 * (Z0 + 2 * start) + 16, Z0 + 2 * start, 0)
                with act.Fori(start, stop - 1) as i:
                    round_unit(i * 16 + (8 * Z0 + 16), i * 2 + (Z0 + 1), 1)
                    z_copy(0, i * 2)
                    round_unit(i * 16 + (8 * Z0 + 32), i * 2 + (Z0 + 2), 0)
                    z_copy(1, i * 2 + 1)
                i = stop - 1
                round_unit(8 * (Z0 + 2 * i) + 16, Z0 + 2 * i + 1, 1)
                z_copy(0, 2 * i)
                z_copy(1, 2 * i + 1)

            z_blocks(0, 2)
            act.wait_ge(iw_made, 1)
            act.activation(iw[:, 0:3, :], aux[:, 0, 0:96].rearrange("p (i n) -> p i n", i=3), ACT.Copy,
                           scale=(IDX_HEADS * HD) ** -0.5)
            act.activation(iw[0:NSAMPLE, 3, :], aux[0:NSAMPLE, 0, 96:128], ACT.Copy,
                           scale=(IDX_HEADS * HD) ** -0.5).then_inc(iw_ready, 1)
            for m in range(4 * IDX_HEADS):
                _, nq, nk, _ = TILES[1 + m // IDX_HEADS]
                act.wait_ge(logit_made, m + 1)
                if m >= 2:
                    act.wait_ge(logit_used, m - 1)
                act.activation(tmp_a[0:nq, m % 2, 0:nk], aux[0:nq, 1 + m % 3, 0:nk], ACT.Relu).then_inc(relu_ready, 1)
            z_blocks(2, NZ // 2)

            act.wait_ge(v_turned, 1)
            act.activation(v_prompt[:, :, :], aux[:, 0, :].rearrange("p (i n) -> p i n", i=4), ACT.Copy).then_inc(v_ready, 1)
            act.activation(v_sample[0:NSAMPLE, 2, :], aux[0:NSAMPLE, 1, 0:P], ACT.Copy).then_inc(v_ready, 1)
            act.wait_ge(qk_ss, 5)
            act.activation(halves(rstd[0:10, :]), aux[0:10, 2:4, 0:HALF], ACT.Sqrt, bias=eps[0:10, :],
                           scale=1.0 / HD).then_inc(qk_rms, 1)
            for j in range(2):
                act.wait_ge(za_made, j + 1)
                act.activation(halves(exp_q[:, j, :]), acc[:, 2 * j:2 * j + 2, 0:HALF], ACT.Identity,
                               bias=b_a[:, j:j + 1]).then_inc(act_step, 1)
            steps[0] += 2
            act.wait_ge(act_step, steps[0])
            for f, scaling, shift in ((ACT.Abs, 1.0, 0.0), (ACT.Exp, -1.0, 0.0), (ACT.Ln, 1.0, 1.0)):
                source = exp_q if f == ACT.Abs else exp_k
                settle(act.activation(exp_k[:, :, :], source[:, :, :], f, bias=shift, scale=scaling))
            act.sem_inc(log_ready, 1)
            act.wait_ge(decay_ready, 1)
            act.activation(exp_q[:, :, :], decay[:, :, :], ACT.Exp, scale=1.0 / TAU).then_inc(exp_ready, 1)
            act.activation(exp_k[:, :, :], decay[:, :, :], ACT.Exp, scale=-1.0 / TAU).then_inc(exp_ready, 1)
            act.activation(etot[:, :, :], decay[:, :, GBLOCK - 1:T:GBLOCK], ACT.Exp, scale=1.0 / TAU).then_inc(exp_ready, 1)
            act.wait_ge(decay_ready, 2)
            settle(act.activation(exp_end[:, :, :], exp_end[:, :, :], ACT.Exp, scale=1.0 / TAU))
            act.sem_inc(exp_ready, 1)

            for i, (t0, nt, _, _) in enumerate(TILES):
                act.wait_ge(tok_made, i + 1)
                if i >= 2:
                    act.wait_ge(o_made, i - 1)
                act.activation(v_tok[0:nt, i % 2, :], aux[0:nt, 0, :], ACT.Copy)
                if i >= 1:
                    act.wait_ge(block_ready, i)
                act.activation(k_tok[0:nt, :], aux[0:nt, 1, 0:2 * P], ACT.Copy).then_inc(tok_ready, 1)
                act.wait_ge(o_made, i + 1)
                for r in range(2):
                    ins = act.activation(z[:, GV + r:GV + 4:2, t0:t0 + nt],
                                         acc[:, 2 + r, 0:2 * P].rearrange("p (h n) -> p h n", h=2)[:, :, 0:nt], ACT.Copy)
                ins.then_inc(o_ready, 1)
            act.wait_ge(gla_ss, 1)
            act.activation(halves(rstd[0:4, :]), aux[0:4, 0:2, 0:HALF], ACT.Sqrt, bias=eps[0:4, :],
                           scale=1.0 / GLA_DV).then_inc(gla_rms, 1)
            act.activation(z[:, GR:GR + 4, :], z[:, GR:GR + 4, :], ACT.Silu).then_inc(gla_silu, 1)

            def turned(m):
                ti, r = m // HEADS, m % PER_KV
                _, nq, nk, _ = TILES[ti]
                act.wait_ge(pT_made, m + 1)
                if m >= PER_KV:
                    act.wait_ge(pv_made, m // PER_KV)
                full, rest = nk // P, nk % P
                src = aux[:, 2 + m % 2, :].rearrange("p (n q) -> p n q", n=4)
                if rest:
                    act.activation(probs_t[0:rest, full, r, 0:nq], src[0:rest, full, 0:nq], ACT.Copy)
                act.activation(probs_t[:, 0:full, r, 0:nq], src[:, 0:full, 0:nq], ACT.Copy).then_inc(pT_ready, 1)

            def gathered(g):
                ti, kv = g // KV_HEADS, g % KV_HEADS
                t0, nq, _, _ = TILES[ti]
                rows = slice(HD * kv, HD * kv + HD)
                act.wait_ge(pv_made, g + 1)
                act.activation(z[rows, AQ:AQ + 4, t0:t0 + nq],
                               acc[rows, 0, :].rearrange("p (r q) -> p r q", r=4)[:, :, 0:nq], ACT.Copy).then_inc(att_ready, 1)

            total = len(TILES) * HEADS
            for m in range(total + 1):
                if m < total:
                    _, nq, nk, _ = TILES[m // HEADS]
                    act.wait_ge(s_biased, m + 1)
                    act.activation(soft[0:nq, m % 2, 0:nk], soft[0:nq, m % 2, 0:nk], ACT.Exp,
                                   bias=stats[0:nq, m % 2, 1:2], accum_out=stats[0:nq, m % 2, 2:3]).then_inc(p_exp, 1)
                if m >= 1:
                    turned(m - 1)
                    if m % PER_KV == 0:
                        gathered(m // PER_KV - 1)

            paired(WOUT, 0, KD // 2)
            norm(2, 6 * KD)
            ffn(FFN2, DOWN2, NF)
            act.wait_ge(ss_ready, 4)
            act.activation(halves(rstd[:, :]), aux[:, 0:2, 0:HALF], ACT.Sqrt, bias=eps[:, :], scale=1.0 / D).then_inc(rms_ready, 1)

        @block.tensor
        def _(pe):
            pe.sem_inc(used, CREDIT)

            def product(u, slot, b, operand_hi, operand_lo, ks, first, last):
                pe.wait_ge(split, u + (1 + CREDIT))
                for n, k in enumerate(ks):
                    for m, (w, a) in enumerate(((w_hi, operand_hi), (w_hi, operand_lo), (w_lo, operand_hi))):
                        for half in range(2):
                            ins = pe.matmul(acc[:, 2 * b + half, 0:HALF], w[:, slot, n, :],
                                            a[:, k, HALF * half:HALF * (half + 1)],
                                            start=first and n == 0 and m == 0, stop=last and n == len(ks) - 1 and m == 2)
                ins.then_inc(used, 1)

            def mean_square(n):
                pe.wait_ge(sumsq_ready, [8, 16, 24, 32][n])
                for half in range(2):
                    ins = pe.matmul(aux[:, half, 0:HALF], ones[:, :], sumsq[:, HALF * half:HALF * (half + 1)],
                                    start=True, stop=True)
                ins.then_inc(ss_ready, 1)

            def pair_sums(p):
                pe.wait_ge(ada_step, p * 16 + 16)
                pe.wait_ge(ada_kept, p + SPARE)
                for s in range(2):
                    for m in range(2):
                        ins = pe.matmul(aux[:, 3, 2 * m + s:2 * m + s + 1], ada_acc[:, s, P * m:P * m + P], ones[:, 0:1],
                                        start=True, stop=True)
                ins.then_inc(ada_sum, 1)

            def ffn(n, first, down_first):
                done = NF * (n - 1)
                with pe.Fori(0, NF) as f:
                    pe.wait_ge(silu_ready, f + done + SPARE)
                    product(f * 2 + first, 0, 0, h_hi, h_lo, range(KD), True, True)
                    pe.wait_ge(g_full, f + done + SPARE)
                    product(f * 2 + (first + 1), 1, 1, h_hi, h_lo, range(KD), True, True)
                    if n == 1:
                        pair_sums(f)
                pe.wait_ge(g_ready, NF * n + SPARE)
                with pe.Fori(0, KD // 2) as i:
                    for j in range(2):
                        pe.wait_ge(x_added, i * 2 + (2 * KD * (n - 1) + j - 1 + SPARE))
                        for q, (k0, nk) in enumerate(DOWN_PARTS):
                            product(i * 8 + (down_first + 4 * j + q), q % 2, j, g_hi, g_lo, range(k0, k0 + nk),
                                    q == 0, q == 3)
                    if n == 1:
                        pair_sums(i + NF)
                mean_square(2 * n - 1)

            pe.wait_ge(cond_ready, 1)
            pe.wait_ge(consts_ready, 2)
            for u in range(START):
                pe.wait_ge(start_in[u // 4], 16)
                for k in range(KD):
                    ins = pe.matmul(aux[:, 2, 2 * u:2 * u + 2], ada_start[:, u, k, :], scond[:, k, :],
                                    start=(k == 0), stop=(k == KD - 1))
            ins.then_inc(start_sum, 1)
            mean_square(0)
            pe.wait_ge(h_ready, KD)
            ffn(1, FFN1, DOWN1)

            def z_blocks(start, stop, pairs):
                with pe.Fori(start, stop) as i:
                    for j in range(2):
                        pe.wait_ge(z_ready, i * 2 + (j - 1 + SPARE))
                        product(i * 2 + (Z0 + j), j, j, h_hi, h_lo, range(KD), True, True)
                    if pairs:
                        pair_sums(i + (NF + KD // 2))

            pe.wait_ge(h_ready, 2 * KD)
            z_blocks(0, 2, True)
            pe.wait_ge(z_ready, 4 + SPARE)
            pe.wait_ge(mixer_in, MIXER_LOADS)
            pe.wait_ge(ada_kept, NPAIR + SPARE)
            for n, (t0, nq, _, _) in enumerate(TILES[1:]):
                ins = pe.transpose(aux[0:nq, 0, 32 * n:32 * n + 32], z[0:32, GA, t0:t0 + nq], ident[0:32, 0:32])
            ins.then_inc(iw_made, 1)
            for m in range(4 * IDX_HEADS):
                t0, nq, nk, _ = TILES[1 + m // IDX_HEADS]
                h = m % IDX_HEADS
                rows = slice(HD * (h % 2), HD * (h % 2) + HD)
                if m >= 3:
                    pe.wait_ge(relu_ready, m - 2)
                if m // IDX_HEADS == 3:
                    pe.wait_ge(logit_used, 3 * IDX_HEADS)
                keys = ikT_sample[rows, :] if m // IDX_HEADS == 3 else z[rows, IK, 0:nk]
                pe.matmul(aux[0:nq, 1 + m % 3, 0:nk], z[rows, IQ + h // 2, t0:t0 + nq], keys,
                          start=True, stop=True).then_inc(logit_made, 1)
            z_blocks(2, NZ // 2, False)

            pe.wait_ge(z_ready, NZ + SPARE)
            pe.wait_ge(relu_ready, 4 * IDX_HEADS)
            for i in range(4):
                pe.transpose(aux[:, 0, P * i:P * i + P], z[:, AV, P * i:P * i + P], ident)
            pe.transpose(aux[0:NSAMPLE, 1, 0:P], z[:, AV, NPROMPT:T], ident).then_inc(v_turned, 1)
            for j in range(2):
                for half in range(2):
                    ins = pe.matmul(acc[:, 2 * j + half, 0:HALF], w_a2[:, P * j:P * j + P],
                                    z[0:LOWRANK, GA, HALF * half:HALF * (half + 1)], start=True, stop=True)
                ins.then_inc(za_made, 1)
            for j in range(5):
                pe.wait_ge(qk_sq, j + 1)
                for half in range(2):
                    ins = pe.matmul(aux[0:10, 2 + half, 0:HALF], qk_sum[:, j, :], (tmp_a if j % 4 < 2 else tmp_b)[:, j % 2, HALF * half:HALF * (half + 1)],
                                    start=(j == 0), stop=(j == 4))
                ins.then_inc(qk_ss, 1)
            pe.wait_ge(qk_rstd, 1)
            for j in range(5):
                if j < 2:
                    pe.wait_ge(exp_ready, 1)
                else:
                    pe.wait_ge(qk_ready, j - 1)
                for half in range(2):
                    ins = pe.matmul(acc[:, 2 * (j % 2) + half, 0:HALF], qk_spread[0:10, j, :],
                                    rstd[0:10, HALF * half:HALF * (half + 1)], start=True, stop=True)
                ins.then_inc(qk_wide, 1)
            pe.wait_ge(qk_ready, 5)

            pe.wait_ge(v_ready, 2)
            pe.wait_ge(gla_in_ready, 2)
            for i, (t0, nt, _, _) in enumerate(TILES):
                nb, par = nt // GBLOCK, i % 2
                if i:
                    pe.wait_ge(tok_ready, i)
                for h in range(GLA_HEADS):
                    pe.transpose(aux[0:nt, 0, P * h:P * h + P], z[:, GV + h, t0:t0 + nt], ident)
                for j in range(2):
                    ins = pe.transpose(aux[0:nt, 1, P * j:P * j + P], z[:, GK + j, t0:t0 + nt], ident)
                ins.then_inc(tok_made, 1)
                if i:
                    pe.wait_ge(attn_ready, i)
                for h in range(GLA_HEADS):
                    rows = slice(GLA_DK * (h % 2), GLA_DK * (h % 2) + GLA_DK)
                    ins = pe.matmul(aux[0:nt, 2 + h % 2, P * (h // 2):P * (h // 2) + nt], k_dec[rows, h // 2, t0:t0 + nt],
                                    z[rows, GQ + h // 2, t0:t0 + nt], start=True, stop=True)
                ins.then_inc(attn_made, 1)
                pe.wait_ge(block_ready, i + 1)
                for b in range(nb):
                    done = 8 * i + b
                    if done >= 2:
                        pe.wait_ge(s_ready, done - 1)
                    for j in range(2):
                        ins = pe.matmul(acc[:, b % 2, 256 * j:256 * j + 256], k_block[0:nt, b, P * j:P * j + P],
                                        v_tok[0:nt, par, 256 * j:256 * j + 256], start=True, stop=True)
                    ins.then_inc(u_made, 1)
                pe.wait_ge(attn_ready, i + 1)
                if i:
                    pe.wait_ge(o_ready, i)
                for h in range(GLA_HEADS):
                    at_h = P * (h // 2)
                    ins = pe.matmul(acc[:, 2 + h % 2, at_h:at_h + nt], v_tok[0:nt, par, P * h:P * h + P], attn[0:nt, par, h, 0:nt],
                                    start=(h < 2), stop=False, skip_group_check=True)
                if nt < P:
                    ins.then_inc(o_within, 1)
                    pe.wait_ge(o_within, 1)
                for b in range(nb):
                    pe.wait_ge(s_first, i + 1) if b == 0 else pe.wait_ge(s_ready, 8 * i + b)
                    for h in range(GLA_HEADS):
                        r = h % 2
                        rows = slice(GLA_DK * r, GLA_DK * r + GLA_DK)
                        at_h = P * (h // 2) + GBLOCK * b
                        ins = pe.matmul(acc[:, 2 + r, at_h:at_h + GBLOCK],
                                        state[rows, h // 2, b, GLA_DV * r:GLA_DV * (r + 1)],
                                        z[rows, GQ + h // 2, t0 + GBLOCK * b:t0 + GBLOCK * (b + 1)],
                                        start=False, stop=(b == nb - 1), skip_group_check=True)
                ins.then_inc(o_made, 1)
            for h in range(GLA_HEADS):
                pe.wait_ge(gla_sq, h + 1)
                for half in range(2):
                    ins = pe.matmul(aux[0:4, half, 0:HALF], gla_sum[:, h, :], (tmp_a if h < 2 else tmp_b)[:, h % 2, HALF * half:HALF * (half + 1)],
                                    start=(h == 0), stop=(h == 3))
            ins.then_inc(gla_ss, 1)
            pe.wait_ge(gla_rstd, 1)
            for h in range(GLA_HEADS):
                if h >= 2:
                    pe.wait_ge(gla_in_ready, 3 + h - 2)
                for half in range(2):
                    ins = pe.matmul(acc[:, 2 * (h % 2) + half, 0:HALF], gla_spread[0:4, h, :],
                                    rstd[0:4, HALF * half:HALF * (half + 1)], start=True, stop=True)
                ins.then_inc(gla_wide, 1)
            pe.wait_ge(gla_in_ready, 2 + 4)

            def turn(m):
                _, nq, nk, _ = TILES[m // HEADS]
                pe.wait_ge(p_ready, m + 1)
                if m >= 2:
                    pe.wait_ge(pT_ready, m - 1)
                for n in range(-(-nk // P)):
                    w = min(P, nk - P * n)
                    ins = pe.transpose(aux[0:w, 2 + m % 2, P * n:P * n + nq], soft[0:nq, m % 2, P * n:P * n + w],
                                       ident[0:nq, 0:nq])
                ins.then_inc(pT_made, 1)

            def weigh(g):
                ti, kv = g // KV_HEADS, g % KV_HEADS
                _, nq, nk, _ = TILES[ti]
                v = v_sample if ti == SAMPLE else v_prompt
                pe.wait_ge(pT_ready, PER_KV * (g + 1))
                if g:
                    pe.wait_ge(att_ready, g)
                last = -(-nk // P) - 1
                for n in range(last + 1):
                    w = min(P, nk - P * n)
                    if nq == P:
                        out, rhs = acc[HD * kv:HD * kv + HD, 0, :], probs_t[0:w, n, :, :].rearrange("p r q -> p (r q)")
                    else:
                        out = acc[HD * kv:HD * kv + HD, 0, :].rearrange("p (r q) -> p r q", r=4)[:, :, 0:nq]
                        rhs = probs_t[0:w, n, :, 0:nq]
                    ins = pe.matmul(out, v[0:w, n, HD * kv:HD * kv + HD], rhs, start=(n == 0), stop=(n == last))
                ins.then_inc(pv_made, 1)

            total = len(TILES) * HEADS
            for m in range(total + 2):
                if m < total:
                    ti, kv, r = m // HEADS, m % HEADS // PER_KV, m % PER_KV
                    t0, nq, nk, _ = TILES[ti]
                    rows = slice(HD * kv, HD * kv + HD)
                    if m >= 2:
                        pe.wait_ge(s_biased, m - 1)
                    keys = kT_sample[rows, :] if ti == SAMPLE else z[rows, AK, 0:nk]
                    pe.matmul(aux[0:nq, m % 2, 0:nk], z[rows, AQ + r, t0:t0 + nq], keys, start=True, stop=True).then_inc(s_made, 1)
                if 1 <= m <= total:
                    turn(m - 1)
                    if m % PER_KV == 0:
                        weigh(m // PER_KV - 1)

            pe.wait_ge(mix_ready, KD)
            with pe.Fori(0, KD // 2) as i:
                for j in range(2):
                    pe.wait_ge(x_added, i * 2 + (KD + j - 1 + SPARE))
                    product(i * 2 + (WOUT + j), j, j, h_hi, h_lo, range(KD), True, True)
            mean_square(2)
            pe.wait_ge(h_ready, 3 * KD)
            ffn(2, FFN2, DOWN2)

        @block.vector
        def _(vec):
            steps = [0]
            for s in (x_added, g_full, g_ready, ada_used, ada_kept, top_taken):
                vec.sem_inc(s, SPARE)

            def mark(ins):
                steps[0] += 1
                ins.then_inc(vec_step, 1)
                return steps[0]

            def settle(ins):
                vec.wait_ge(vec_step, mark(ins))

            def modulate(n, scale_at, gate_at):
                wide = gains[:, n, :].rearrange("p (k o) -> p k o", o=1).to_broadcast([P, KD, 2])
                settle(vec.tensor_scalar(scale[:, :, :], mod[:, scale_at:scale_at + KD, :], 1.0, None, ALU.add))
                vec.tensor_tensor(scale[:, :, :], scale[:, :, :], wide, ALU.mult).then_inc(mod_ready, 1)

            def out_gate(gate_at, factor):
                settle(vec.tensor_scalar(gate[:, :, :], mod[:, gate_at:gate_at + KD, :], factor, None, ALU.mult))

            def norm(n):
                vec.wait_ge(rms_ready, n + 1)
                settle(vec.reciprocal(rstd[:, :], rstd[:, :]))
                for k in range(KD + 1):
                    if k < KD:
                        if k >= 2:
                            vec.wait_ge(shifted, KD * n + k - 1)
                        vec.tensor_tensor(tmp_a[:, k % 2, :], x[:, k, :], rstd[:, :], ALU.mult).then_inc(scaled, 1)
                    if k:
                        vec.wait_ge(h_rounded, KD * n + k)
                        vec.tensor_tensor(h_lo[:, k - 1, :], tmp_b[:, (k - 1) % 2, :], h_hi[:, k - 1, :].bitcast(F32),
                                          ALU.subtract).then_inc(h_ready, 1)

            def pair(p):
                vec.wait_ge(ada_in, p * 16 + 16)
                for k in range(KD):
                    for s in range(2):
                        n = 2 * k + s
                        if k == 0:
                            ins = vec.tensor_scalar(ada_acc[:, s, :], ada[:, k, :], scond[:, k, s:s + 1], None, ALU.mult)
                        else:
                            vec.wait_ge(ada_step, p * 16 + (n - 1))
                            ins = vec.scalar_tensor_tensor(ada_acc[:, s, :], ada[:, k, :], scond[:, k, s:s + 1],
                                                           ada_acc[:, s, :], ALU.mult, ALU.add)
                        ins.then_inc(ada_step, 1)
                vec.wait_ge(ada_step, p * 16 + 16)
                vec.sem_inc(ada_used, 1)

            def keep_pair(p):
                vec.wait_ge(ada_sum, p + 1)
                vec.tensor_tensor(mod[:, bass.ds(p * 2 + START, 2), :], aux[:, 3, 0:4].rearrange("p (m s) -> p m s", m=2),
                                  b_ada[:, bass.ds(p * 2 + START, 2)].rearrange("p (m o) -> p m o", o=1).to_broadcast([P, 2, 2]),
                                  ALU.add).then_inc(ada_kept, 1)

            def add_out(d, b, count, made):
                vec.wait_ge(used, made)
                a = accumulator(b)
                for lo, hi, s, last in ((0, HALF, 0, 0), (HALF, NPROMPT, 0, 0), (NPROMPT, T, 1, 1)):
                    part = a[:, lo // HALF, lo % HALF:lo % HALF + hi - lo]
                    xs = x[:, bass.ds(d, 1), lo:hi].rearrange("p o n -> p (o n)")
                    gs = gate[:, bass.ds(d, 1), s:s + 1].rearrange("p o n -> p (o n)")
                    ins = vec.scalar_tensor_tensor(xs, part, gs, xs, ALU.mult, ALU.add)
                    if last:
                        ins.then_inc(x_added, 1)
                    else:
                        ins.then_inc(x_part, 1)
                vec.wait_ge(x_added, count + (1 + SPARE))
                vec.wait_ge(x_part, count * 2 + 2)
                xs = x[:, bass.ds(d, 1), :].rearrange("p o n -> p (o n)")
                vec.tensor_tensor(tmp_b[:, b, :], xs, xs, ALU.mult).then_inc(square_made, 1)
                vec.wait_ge(square_made, count + 1)
                vec.wait_ge(sumsq_ready, count + KD)
                vec.tensor_tensor(sumsq[:, :], sumsq[:, :], tmp_b[:, b, :], ALU.add).then_inc(sumsq_ready, 1)

            def zero_sumsq():
                settle(vec.memset(sumsq[:, :], 0.0))

            def ffn(n, added):
                down_first = DOWN1 if n == 1 else DOWN2
                done = NF * (n - 1)
                with vec.Fori(0, NF) as f:
                    if n == 1:
                        pair(f)
                    vec.wait_ge(silu_ready, f + (done + 1) + SPARE)
                    vec.wait_ge(used, f * 2 + ((FFN1 if n == 1 else FFN2) + 2 + CREDIT))
                    vec.wait_ge(g_ready, f + done + SPARE)
                    vec.tensor_tensor(halves(tmp_a[:, 1, :]), halves(tmp_a[:, 0, :]), accumulator(1), ALU.mult).then_inc(g_full, 1)
                    vec.wait_ge(g_full, f + (done + 1) + SPARE)
                    hi = g_hi[:, bass.ds(f, 1), :].rearrange("p o n -> p (o n)")
                    lo = g_lo[:, bass.ds(f, 1), :].rearrange("p o n -> p (o n)")
                    vec.tensor_copy(hi, tmp_a[:, 1, :]).then_inc(g_rounded, 1)
                    vec.wait_ge(g_rounded, f + (done + 1))
                    vec.tensor_tensor(lo, tmp_a[:, 1, :], hi.bitcast(F32), ALU.subtract).then_inc(g_ready, 1)
                    if n == 1:
                        keep_pair(f)
                if n == 1:
                    vec.wait_ge(ada_kept, NF + SPARE)
                out_gate(2 * KD if n == 1 else 8 * KD, 0.5)
                zero_sumsq()
                with vec.Fori(0, KD // 2) as i:
                    if n == 1:
                        pair(i + NF)
                    for j in range(2):
                        add_out(i * 2 + j, j, i * 2 + (added + j), i * 8 + (down_first + 4 * j + 4 + CREDIT))
                    if n == 1:
                        keep_pair(i + NF)

            vec.wait_ge(x_in, 16)
            settle(vec.memset(sumsq[:, :], 0.0))
            for k in range(KD):
                vec.wait_ge(sq_ready, k + 1)
                if k:
                    vec.wait_ge(sumsq_ready, k)
                vec.tensor_tensor(sumsq[:, :], sumsq[:, :], tmp_b[:, k % 2, :], ALU.add).then_inc(sumsq_ready, 1)
            vec.wait_ge(start_sum, 1)
            vec.wait_ge(small_in, 48)
            settle(vec.tensor_tensor(mod[:, 0:START, :], aux[:, 2, 0:2 * START].rearrange("p (u s) -> p u s", s=2),
                                     b_ada[:, 0:START].rearrange("p (u o) -> p u o", o=1).to_broadcast([P, START, 2]), ALU.add))
            modulate(0, KD, None)
            norm(0)
            ffn(1, 0)
            vec.wait_ge(ada_kept, NF + KD // 2 + SPARE)
            modulate(1, 4 * KD, None)
            norm(1)
            with vec.Fori(0, 2) as i:
                pair(i + (NF + KD // 2))
                keep_pair(i + (NF + KD // 2))

            vec.wait_ge(mixer_in, MIXER_LOADS)
            vec.wait_ge(z_ready, 4 + SPARE)
            mark(vec.tensor_copy(ikT_sample[:, PAST:LSAMPLE], z[:, IK, NPROMPT:T]))
            vec.wait_ge(vec_step, steps[0])
            vec.wait_ge(iw_ready, 1)
            for m in range(4 * IDX_HEADS):
                n, h = m // IDX_HEADS, m % IDX_HEADS
                _, nq, nk, _ = TILES[1 + n]
                vec.wait_ge(relu_ready, m + 1)
                weight = iw[0:nq, n, LOWRANK + h:LOWRANK + h + 1]
                if h == 0:
                    ins = vec.tensor_scalar(score[0:nq, n, 0:nk], tmp_a[0:nq, m % 2, 0:nk], weight, None, ALU.mult)
                else:
                    vec.wait_ge(logit_used, m)
                    ins = vec.scalar_tensor_tensor(score[0:nq, n, 0:nk], tmp_a[0:nq, m % 2, 0:nk], weight,
                                                   score[0:nq, n, 0:nk], ALU.mult, ALU.add)
                ins.then_inc(logit_used, 1)
            vec.wait_ge(logit_used, 4 * IDX_HEADS)
            for n in range(3):
                nk = TILES[1 + n][2]
                mark(vec.memset(score[0:64, n, nk - 64:nk], INADMISSIBLE))
            mark(vec.memset(bias0[:, :], 0.0))
            vec.wait_ge(vec_step, steps[0])
            settle(vec.memset(bias0[0:64, 64:P], DROPPED))

            def top_rounds(start, stop, tiles, before):
                each = len(tiles)
                with vec.Fori(start, stop) as i:
                    for q, n in enumerate(tiles):
                        _, nq, nk, _ = TILES[1 + n]
                        vec.wait_ge(top_taken, i * each + (before - start * each + q) + SPARE)
                        vec.sem_inc(tick, 1)
                        vec.max(top[0:nq, q, :], score[0:nq, n, 0:nk]).then_inc(top_found, 1)
                        vec.wait_ge(top_found, i * each + (before - start * each + q + 1))
                        vec.sem_inc(tick, 1)
                        vec.match_replace(score[0:nq, n, 0:nk], top[0:nq, q, :], score[0:nq, n, 0:nk], TAKEN).then_inc(top_taken, 1)

            rounds_s, rounds_p = TILES[SAMPLE][3], TILES[1][3]
            top_rounds(0, rounds_s, (3, 0, 1, 2), 0)
            top_rounds(rounds_s, rounds_p, (0, 1, 2), 4 * rounds_s)
            vec.wait_ge(top_taken, 4 * rounds_s + 3 * (rounds_p - rounds_s) + SPARE)
            for n in range(4):
                _, nq, nk, _ = TILES[1 + n]
                mark(vec.tensor_scalar(score[0:nq, n, 0:nk], score[0:nq, n, 0:nk], 0.5 * (INADMISSIBLE + TAKEN), DROPPED,
                                       ALU.is_gt, ALU.mult))
            vec.wait_ge(vec_step, steps[0])

            vec.wait_ge(z_ready, NZ + SPARE)
            tiles = [AK, AQ, AQ + 1, AQ + 2, AQ + 3]
            for j, n in enumerate(tiles):
                if j == 4:
                    vec.wait_ge(qk_ss, 1)
                vec.tensor_tensor((tmp_a if j % 4 < 2 else tmp_b)[:, j % 2, :], z[:, n, :], z[:, n, :], ALU.mult).then_inc(qk_sq, 1)
            vec.wait_ge(log_ready, 1)
            settle(vec.tensor_scalar(exp_q[:, :, :], exp_q[:, :, :], 0.0, None, ALU.min))
            settle(vec.tensor_tensor(exp_q[:, :, :], exp_q[:, :, :], exp_k[:, :, :], ALU.subtract))
            for j in range(2):
                settle(vec.tensor_tensor_scan(decay[:, j, :], c("carry"), exp_q[:, j, :], 0.0, ALU.mult, ALU.add))
            vec.sem_inc(decay_ready, 1)
            blocks = decay[:, :, :].rearrange("p j (b n) -> p j b n", n=GBLOCK)
            for j in range(2):
                ins = vec.tensor_tensor(exp_end[:, j, :].rearrange("p (b n) -> p b n", n=GBLOCK),
                                        blocks[:, j, :, GBLOCK - 1:GBLOCK].to_broadcast([P, T // GBLOCK, GBLOCK]),
                                        blocks[:, j, :, :], ALU.subtract)
                settle(ins)
            vec.sem_inc(decay_ready, 1)
            vec.wait_ge(qk_rms, 1)
            settle(vec.reciprocal(rstd[0:10, :], rstd[0:10, :]))
            vec.sem_inc(qk_rstd, 1)
            settle(vec.tensor_scalar(gain_q8, gain_q, HD ** -0.5, None, ALU.mult))
            for j, n in enumerate(tiles):
                vec.wait_ge(qk_wide, j + 1)
                vec.scalar_tensor_tensor(halves(z[:, n, :]), halves(z[:, n, :]), gain_k if j == 0 else gain_q8,
                                         accumulator(j % 2), ALU.mult, ALU.mult).then_inc(qk_ready, 1)
            vec.wait_ge(qk_ready, 5)
            mark(vec.tensor_copy(kT_sample[:, PAST:LSAMPLE], z[:, AK, NPROMPT:T]))
            vec.wait_ge(exp_ready, 4)
            for j in range(2):
                mark(vec.scalar_tensor_tensor(z[:, GQ + j, :], z[:, GQ + j, :], GLA_DK ** -0.5, exp_q[:, j, :], ALU.mult, ALU.mult))
                mark(vec.tensor_tensor(k_dec[:, j, :], z[:, GK + j, :], exp_k[:, j, :], ALU.mult))
                vec.wait_ge(vec_step, steps[0])
                vec.tensor_tensor(z[:, GK + j, :], z[:, GK + j, :], exp_end[:, j, :], ALU.mult).then_inc(gla_in_ready, 1)
            mark(vec.memset(attn[:, :, :, :], 0.0))
            mark(vec.memset(state[:, :, 0, :], 0.0))
            vec.wait_ge(vec_step, steps[0])
            vec.sem_inc(s_first, 1)

            for i, (t0, nt, _, _) in enumerate(TILES):
                nb = nt // GBLOCK
                vec.wait_ge(attn_made, i + 1)
                if i >= 2:
                    vec.wait_ge(o_made, i - 1)
                mask = c("causal", nt)[:, 0:nt].bitcast(I32).rearrange("p (o n) -> p o n", o=1).to_broadcast([nt, 2, nt])
                for r in range(2):
                    ins = vec.copy_predicated(attn[0:nt, i % 2, r:4:2, 0:nt], mask,
                                              aux[0:nt, 2 + r, 0:2 * P].rearrange("p (h n) -> p h n", h=2)[:, :, 0:nt])
                ins.then_inc(attn_ready, 1)
                if i:
                    vec.wait_ge(o_made, i)
                    vec.wait_ge(s_ready, 8 * i)
                    if i < SAMPLE:
                        settle(vec.tensor_copy(state[:, :, 0, :], state[:, :, 8, :]))
                    else:
                        for r in range(2):
                            rows = slice(GLA_DK * r, GLA_DK * (r + 1))
                            mark(vec.tensor_copy(state[rows, :, 0, GLA_DV * r:GLA_DV * (r + 1)], state_in[rows, :, :]))
                        vec.wait_ge(vec_step, steps[0])
                    vec.sem_inc(s_first, 1)
                for b in range(nb):
                    n = 8 * i + b
                    vec.wait_ge(u_made, n + 1)
                    if b:
                        vec.wait_ge(s_ready, n)
                    for j in range(2):
                        ins = vec.scalar_tensor_tensor(state[:, j, b + 1, :], state[:, j, b, :], etot[:, j, n:n + 1],
                                                       acc[:, b % 2, 256 * j:256 * j + 256], ALU.mult, ALU.add)
                        if j == 0:
                            mark(ins)
                    vec.wait_ge(vec_step, steps[0])
                    ins.then_inc(s_ready, 1)
            vec.wait_ge(o_ready, len(TILES))
            for h in range(GLA_HEADS):
                vec.tensor_tensor((tmp_a if h < 2 else tmp_b)[:, h % 2, :], z[:, GV + h, :], z[:, GV + h, :], ALU.mult).then_inc(gla_sq, 1)
            vec.wait_ge(gla_rms, 1)
            settle(vec.reciprocal(rstd[0:4, :], rstd[0:4, :]))
            vec.sem_inc(gla_rstd, 1)
            vec.wait_ge(gla_silu, 1)
            for h in range(GLA_HEADS):
                vec.wait_ge(gla_wide, h + 1)
                vec.scalar_tensor_tensor(halves(z[:, GV + h, :]), halves(z[:, GV + h, :]), gain_gla,
                                         accumulator(h % 2), ALU.mult, ALU.mult).then_inc(gla_in_ready, 1)
                vec.wait_ge(gla_in_ready, 2 + h + 1)
                mark(vec.tensor_tensor(z[:, GV + h, :], z[:, GV + h, :], z[:, GR + h, :], ALU.mult))

            def scaled_probs(m):
                _, nq, _, _ = TILES[m // HEADS]
                nk = TILES[m // HEADS][2]
                vec.wait_ge(p_exp, m + 1)
                settle(vec.reciprocal(stats[0:nq, m % 2, 3:4], stats[0:nq, m % 2, 2:3]))
                vec.tensor_scalar(soft[0:nq, m % 2, 0:nk], soft[0:nq, m % 2, 0:nk], stats[0:nq, m % 2, 3:4], None,
                                  ALU.mult).then_inc(p_ready, 1)

            total = len(TILES) * HEADS
            for m in range(total + 1):
                if m < total:
                    ti = m // HEADS
                    _, nq, nk, _ = TILES[ti]
                    first_dist = 384 - (P * ti if ti != SAMPLE else PAST)
                    dist = c("dist", nq)[:, first_dist:first_dist + nk]
                    dropped = bias0[0:nq, 0:nk] if ti == 0 else score[0:nq, ti - 1, 0:nk]
                    settle(vec.scalar_tensor_tensor(slant[0:nq, 0:nk], dist, -(2.0 ** -(m % HEADS + 1)), dropped,
                                                    ALU.mult, ALU.add))
                    vec.wait_ge(s_made, m + 1)
                    if m >= 2:
                        vec.wait_ge(pT_made, m - 1)
                    settle(vec.tensor_tensor_reduce(soft[0:nq, m % 2, 0:nk], aux[0:nq, m % 2, 0:nk], slant[0:nq, 0:nk],
                                                    1.0, TAKEN, ALU.add, ALU.max, stats[0:nq, m % 2, 0:1]))
                    vec.tensor_scalar(stats[0:nq, m % 2, 1:2], stats[0:nq, m % 2, 0:1], -1.0, None, ALU.mult).then_inc(s_biased, 1)
                if m:
                    scaled_probs(m - 1)

            vec.wait_ge(att_ready, len(TILES) * KV_HEADS)
            vec.wait_ge(vec_step, steps[0])
            vec.wait_ge(p_ready, total)
            vec.wait_ge(s_biased, total)
            for k in range(KD):
                source = z[:, GV + k, :] if k < 4 else z[:, AQ + k - 4, :]
                settle(vec.tensor_copy(h_hi[:, k, :], source))
                vec.tensor_tensor(h_lo[:, k, :], source, h_hi[:, k, :].bitcast(F32), ALU.subtract).then_inc(mix_ready, 1)
            out_gate(5 * KD, 1.0)
            zero_sumsq()
            with vec.Fori(0, KD // 2) as i:
                for j in range(2):
                    add_out(i * 2 + j, j, i * 2 + (KD + j), i * 2 + (WOUT + j + 1 + CREDIT))
            modulate(2, 7 * KD, None)
            norm(2)
            vec.wait_ge(stored, 16 * 7)
            ffn(2, 2 * KD)
            vec.wait_ge(rms_ready, 4)
            settle(vec.reciprocal(rstd[:, :], rstd[:, :]))
            for k in range(KD):
                if k >= 4:
                    vec.wait_ge(y_stored[k % 4], 16 * (k // 4))
                y = (tmp_a if k % 4 < 2 else tmp_b)[:, k % 2, :]
                vec.scalar_tensor_tensor(y, x[:, k, :], gains[:, 3, k:k + 1], rstd[:, :], ALU.mult, ALU.mult).then_inc(y_ready, 1)


def constants():
    p = np.arange(P)
    out = np.zeros((P, NCONST), np.float32)

    def put(name, value, rows=P):
        a, w = CONST_AT[name]
        out[0:rows, a:a + w] = np.asarray(value, np.float32).reshape(rows, w)

    put("ident", np.eye(P))
    put("causal", (p[:, None] // GBLOCK == p[None, :] // GBLOCK) & (p[:, None] <= p[None, :]))
    put("block", p[:, None] // GBLOCK == np.arange(8)[None, :])
    put("carry", np.tile(np.arange(T) % GBLOCK != 0, (P, 1)))
    put("dist", np.abs(np.arange(512)[None, :] - 384 - p[:, None]))
    row = np.arange(10)
    tile = np.arange(5)
    belongs = row[None, None, :] == 2 * tile[None, :, None] + p[:, None, None] // HD
    put("qk_sum", belongs)
    put("qk_spread", belongs.transpose(2, 1, 0), 10)
    head = np.arange(4)
    own = np.broadcast_to(head[None, :, None] == head[None, None, :], (P, 4, 4))
    put("gla_sum", own)
    put("gla_spread", own.transpose(2, 1, 0), 4)
    return out


INPUTS = {
    "x": (P, KD, T), "cond": (P, KD, 2), "b_ada": (P, 9 * KD), "gains": (P, 4, KD), "small": (P, 6), "const": (P, NCONST),
    "w_ada_start": (P, START, D), "w_ada_pairs": (NPAIR, P, 2 * D), "w_in": (NZ, P, D), "w_a2": (LOWRANK, 2 * P),
    "w_out": (KD, P, D), "w1_gate": (NF, P, D), "w1_up": (NF, P, D), "w1_down": (KD, P, DFF),
    "w2_gate": (NF, P, D), "w2_up": (NF, P, D), "w2_down": (KD, P, DFF),
    "cache_kT": (P, PAST), "cache_ikT": (P, PAST), "cache_v": (P, 2, P), "state": (P, 2, GLA_DV),
}
OUTPUTS = {"yT": (P, KD, T), "kT": (P, T), "vT": (P, T), "ikT": (HD, T), "state_prompt": (P, 2, GLA_DV),
           "state_sample": (P, 2, GLA_DV)}


def laid_out(v):
    v = {n: np.asarray(a) for n, a in v.items()}

    def units(w):
        k, n = w.shape
        return w.reshape(k // P, P, n // P, P).transpose(2, 1, 0, 3).reshape(n // P, P, k)

    def by_partition(a):
        return a.reshape(-1, P).T

    out = {}
    x = np.concatenate([v["x_prompt"][0], v["x_sample"][0]])
    out["x"] = x.T.reshape(KD, P, T).transpose(1, 0, 2)
    c = np.stack([v["c_prompt"][0], v["c_sample"][0]])
    out["cond"] = c.T.reshape(KD, P, 2).transpose(1, 0, 2)
    out["b_ada"] = by_partition(v["b_ada"][0])
    out["gains"] = np.stack([by_partition(v[n][0]) for n in ("g_ffn1", "g_mix", "g_ffn2", "g_out")], axis=1)
    b_a = by_partition(v["b_a"][0])
    out["small"] = np.stack([np.tile(v["g_q"][0], 2), np.tile(v["g_k"][0], 2), v["g_gla"][0],
                             np.zeros(P, np.float32), b_a[:, 0], b_a[:, 1]], axis=1)
    out["const"] = constants()
    ada = units(v["w_ada"][0])
    out["w_ada_start"] = ada[:START].transpose(1, 0, 2)
    pairs = ada[START:].reshape(NPAIR, 2, P, KD, P)
    out["w_ada_pairs"] = pairs.transpose(0, 2, 3, 1, 4).reshape(NPAIR, P, 2 * D)
    sizes = (256, 256, 512, LOWRANK, 512, 512, 128, 128, 256, 64, 4)
    gq, gk, gv, ga, gr, aq, ak, av, iq, ik, iw = np.split(v["w_in"][0], np.cumsum(sizes)[:-1], axis=1)
    paired = aq.reshape(D, KV_HEADS, PER_KV, HD).transpose(0, 2, 1, 3).reshape(D, HEADS * HD)
    padding = np.zeros((D, P - LOWRANK - IDX_HEADS), np.float32)
    out["w_in"] = units(np.concatenate([iq, ik, ik, ga, iw, padding, ak, av, paired, gq, gk, gv, gr], axis=1))
    out["w_a2"] = v["w_a2"][0]
    w_out = v["w_out"][0]
    att = w_out[512:].reshape(KV_HEADS, PER_KV, HD, D).transpose(1, 0, 2, 3).reshape(512, D)
    out["w_out"] = units(np.concatenate([w_out[:512], att]))
    for n in ("w1_gate", "w1_up", "w1_down", "w2_gate", "w2_up", "w2_down"):
        out[n] = units(v[n][0])
    out["cache_kT"] = v["cache_k"][0, 0].reshape(PAST, P).T
    ik_past = v["cache_idx_k"][0, 0].T
    out["cache_ikT"] = np.concatenate([ik_past, ik_past])
    out["cache_v"] = v["cache_v"][0, 0].reshape(2, P, P).transpose(1, 0, 2)
    out["state"] = v["state_gla"][0, 0].reshape(2, P, GLA_DV).transpose(1, 0, 2)
    return {n: np.ascontiguousarray(out[n]) for n in INPUTS}


def kernel(**inputs):
    import concourse.bacc as bacc
    from concourse.bass_utils import run_bass_kernel_spmd

    nc = bacc.Bacc("TRN2", target_bir_lowering=False, num_devices=1)
    given = {n: nc.dram_tensor(f"{n}_in", shape, F32, kind="ExternalInput").ap() for n, shape in INPUTS.items()}
    made = {n: nc.dram_tensor(f"{n}_out", shape, F32, kind="ExternalOutput").ap() for n, shape in OUTPUTS.items()}
    program(nc, given, made)
    r = run_bass_kernel_spmd(nc, [{f"{n}_in": a for n, a in laid_out(inputs).items()}], core_ids=[0]).results[0]

    y = r["yT_out"].transpose(2, 1, 0).reshape(T, D)
    k, v = (r[n].T.reshape(T, KV_HEADS, HD) for n in ("kT_out", "vT_out"))
    ik = r["ikT_out"].T
    first, second = (r[n].transpose(1, 0, 2).reshape(1, 1, GLA_HEADS, GLA_DK, GLA_DV)
                     for n in ("state_prompt_out", "state_sample_out"))
    a, b = slice(0, NPROMPT), slice(NPROMPT, T)
    return (y[a][None], y[b][None], k[a][None, None], v[a][None, None], ik[a][None, None], first,
            k[b][None, None], v[b][None, None], ik[b][None, None], second)
```

```python
from contextlib import ExitStack

import numpy as np

import concourse.bass as bass
from concourse import mybir

ALU = mybir.AluOpType
ACT = mybir.ActivationFunctionType
F32 = mybir.dt.float32
F32R = mybir.dt.float32r
I32 = mybir.dt.int32

P = 128
D = 1024
KD = D // P
DFF = 2816
NF = DFF // P
NPROMPT = 512
NSAMPLE = 64
T = NPROMPT + NSAMPLE
HALF = T // 2
PAST = 256
LSAMPLE = PAST + NSAMPLE
CREDIT = 2
SPARE = 2

GLA_HEADS, GLA_DK, GLA_DV, LOWRANK, GBLOCK = 4, 64, 128, 16, 16
TAU = 16.0
HEADS, KV_HEADS, HD = 8, 2, 64
PER_KV = HEADS // KV_HEADS
IDX_HEADS = 4
EPS = 1e-6
TOPK_PROMPT = min(256, NPROMPT // 4)
TOPK_SAMPLE = min(256, LSAMPLE // 4)
INADMISSIBLE = -3.0e38
TAKEN = -3.4e38
DROPPED = -1.0e30

IQ, IK, GA, AK, AV, AQ, GQ, GK, GV, GR = 0, 2, 3, 4, 5, 6, 10, 12, 14, 18
NZ = 22

START_PAIRS = KD // 2
NPAIR = (9 * KD - KD) // 2
BESIDE = NPAIR - START_PAIRS
MIXER_LOADS = 16 * 7
DOWN_PARTS = ((0, 6), (6, 5), (11, 6), (17, 5))

TILES = [(P * i, P, P * (i + 1), TOPK_PROMPT // 8) for i in range(4)] + [(NPROMPT, NSAMPLE, LSAMPLE, TOPK_SAMPLE // 8)]
SAMPLE = 4

CONST_AT = {}
for _name, _width in (("ident", P), ("causal", P), ("block", 8), ("carry", T), ("dist", 512), ("qk_sum", 50),
                      ("qk_spread", 5 * P), ("gla_sum", 16), ("gla_spread", 4 * P)):
    CONST_AT[_name] = (sum(w for _, w in CONST_AT.values()), _width)
NCONST = sum(w for _, w in CONST_AT.values())


def program(nc, I, O):
    with ExitStack() as ctx:
        at = [-(-nc.sbuf_base // 64) * 64]

        def place(name, shape, dt=F32, offset=None):
            size = 4 * int(np.prod(shape[1:]))
            if offset is None:
                offset = at[0]
                at[0] += -(-size // 32) * 32
            return nc.alloc_sbuf_tensor_at(name, list(shape), dt, offset=offset)

        x = place("x", [P, KD, T])
        mod = place("mod", [P, 9 * KD, 2])
        b_ada = place("b_ada", [P, 9 * KD])
        gains = place("gains", [P, 4, KD])
        cond = place("cond", [P, KD, 2])
        scond = place("scond", [P, KD, 2])
        scale = place("scale", [P, KD, 2])
        gate = place("gate", [P, KD, 2])
        eps = place("eps", [P, 1])
        ones = place("ones", [P, P])
        sumsq = place("sumsq", [P, T])
        rstd = place("rstd", [P, T])
        tmp_a = place("tmp_a", [P, 2, T])
        tmp_b = place("tmp_b", [P, 2, T])
        ada_acc = place("ada_acc", [P, 2, 2 * P])
        raw = place("raw", [P, 2, KD, P])
        w_hi = place("w_hi", [P, 2, KD, P], F32R)
        w_lo = place("w_lo", [P, 2, KD, P], F32R)
        ada_at = at[0]
        ada = place("ada", [P, KD, 2 * P])
        h_at = at[0]
        h_hi = place("h_hi", [P, KD, T], F32R)
        h_lo = place("h_lo", [P, KD, T], F32R)
        g_at = at[0]
        g_hi = place("g_hi", [P, NF, T], F32R)
        g_lo = place("g_lo", [P, NF, T], F32R)
        end = at[0]
        assert end <= nc.sbuf_usable_end
        at[0] = g_at
        ada_units = place("ada_units", [P, KD, KD, P])
        ada_pairs = place("ada_pairs", [P, START_PAIRS, KD, 2 * P])
        start_acc = place("start_acc", [P, START_PAIRS, 2, 2 * P])
        assert at[0] <= end
        at[0] = g_at
        z = place("z", [P, NZ, T])
        const = place("const", [P, NCONST])
        score = place("score", [P, 4, 512])
        bias0 = place("bias0", [P, P])
        v_prompt = place("v_prompt", [P, 4, P])
        v_sample = place("v_sample", [P, 3, P])
        kT_sample = place("kT_sample", [P, LSAMPLE])
        ikT_sample = place("ikT_sample", [P, LSAMPLE])
        iw = place("iw", [P, 4, 32])
        k_dec = place("k_dec", [P, 2, T])
        w_a2 = place("w_a2", [LOWRANK, 2 * P])
        small = place("small", [P, 8])
        etot = place("etot", [P, 2, T // GBLOCK])
        state_at = at[0]
        state = place("state", [P, 2, 9, 2 * GLA_DV])
        stats = place("stats", [P, 2, 4])
        top = place("top", [P, 4, 8])
        state_in = place("state_in", [P, 2, GLA_DV])
        assert at[0] <= nc.sbuf_usable_end
        after = at[0]
        at[0] = state_at
        decay = place("decay", [P, 2, T])
        exp_q = place("exp_q", [P, 2, T])
        exp_k = place("exp_k", [P, 2, T])
        exp_end = place("exp_end", [P, 2, T])
        assert at[0] <= after
        at[0] = h_at
        gla_square = place("gla_square", [P, GLA_HEADS, T])
        v_tok = place("v_tok", [P, 2, 4 * GLA_DV])
        k_tok = place("k_tok", [P, 2 * P])
        k_block = place("k_block", [P, 8, 2 * P])
        attn = place("attn", [P, 2, GLA_HEADS, P])
        assert at[0] <= g_at
        probs_t = place("probs_t", [P, 4, PER_KV, P], F32, offset=ada_at)

        def c(name, rows=P):
            a, w = CONST_AT[name]
            return const[0:rows, a:a + w]

        ident = c("ident")
        qk_sum = c("qk_sum").rearrange("p (j r) -> p j r", j=5)
        qk_spread = c("qk_spread").rearrange("p (j r) -> p j r", j=5)
        gla_sum = c("gla_sum").rearrange("p (j r) -> p j r", j=4)
        gla_spread = c("gla_spread").rearrange("p (j r) -> p j r", j=4)
        gain_q, gain_k, gain_gla, gain_q8 = (small[:, n:n + 1] for n in range(4))
        b_a = small[:, 4:6]

        acc = ctx.enter_context(nc.psum_tensor("acc", [P, 4, 512], F32))
        aux = ctx.enter_context(nc.psum_tensor("aux", [P, 4, 512], F32))

        def sem(name):
            return ctx.enter_context(nc.semaphore(name))

        def accumulator(b):
            return acc[:, 2 * b:2 * b + 2, 0:HALF]

        def wide(b):
            return aux[:, 2 * b:2 * b + 2, 0:HALF]

        def halves(ap):
            return ap.rearrange("p (a n) -> p a n", a=2)

        small_in, x_in, mixer_in = sem("small_in"), sem("x_in"), sem("mixer_in")
        start_in = [sem(f"start_in{n}") for n in range(4)]
        start_pair_made, start_pair_sum, start_step = sem("start_pair_made"), sem("start_pair_sum"), sem("start_step")
        raw_in = [sem(f"raw_in{n}") for n in range(2)]
        ada_in = sem("ada_in")
        rounded, split, used = sem("rounded"), sem("split"), sem("used")
        cond_ready, start_sum, ada_step, ada_used, ada_sum, ada_kept = (
            sem(n) for n in ("cond_ready", "start_sum", "ada_step", "ada_used", "ada_sum", "ada_kept"))
        mod_ready = sem("mod_ready")
        consts_ready, sq_ready, sumsq_ready, ss_ready, rms_ready, rstd_ready, scaled_even, scaled_odd, shifted, h_rounded, h_ready = (
            sem(n) for n in ("consts_ready", "sq_ready", "sumsq_ready", "ss_ready", "rms_ready", "rstd_ready",
                             "scaled_even", "scaled_odd", "shifted", "h_rounded", "h_ready"))
        silu_ready, g_full, g_rounded, g_ready, x_part, x_added, square_made = (
            sem(n) for n in ("silu_ready", "g_full", "g_rounded", "g_ready", "x_part", "x_added", "square_made"))
        z_ready, mix_rounded, mix_ready = sem("z_ready"), sem("mix_rounded"), sem("mix_ready")
        iw_made, iw_ready, logit_made, relu_ready, logit_used = (
            sem(n) for n in ("iw_made", "iw_ready", "logit_made", "relu_ready", "logit_used"))
        top_found, top_taken, tick = sem("top_found"), sem("top_taken"), sem("tick")
        za_made, log_ready, decay_ready, exp_ready, gla_in_ready = (
            sem(n) for n in ("za_made", "log_ready", "decay_ready", "exp_ready", "gla_in_ready"))
        qk_sq, qk_ss, qk_rms, qk_rstd, qk_wide, qk_ready = (
            sem(n) for n in ("qk_sq", "qk_ss", "qk_rms", "qk_rstd", "qk_wide", "qk_ready"))
        v_turned, v_ready = sem("v_turned"), sem("v_ready")
        tok_made, tok_ready, block_ready, attn_made, attn_ready, u_made, s_ready, inter_made, o_ready, s_first = (
            sem(n) for n in ("tok_made", "tok_ready", "block_ready", "attn_made", "attn_ready", "u_made",
                             "s_ready", "inter_made", "o_ready", "s_first"))
        o_within = sem("o_within")
        gla_sq, gla_ss, gla_rms, gla_rstd, gla_wide, gla_silu = (
            sem(n) for n in ("gla_sq", "gla_ss", "gla_rms", "gla_rstd", "gla_wide", "gla_silu"))
        s_made, s_biased, p_exp, p_ready, pT_made, pT_ready, pv_made, att_ready = (
            sem(n) for n in ("s_made", "s_biased", "p_exp", "p_ready", "pT_made", "pT_ready", "pv_made",
                             "att_ready"))
        y_ready = sem("y_ready")
        stored, y_stored = sem("stored"), [sem(f"y_stored{n}") for n in range(4)]
        act_step, vec_step = sem("act_step"), sem("vec_step")

        FFN1, DOWN1, Z0, WOUT, FFN2, DOWN2 = np.cumsum([0, 2 * NF, 4 * KD, NZ, KD, 2 * NF]).tolist()

        SLOTS = len(TILES) * HEADS
        STEPS = T // GBLOCK

        def gla_steps(m):
            return [2 * m, 2 * m + 1] if m < 4 else [m + 4] if m + 4 < STEPS + 3 else []

        def state_slot(n):
            return (n + n // (NPROMPT // GBLOCK)) % 9

        def first_free(n):
            return n - 7 + n // (NPROMPT // GBLOCK)

        block = ctx.enter_context(nc.Block())

        @block.sync
        def _(sp):
            def load(u, slot, source, nk=KD):
                sp.wait_ge(split, u + 1)
                sp.dma_start(raw[:, slot, 0:nk, :], source.rearrange("p (k n) -> p k n", k=nk)).then_inc(raw_in[slot], 16)

            def load_pair(p):
                sp.wait_ge(ada_used, p + SPARE)
                sp.dma_start(ada[:, :, :], I["w_ada_pairs"][p + START_PAIRS].rearrange("p (k n) -> p k n", k=KD)).then_inc(ada_in, 16)

            def load_ffn(n, first, down_first):
                w_gate, w_up, w_down = I[f"w{n}_gate"], I[f"w{n}_up"], I[f"w{n}_down"]
                with sp.Fori(0, NF) as f:
                    load(f * 2 + first, 0, w_gate[f])
                    load(f * 2 + (first + 1), 1, w_up[f])
                    if n == 1:
                        load_pair(f)
                with sp.Fori(0, KD // 2) as i:
                    for j in range(2):
                        for q, (k0, nk) in enumerate(DOWN_PARTS):
                            load(i * 8 + (down_first + 4 * j + q), q % 2, w_down[i * 2 + j][:, k0 * P:(k0 + nk) * P], nk)
                    if n == 1:
                        load_pair(i + NF)

            sp.dma_start(cond[:, :, :], I["cond"]).then_inc(small_in, 16)
            sp.dma_start(b_ada[:, :], I["b_ada"]).then_inc(small_in, 16)
            sp.dma_start(gains[:, :, :], I["gains"]).then_inc(small_in, 16)
            half = KD // 2

            def load_units(n):
                sp.dma_start(ada_units[:, half * n:half * n + half, :, :],
                             I["w_ada_units"][:, half * n:half * n + half, :].rearrange("p m (k n) -> p m k n", k=KD)
                             ).then_inc(start_in[n], 16)

            def load_start_pairs(n):
                sp.dma_start(ada_pairs[:, 2 * n:2 * n + 2, :, :],
                             I["w_ada_pairs"][2 * n:2 * n + 2].rearrange("m p (k n) -> p m k n", k=KD)
                             ).then_inc(start_in[2 + n], 16)

            load_units(0)
            load_start_pairs(0)
            sp.dma_start(x[:, :, :], I["x"]).then_inc(x_in, 16)
            load_units(1)
            load_start_pairs(1)
            load_ffn(1, FFN1, DOWN1)
            with sp.Fori(0, 2) as i:
                for j in range(2):
                    load(i * 2 + (Z0 + j), j, I["w_in"][i * 2 + j])
                load_pair(i + (NF + KD // 2))
            sp.wait_ge(used, Z0 + CREDIT)
            for dst, name in ((const[:, :], "const"), (small[:, 0:6], "small"), (w_a2[:, :], "w_a2"),
                              (kT_sample[:, 0:PAST], "cache_kT"), (ikT_sample[:, 0:PAST], "cache_ikT"),
                              (v_sample[:, 0:2, :], "cache_v"), (state_in[:, :, :], "state")):
                sp.dma_start(dst, I[name]).then_inc(mixer_in, 16)
            with sp.Fori(2, NZ // 2) as i:
                for j in range(2):
                    load(i * 2 + (Z0 + j), j, I["w_in"][i * 2 + j])
            for j in range(2):
                load(WOUT + j, j, I["w_out"][j])
            sp.wait_ge(v_ready, 2)
            sp.dma_start(O["ikT"], z[0:HD, IK, :]).then_inc(stored, 16)
            sp.dma_start(O["vT"], z[:, AV, :]).then_inc(stored, 16)
            sp.wait_ge(qk_ready, 5)
            sp.dma_start(O["kT"], z[:, AK, :]).then_inc(stored, 16)
            sp.wait_ge(s_ready, NPROMPT // GBLOCK)
            for r in range(2):
                rows = slice(GLA_DK * r, GLA_DK * (r + 1))
                sp.dma_start(O["state_prompt"][rows], state[rows, :, (NPROMPT // GBLOCK) % 9, GLA_DV * r:GLA_DV * (r + 1)]).then_inc(stored, 16)
            sp.wait_ge(s_ready, STEPS)
            for r in range(2):
                rows = slice(GLA_DK * r, GLA_DK * (r + 1))
                sp.dma_start(O["state_sample"][rows], state[rows, :, (STEPS + 1) % 9, GLA_DV * r:GLA_DV * (r + 1)]).then_inc(stored, 16)
            with sp.Fori(1, KD // 2) as i:
                for j in range(2):
                    load(i * 2 + (WOUT + j), j, I["w_out"][i * 2 + j])
            load_ffn(2, FFN2, DOWN2)
            for k in range(KD):
                sp.wait_ge(y_ready, k + 1)
                sp.dma_start(O["yT"][:, k, :], tmp_a[:, k % 2, :] if k % 4 < 2 else tmp_b[:, k % 2, :]).then_inc(y_stored[k % 4], 16)
            for n in range(4):
                sp.wait_ge(y_stored[n], 16 * KD // 4)
            sp.wait_ge(stored, 16 * 7)

        @block.gpsimd
        def _(pool):
            pool.sem_inc(split, CREDIT)
            pool.memset(ones[:, :], 1.0).then_inc(consts_ready, 1)
            pool.memset(eps[:, :], EPS).then_inc(consts_ready, 1)

            def low_half(u, slot, nk=KD):
                pool.wait_ge(rounded, u + 1)
                pool.tensor_tensor(w_lo[:, slot, 0:nk, :], raw[:, slot, 0:nk, :], w_hi[:, slot, 0:nk, :].bitcast(F32),
                                   ALU.subtract).then_inc(split, 1)

            def ahead(first, down_first, next_size):
                with pool.Fori(0, NF // 2 - 1) as i:
                    for s in range(4):
                        low_half(i * 4 + (first + 2 + s), s % 2)
                for s in range(4):
                    low_half(down_first - 2 + s, s % 2, KD if s < 2 else DOWN_PARTS[s % 2][1])
                with pool.Fori(0, KD // 2 - 1) as i:
                    for q in range(8):
                        low_half(i * 8 + (down_first + 2 + q), q % 2, DOWN_PARTS[q % 2][1])
                for q in range(6):
                    low_half(down_first + 4 * KD - 6 + q, q % 2, DOWN_PARTS[q % 2][1])
                for s in range(2 if next_size else 0):
                    low_half(down_first + 4 * KD + s, s, next_size)

            def paired(first, count):
                with pool.Fori(0, count // 2) as i:
                    for s in range(2):
                        low_half(i * 2 + (first + s), s)

            def scale_odd(n):
                pool.wait_ge(rstd_ready, n + 1)
                for k in range(1, KD, 2):
                    if k > 1:
                        pool.wait_ge(shifted, KD * n + k - 1)
                    pool.tensor_tensor(tmp_a[:, 1, :], x[:, k, :], rstd[:, :], ALU.mult).then_inc(scaled_odd, 1)

            for s in range(2):
                low_half(s, s)
            scale_odd(0)
            ahead(FFN1, DOWN1, KD)
            scale_odd(1)
            paired(Z0 + 2, NZ)
            pool.wait_ge(mixer_in, MIXER_LOADS)
            for i, (t0, nt, _, _) in enumerate(TILES):
                for half in range(nt // (4 * GBLOCK)):
                    blocks = slice(4 * half, 4 * half + 4)
                    pool.wait_ge(tok_ready, i + 1)
                    if i:
                        pool.wait_ge(u_made, 8 * i - 4 + 4 * half)
                    pool.tensor_tensor(
                        k_block[0:nt, blocks, :],
                        k_tok[0:nt, :].rearrange("p (o n) -> p o n", o=1).to_broadcast([nt, 4, 2 * P]),
                        c("block", nt)[:, blocks].rearrange("p (n o) -> p n o", o=1).to_broadcast([nt, 4, 2 * P]),
                        ALU.mult).then_inc(block_ready, 1)
            paired(WOUT + 2, KD)
            scale_odd(2)
            ahead(FFN2, DOWN2, 0)

        @block.scalar
        def _(act):
            steps = [0]
            for s in (z_ready, silu_ready):
                act.sem_inc(s, SPARE)

            def settle(ins):
                steps[0] += 1
                ins.then_inc(act_step, 1)
                act.wait_ge(act_step, steps[0])

            def round_unit(n, u, slot, nk=KD):
                act.wait_ge(raw_in[slot], n)
                act.wait_ge(used, u + 1)
                act.activation(w_hi[:, slot, 0:nk, :], raw[:, slot, 0:nk, :], ACT.Copy).then_inc(rounded, 1)

            def round_next(u, slot, nk=KD):
                round_unit(16 * (u // 2 + 1), u, slot, nk)

            def norm(n, shift_at):
                act.wait_ge(ss_ready, n + 1)
                act.activation(halves(rstd[:, :]), aux[:, 0:2, 0:HALF], ACT.Sqrt, bias=eps[:, :], scale=1.0 / D).then_inc(rms_ready, 1)
                act.wait_ge(mod_ready, 1 + n)
                for k in range(KD):
                    act.wait_ge(scaled_odd if k % 2 else scaled_even, KD // 2 * n + k // 2 + 1)
                    if KD * n + k >= 2:
                        act.wait_ge(h_ready, KD * n + k - 1)
                    for s, cols in enumerate((slice(0, NPROMPT), slice(NPROMPT, T))):
                        ins = act.activation(tmp_b[:, k % 2, cols], tmp_a[:, k % 2, cols], ACT.Identity,
                                             bias=mod[:, shift_at + k, s:s + 1], scale=scale[:, k, s:s + 1])
                    ins.then_inc(shifted, 1)
                    if k % 2:
                        act.wait_ge(shifted, KD * n + k + 1)
                        act.activation(h_hi[:, k, :], tmp_b[:, 1, :], ACT.Copy).then_inc(h_rounded, 1)

            def ffn(n, first, down_first, next_size):
                done = NF * (n - 1)

                def silu(f):
                    act.wait_ge(used, f * 2 + (first + 1 + CREDIT))
                    act.wait_ge(g_full, f + (done + SPARE))
                    act.activation(halves(tmp_a[:, 0, :]), accumulator(0), ACT.Silu).then_inc(silu_ready, 1)

                act.preload_act_table(ACT.Silu)
                with act.Fori(0, NF // 2 - 1) as i:
                    for s in range(4):
                        round_unit(i * 32 + (8 * first + 16 * (s // 2) + 32), i * 4 + (first + 2 + s), s % 2)
                        if s % 2 == 0:
                            silu(i * 2 + s // 2)
                for s in range(4):
                    round_next(down_first - 2 + s, s % 2, KD if s < 2 else DOWN_PARTS[s % 2][1])
                    if s % 2 == 0:
                        silu(NF - 2 + s // 2)
                with act.Fori(0, KD // 2 - 1) as i:
                    for q in range(8):
                        round_unit(i * 64 + (8 * down_first + 16 * (q // 2) + 32), i * 8 + (down_first + 2 + q), q % 2,
                                   DOWN_PARTS[q % 2][1])
                for q in range(6):
                    round_next(down_first + 4 * KD - 6 + q, q % 2, DOWN_PARTS[q % 2][1])
                for s in range(2 if next_size else 0):
                    round_next(down_first + 4 * KD + s, s, next_size)

            act.wait_ge(small_in, 48)
            act.activation(scond[:, :, :], cond[:, :, :], ACT.Silu).then_inc(cond_ready, 1)
            act.wait_ge(consts_ready, 2)
            for k in range(KD):
                act.wait_ge(x_in, 16)
                if k >= 2:
                    act.wait_ge(sumsq_ready, k - 1)
                act.activation(tmp_b[:, k % 2, :], x[:, k, :], ACT.Square).then_inc(sq_ready, 1)
            for s in range(2):
                round_next(s, s)
            norm(0, 0)
            ffn(1, FFN1, DOWN1, KD)
            norm(1, 3 * KD)

            def z_pair(i):
                for j in range(2):
                    round_unit(i * 16 + (8 * Z0 + 32), i * 2 + (Z0 + 2 + j), j)
                    act.wait_ge(used, i * 2 + (Z0 + j + 1 + CREDIT))
                    act.activation(halves(z[:, bass.ds(i * 2 + j, 1), :].rearrange("p o n -> p (o n)")), accumulator(j),
                                   ACT.Copy).then_inc(z_ready, 1)

            with act.Fori(0, 2) as i:
                z_pair(i)
            act.wait_ge(iw_made, 1)
            act.activation(iw[:, 0:3, :], aux[:, 0, 0:96].rearrange("p (i n) -> p i n", i=3), ACT.Copy,
                           scale=(IDX_HEADS * HD) ** -0.5)
            act.activation(iw[0:NSAMPLE, 3, :], aux[0:NSAMPLE, 0, 96:128], ACT.Copy,
                           scale=(IDX_HEADS * HD) ** -0.5).then_inc(iw_ready, 1)
            for m in range(4 * IDX_HEADS):
                _, nq, nk, _ = TILES[1 + m // IDX_HEADS]
                act.wait_ge(logit_made, m + 1)
                if m >= 2:
                    act.wait_ge(logit_used, m - 1)
                act.activation(tmp_a[0:nq, m % 2, 0:nk], aux[0:nq, 1 + m % 3, 0:nk], ACT.Relu).then_inc(relu_ready, 1)
            z_pair(2)
            for j in range(2):
                act.wait_ge(za_made, j + 1)
                ins = act.activation(halves(exp_q[:, j, :]), wide(j), ACT.Identity, bias=b_a[:, j:j + 1])
                if j == 0:
                    ins.then_inc(act_step, 1)
                    steps[0] += 1
            settle(ins)
            for f, scaling, shift in ((ACT.Abs, 1.0, 0.0), (ACT.Exp, -1.0, 0.0), (ACT.Ln, 1.0, 1.0)):
                source = exp_q if f == ACT.Abs else exp_k
                settle(act.activation(exp_k[:, :, :], source[:, :, :], f, bias=shift, scale=scaling))
            act.sem_inc(log_ready, 1)
            z_pair(3)
            act.wait_ge(decay_ready, 1)
            act.activation(exp_q[:, :, :], decay[:, :, :], ACT.Exp, scale=1.0 / TAU).then_inc(exp_ready, 1)
            act.activation(exp_k[:, :, :], decay[:, :, :], ACT.Exp, scale=-1.0 / TAU).then_inc(exp_ready, 1)
            act.activation(etot[:, :, :], decay[:, :, GBLOCK - 1:T:GBLOCK], ACT.Exp, scale=1.0 / TAU).then_inc(exp_ready, 1)
            z_pair(4)
            act.wait_ge(decay_ready, 2)
            settle(act.activation(exp_end[:, :, :], exp_end[:, :, :], ACT.Exp, scale=1.0 / TAU))
            act.sem_inc(exp_ready, 1)
            act.wait_ge(v_turned, 1)
            act.activation(v_prompt[:, :, :], aux[:, 0, :].rearrange("p (i n) -> p i n", i=4), ACT.Copy).then_inc(v_ready, 1)
            act.activation(v_sample[0:NSAMPLE, 2, :], aux[0:NSAMPLE, 1, 0:P], ACT.Copy).then_inc(v_ready, 1)
            z_pair(5)
            act.wait_ge(qk_ss, 5)
            act.activation(halves(rstd[0:10, :]), aux[0:10, 2:4, 0:HALF], ACT.Sqrt, bias=eps[0:10, :],
                           scale=1.0 / HD).then_inc(qk_rms, 1)
            with act.Fori(6, NZ // 2) as i:
                z_pair(i)
            act.wait_ge(z_ready, NZ + SPARE)
            act.activation(z[:, GR:GR + 4, :], z[:, GR:GR + 4, :], ACT.Silu).then_inc(gla_silu, 1)

            def turned_tile(i):
                _, nt, _, _ = TILES[i]
                act.wait_ge(tok_made, i + 1)
                if i >= 2:
                    act.wait_ge(inter_made, 8 * (i - 1))
                if i:
                    act.wait_ge(block_ready, 2 * i)
                act.activation(v_tok[0:nt, i % 2, :], acc[0:nt, 0, :], ACT.Copy)
                act.activation(k_tok[0:nt, :], acc[0:nt, 1, 0:2 * P], ACT.Copy).then_inc(tok_ready, 1)

            def gla_out(i):
                t0, nt, _, _ = TILES[i]
                act.wait_ge(inter_made, min(8 * (i + 1), STEPS))
                for r in range(2):
                    ins = act.activation(z[:, GV + r:GV + 4:2, t0:t0 + nt],
                                         acc[:, 2 + r, 0:2 * P].rearrange("p (h n) -> p h n", h=2)[:, :, 0:nt], ACT.Copy)
                ins.then_inc(o_ready, 1)

            def gla_step(n):
                i, b = n // 8, n % 8
                if b == 2 and 1 <= i <= SAMPLE:
                    gla_out(i - 1)
                if b == 4 and i < SAMPLE:
                    turned_tile(i + 1)
                if n == STEPS + 2:
                    gla_out(SAMPLE)

            def turned(m):
                ti, r = m // HEADS, m % PER_KV
                _, nq, nk, _ = TILES[ti]
                act.wait_ge(pT_made, m + 1)
                if m >= PER_KV:
                    act.wait_ge(pv_made, m // PER_KV)
                full, rest = nk // P, nk % P
                src = aux[:, 1, :].rearrange("p (n q) -> p n q", n=4)
                if rest:
                    act.activation(probs_t[0:rest, full, r, 0:nq], src[0:rest, full, 0:nq], ACT.Copy)
                act.activation(probs_t[:, 0:full, r, 0:nq], src[:, 0:full, 0:nq], ACT.Copy).then_inc(pT_ready, 1)

            def gathered(g):
                ti, kv = g // KV_HEADS, g % KV_HEADS
                t0, nq, _, _ = TILES[ti]
                rows = slice(HD * kv, HD * kv + HD)
                act.wait_ge(pv_made, g + 1)
                act.activation(z[rows, AQ:AQ + 4, t0:t0 + nq],
                               aux[rows, 2, :].rearrange("p (r q) -> p r q", r=4)[:, :, 0:nq], ACT.Copy).then_inc(att_ready, 1)

            turned_tile(0)
            for m in range(SLOTS + 1):
                for n in gla_steps(m):
                    gla_step(n)
                if m == SLOTS - 4:
                    act.wait_ge(gla_ss, 1)
                    act.activation(halves(rstd[0:4, :]), acc[0:4, 0:2, 0:HALF], ACT.Sqrt, bias=eps[0:4, :],
                                   scale=1.0 / GLA_DV).then_inc(gla_rms, 1)
                if m < SLOTS:
                    _, nq, nk, _ = TILES[m // HEADS]
                    act.wait_ge(s_biased, m + 1)
                    act.activation(tmp_a[0:nq, m % 2, 0:nk], tmp_a[0:nq, m % 2, 0:nk], ACT.Exp,
                                   bias=stats[0:nq, m % 2, 1:2], accum_out=stats[0:nq, m % 2, 2:3]).then_inc(p_exp, 1)
                if m >= 1:
                    turned(m - 1)
                    if m % PER_KV == 0:
                        gathered(m // PER_KV - 1)

            act.wait_ge(att_ready, len(TILES) * KV_HEADS)
            for k in range(KD):
                if k < 4:
                    act.wait_ge(gla_in_ready, 2 + 2 * GLA_HEADS)
                source = z[:, GV + k, :] if k < 4 else z[:, AQ + k - 4, :]
                act.activation(h_hi[:, k, :], source, ACT.Copy).then_inc(mix_rounded, 1)

            with act.Fori(0, KD // 2) as i:
                for s in range(2):
                    round_unit(i * 16 + (8 * WOUT + 32), i * 2 + (WOUT + 2 + s), s)
            norm(2, 6 * KD)
            ffn(2, FFN2, DOWN2, 0)
            act.wait_ge(ss_ready, 4)
            act.activation(halves(rstd[:, :]), aux[:, 0:2, 0:HALF], ACT.Sqrt, bias=eps[:, :], scale=1.0 / D).then_inc(rms_ready, 1)

        @block.tensor
        def _(pe):
            pe.sem_inc(used, CREDIT)

            def product(u, slot, b, operand_hi, operand_lo, ks, first=True, last=True, arrives=None):
                pe.wait_ge(split, u + (1 + CREDIT))
                for n, k in enumerate(ks):
                    if arrives:
                        pe.wait_ge(arrives[0], arrives[1] + k + 1)
                    for m, (w, a) in enumerate(((w_hi, operand_hi), (w_hi, operand_lo), (w_lo, operand_hi))):
                        for half in range(2):
                            ins = pe.matmul(acc[:, 2 * b + half, 0:HALF], w[:, slot, n, :],
                                            a[:, k, HALF * half:HALF * (half + 1)],
                                            start=first and n == 0 and m == 0, stop=last and n == len(ks) - 1 and m == 2)
                ins.then_inc(used, 1)

            def mean_square(n):
                pe.wait_ge(sumsq_ready, [8, 16, 24, 32][n])
                for half in range(2):
                    ins = pe.matmul(aux[:, half, 0:HALF], ones[:, :], sumsq[:, HALF * half:HALF * (half + 1)],
                                    start=True, stop=True)
                ins.then_inc(ss_ready, 1)

            def pair_sums(p):
                pe.wait_ge(ada_step, p * 16 + 16)
                pe.wait_ge(ada_kept, p + SPARE)
                for s in range(2):
                    for m in range(2):
                        ins = pe.matmul(aux[:, 3, 2 * m + s:2 * m + s + 1], ada_acc[:, s, P * m:P * m + P], ones[:, 0:1],
                                        start=True, stop=True)
                ins.then_inc(ada_sum, 1)

            def ffn(n, first, down_first):
                done = NF * (n - 1)

                def hidden(f, arrives=None):
                    pe.wait_ge(silu_ready, f + (done + SPARE))
                    product(f * 2 + first, 0, 0, h_hi, h_lo, range(KD), arrives=arrives)
                    pe.wait_ge(g_full, f + (done + SPARE))
                    product(f * 2 + (first + 1), 1, 1, h_hi, h_lo, range(KD))
                    if n == 1:
                        pair_sums(f)

                hidden(0, (h_ready, 2 * KD * (n - 1)))
                hidden(1)
                with pe.Fori(1, NF // 2) as i:
                    for s in range(2):
                        hidden(i * 2 + s)
                pe.wait_ge(g_ready, NF * n + SPARE)
                with pe.Fori(0, KD // 2) as i:
                    for j in range(2):
                        pe.wait_ge(x_added, i * 2 + (2 * KD * (n - 1) + j - 1 + SPARE))
                        for q, (k0, nk) in enumerate(DOWN_PARTS):
                            product(i * 8 + (down_first + 4 * j + q), q % 2, j, g_hi, g_lo, range(k0, k0 + nk),
                                    q == 0, q == 3)
                    if n == 1:
                        pair_sums(i + NF)
                mean_square(2 * n - 1)

            pe.wait_ge(cond_ready, 1)
            pe.wait_ge(consts_ready, 2)
            for u in range(KD):
                pe.wait_ge(start_in[u // 4], 16)
                for k in range(KD):
                    ins = pe.matmul(aux[:, 2, 2 * u:2 * u + 2], ada_units[:, u, k, :], scond[:, k, :],
                                    start=(k == 0), stop=(k == KD - 1))
            ins.then_inc(start_sum, 1)
            mean_square(0)
            for p in range(START_PAIRS):
                pe.wait_ge(start_pair_made, p + 1)
                for s in range(2):
                    for m in range(2):
                        u = KD + 2 * p + m
                        ins = pe.matmul(aux[:, 2, 2 * u + s:2 * u + s + 1], start_acc[:, p, s, P * m:P * m + P], ones[:, 0:1],
                                        start=True, stop=True)
            ins.then_inc(start_pair_sum, 1)
            ffn(1, FFN1, DOWN1)

            def z_pair(i, arrives=None):
                for j in range(2):
                    pe.wait_ge(z_ready, i * 2 + (j - 1 + SPARE))
                    product(i * 2 + (Z0 + j), j, j, h_hi, h_lo, range(KD), arrives=arrives if j == 0 else None)

            for i in range(2):
                z_pair(i, (h_ready, KD) if i == 0 else None)
                pair_sums(i + (NF + KD // 2))
            pe.wait_ge(z_ready, 4 + SPARE)
            pe.wait_ge(mixer_in, MIXER_LOADS)
            pe.wait_ge(ada_kept, BESIDE + SPARE)
            for n, (t0, nq, _, _) in enumerate(TILES[1:]):
                ins = pe.transpose(aux[0:nq, 0, 32 * n:32 * n + 32], z[0:32, GA, t0:t0 + nq], ident[0:32, 0:32])
            ins.then_inc(iw_made, 1)
            for m in range(4 * IDX_HEADS):
                t0, nq, nk, _ = TILES[1 + m // IDX_HEADS]
                h = m % IDX_HEADS
                rows = slice(HD * (h % 2), HD * (h % 2) + HD)
                if m >= 3:
                    pe.wait_ge(relu_ready, m - 2)
                if m // IDX_HEADS == 3:
                    pe.wait_ge(logit_used, 3 * IDX_HEADS)
                keys = ikT_sample[rows, :] if m // IDX_HEADS == 3 else z[rows, IK, 0:nk]
                pe.matmul(aux[0:nq, 1 + m % 3, 0:nk], z[rows, IQ + h // 2, t0:t0 + nq], keys,
                          start=True, stop=True).then_inc(logit_made, 1)
            pe.wait_ge(relu_ready, 4 * IDX_HEADS)
            for j in range(2):
                for half in range(2):
                    ins = pe.matmul(aux[:, 2 * j + half, 0:HALF], w_a2[:, P * j:P * j + P],
                                    z[0:LOWRANK, GA, HALF * half:HALF * (half + 1)], start=True, stop=True)
                ins.then_inc(za_made, 1)
            with pe.Fori(2, 5) as i:
                z_pair(i)
            pe.wait_ge(z_ready, AV + 1 + SPARE)
            pe.wait_ge(log_ready, 1)
            for i in range(4):
                pe.transpose(aux[:, 0, P * i:P * i + P], z[:, AV, P * i:P * i + P], ident)
            pe.transpose(aux[0:NSAMPLE, 1, 0:P], z[:, AV, NPROMPT:T], ident).then_inc(v_turned, 1)
            z_pair(5)
            for j in range(5):
                pe.wait_ge(qk_sq, j + 1)
                for half in range(2):
                    ins = pe.matmul(aux[0:10, 2 + half, 0:HALF], qk_sum[:, j, :],
                                    (tmp_a if j % 4 < 2 else tmp_b)[:, j % 2, HALF * half:HALF * (half + 1)],
                                    start=(j == 0), stop=(j == 4))
                ins.then_inc(qk_ss, 1)
            z_pair(6)
            z_pair(7)
            pe.wait_ge(qk_rstd, 1)
            pe.wait_ge(v_ready, 2)
            for j in range(5):
                if j >= 2:
                    pe.wait_ge(qk_ready, j - 1)
                for half in range(2):
                    ins = pe.matmul(aux[:, 2 * (j % 2) + half, 0:HALF], qk_spread[0:10, j, :],
                                    rstd[0:10, HALF * half:HALF * (half + 1)], start=True, stop=True)
                ins.then_inc(qk_wide, 1)
                if j == 1 or j == 3:
                    z_pair(8 + j // 2)
            z_pair(10)

            def turn_tile(i):
                t0, nt, _, _ = TILES[i]
                if i:
                    pe.wait_ge(attn_ready, i)
                for h in range(GLA_HEADS):
                    pe.transpose(acc[0:nt, 0, P * h:P * h + P], z[:, GV + h, t0:t0 + nt], ident)
                for j in range(2):
                    ins = pe.transpose(acc[0:nt, 1, P * j:P * j + P], z[:, GK + j, t0:t0 + nt], ident)
                ins.then_inc(tok_made, 1)

            def tile_scores(i):
                t0, nt, _, _ = TILES[i]
                pe.wait_ge(tok_ready, i + 1)
                for h in range(GLA_HEADS):
                    rows = slice(GLA_DK * (h % 2), GLA_DK * (h % 2) + GLA_DK)
                    ins = pe.matmul(acc[0:nt, h % 2, P * (h // 2):P * (h // 2) + nt], k_dec[rows, h // 2, t0:t0 + nt],
                                    z[rows, GQ + h // 2, t0:t0 + nt], start=True, stop=True)
                ins.then_inc(attn_made, 1)

            def addition(n):
                i, b = n // 8, n % 8
                _, nt, _, _ = TILES[i]
                pe.wait_ge(block_ready, 2 * i + b // 4 + 1)
                if n:
                    pe.wait_ge(s_ready, n)
                for j in range(2):
                    ins = pe.matmul(aux[:, 3, 256 * j:256 * j + 256], k_block[0:nt, b, P * j:P * j + P],
                                    v_tok[0:nt, i % 2, 256 * j:256 * j + 256], start=True, stop=True)
                ins.then_inc(u_made, 1)

            def within(i):
                _, nt, _, _ = TILES[i]
                pe.wait_ge(attn_ready, i + 1)
                if i:
                    pe.wait_ge(o_ready, i)
                for h in range(GLA_HEADS):
                    at_h = P * (h // 2)
                    ins = pe.matmul(acc[:, 2 + h % 2, at_h:at_h + nt], v_tok[0:nt, i % 2, P * h:P * h + P],
                                    attn[0:nt, i % 2, h, 0:nt], start=(h < 2), stop=False, skip_group_check=True)
                if nt < P:
                    ins.then_inc(o_within, 1)
                    pe.wait_ge(o_within, 1)

            def from_state(n):
                i, b = n // 8, n % 8
                t0 = TILES[i][0] + GBLOCK * b
                if n % (NPROMPT // GBLOCK) == 0:
                    pe.wait_ge(s_first, 1 + n // (NPROMPT // GBLOCK))
                else:
                    pe.wait_ge(s_ready, n)
                for h in range(GLA_HEADS):
                    r = h % 2
                    rows = slice(GLA_DK * r, GLA_DK * r + GLA_DK)
                    at_h = P * (h // 2) + GBLOCK * b
                    ins = pe.matmul(acc[:, 2 + r, at_h:at_h + GBLOCK],
                                    state[rows, h // 2, state_slot(n), GLA_DV * r:GLA_DV * (r + 1)],
                                    z[rows, GQ + h // 2, t0:t0 + GBLOCK],
                                    start=False, stop=(b == 7 or n == STEPS - 1), skip_group_check=True)
                ins.then_inc(inter_made, 1)

            def gla_step(n):
                i, b = n // 8, n % 8
                if n < STEPS:
                    addition(n)
                if b == 2 and n < STEPS:
                    within(i)
                if 2 <= n < STEPS + 2:
                    from_state(n - 2)
                if b == 3 and i < SAMPLE:
                    turn_tile(i + 1)
                if b == 6 and i < SAMPLE:
                    tile_scores(i + 1)

            def gla_mean_square():
                for h in range(GLA_HEADS):
                    pe.wait_ge(gla_sq, h + 1)
                    for half in range(2):
                        ins = pe.matmul(acc[0:4, half, 0:HALF], gla_sum[:, h, :],
                                        gla_square[:, h, HALF * half:HALF * (half + 1)], start=(h == 0), stop=(h == 3))
                ins.then_inc(gla_ss, 1)

            def gla_spread_out(h):
                pe.wait_ge(gla_rstd, 1)
                if h >= 2:
                    pe.wait_ge(gla_in_ready, 2 + 2 * (h - 2) + 1)
                for half in range(2):
                    ins = pe.matmul(acc[:, 2 * (h % 2) + half, 0:HALF], gla_spread[0:4, h, :],
                                    rstd[0:4, HALF * half:HALF * (half + 1)], start=True, stop=True)
                ins.then_inc(gla_wide, 1)

            def turn(m):
                _, nq, nk, _ = TILES[m // HEADS]
                pe.wait_ge(p_ready, m + 1)
                if m:
                    pe.wait_ge(pT_ready, m)
                for n in range(-(-nk // P)):
                    w = min(P, nk - P * n)
                    ins = pe.transpose(aux[0:w, 1, P * n:P * n + nq], tmp_a[0:nq, m % 2, P * n:P * n + w],
                                       ident[0:nq, 0:nq])
                ins.then_inc(pT_made, 1)

            def weigh(g):
                ti, kv = g // KV_HEADS, g % KV_HEADS
                _, nq, nk, _ = TILES[ti]
                v = v_sample if ti == SAMPLE else v_prompt
                pe.wait_ge(pT_ready, PER_KV * (g + 1))
                if g:
                    pe.wait_ge(att_ready, g)
                last = -(-nk // P) - 1
                for n in range(last + 1):
                    w = min(P, nk - P * n)
                    if nq == P:
                        out, rhs = aux[HD * kv:HD * kv + HD, 2, :], probs_t[0:w, n, :, :].rearrange("p r q -> p (r q)")
                    else:
                        out = aux[HD * kv:HD * kv + HD, 2, :].rearrange("p (r q) -> p r q", r=4)[:, :, 0:nq]
                        rhs = probs_t[0:w, n, :, 0:nq]
                    ins = pe.matmul(out, v[0:w, n, HD * kv:HD * kv + HD], rhs, start=(n == 0), stop=(n == last))
                ins.then_inc(pv_made, 1)

            pe.wait_ge(gla_in_ready, 2)
            pe.wait_ge(z_ready, NZ + SPARE)
            turn_tile(0)
            tile_scores(0)
            pe.wait_ge(qk_ready, 5)
            for m in range(SLOTS + 1):
                if m < SLOTS:
                    ti, kv, r = m // HEADS, m % HEADS // PER_KV, m % PER_KV
                    t0, nq, nk, _ = TILES[ti]
                    rows = slice(HD * kv, HD * kv + HD)
                    if m:
                        pe.wait_ge(s_biased, m)
                    keys = kT_sample[rows, :] if ti == SAMPLE else z[rows, AK, 0:nk]
                    pe.matmul(aux[0:nq, 0, 0:nk], z[rows, AQ + r, t0:t0 + nq], keys, start=True, stop=True).then_inc(s_made, 1)
                for n in gla_steps(m):
                    gla_step(n)
                if m == SLOTS - 4:
                    gla_mean_square()
                if m == SLOTS - 2:
                    gla_spread_out(0)
                    gla_spread_out(1)
                if m >= 1:
                    turn(m - 1)
                    if m % PER_KV == 0:
                        weigh(m // PER_KV - 1)
                if m == SLOTS - 1:
                    gla_spread_out(2)
                    gla_spread_out(3)

            for j in range(2):
                product(WOUT + j, j, j, h_hi, h_lo, range(KD), arrives=(mix_ready, 0) if j == 0 else None)
            with pe.Fori(1, KD // 2) as i:
                for j in range(2):
                    pe.wait_ge(x_added, i * 2 + (KD + j - 1 + SPARE))
                    product(i * 2 + (WOUT + j), j, j, h_hi, h_lo, range(KD))
            mean_square(2)
            ffn(2, FFN2, DOWN2)

        @block.vector
        def _(vec):
            steps = [0]
            for s in (x_added, g_full, g_ready, ada_used, ada_kept, top_taken):
                vec.sem_inc(s, SPARE)

            def mark(ins):
                steps[0] += 1
                ins.then_inc(vec_step, 1)
                return steps[0]

            def settle(ins):
                vec.wait_ge(vec_step, mark(ins))

            def modulate(n, scale_at, gate_at):
                wide = gains[:, n, :].rearrange("p (k o) -> p k o", o=1).to_broadcast([P, KD, 2])
                settle(vec.tensor_scalar(scale[:, :, :], mod[:, scale_at:scale_at + KD, :], 1.0, None, ALU.add))
                vec.tensor_tensor(scale[:, :, :], scale[:, :, :], wide, ALU.mult).then_inc(mod_ready, 1)

            def out_gate(gate_at, factor):
                settle(vec.tensor_scalar(gate[:, :, :], mod[:, gate_at:gate_at + KD, :], factor, None, ALU.mult))

            def norm(n):
                vec.wait_ge(rms_ready, n + 1)
                vec.reciprocal(rstd[:, :], rstd[:, :]).then_inc(rstd_ready, 1)
                vec.wait_ge(rstd_ready, n + 1)

                def scale_even(k):
                    vec.tensor_tensor(tmp_a[:, 0, :], x[:, k, :], rstd[:, :], ALU.mult).then_inc(scaled_even, 1)

                scale_even(0)
                for k in range(KD):
                    if k % 2 == 0:
                        vec.wait_ge(shifted, KD * n + k + 1)
                        rounded_h = mark(vec.tensor_copy(h_hi[:, k, :], tmp_b[:, 0, :]))
                        if k + 2 < KD:
                            scale_even(k + 2)
                        vec.wait_ge(vec_step, rounded_h)
                    else:
                        vec.wait_ge(h_rounded, KD // 2 * n + k // 2 + 1)
                    vec.tensor_tensor(h_lo[:, k, :], tmp_b[:, k % 2, :], h_hi[:, k, :].bitcast(F32),
                                      ALU.subtract).then_inc(h_ready, 1)

            def pair(p):
                vec.wait_ge(ada_in, p * 16 + 16)
                for k in range(KD):
                    for s in range(2):
                        n = 2 * k + s
                        if k == 0:
                            ins = vec.tensor_scalar(ada_acc[:, s, :], ada[:, k, :], scond[:, k, s:s + 1], None, ALU.mult)
                        else:
                            vec.wait_ge(ada_step, p * 16 + (n - 1))
                            ins = vec.scalar_tensor_tensor(ada_acc[:, s, :], ada[:, k, :], scond[:, k, s:s + 1],
                                                           ada_acc[:, s, :], ALU.mult, ALU.add)
                        ins.then_inc(ada_step, 1)
                vec.wait_ge(ada_step, p * 16 + 16)
                vec.sem_inc(ada_used, 1)

            def keep_pair(p):
                vec.wait_ge(ada_sum, p + 1)
                vec.tensor_tensor(mod[:, bass.ds(p * 2 + 2 * KD, 2), :], aux[:, 3, 0:4].rearrange("p (m s) -> p m s", m=2),
                                  b_ada[:, bass.ds(p * 2 + 2 * KD, 2)].rearrange("p (m o) -> p m o", o=1).to_broadcast([P, 2, 2]),
                                  ALU.add).then_inc(ada_kept, 1)

            def add_out(d, b, count, made):
                vec.wait_ge(used, made)
                a = accumulator(b)
                for lo, hi, s, last in ((0, HALF, 0, 0), (HALF, NPROMPT, 0, 0), (NPROMPT, T, 1, 1)):
                    part = a[:, lo // HALF, lo % HALF:lo % HALF + hi - lo]
                    xs = x[:, bass.ds(d, 1), lo:hi].rearrange("p o n -> p (o n)")
                    gs = gate[:, bass.ds(d, 1), s:s + 1].rearrange("p o n -> p (o n)")
                    ins = vec.scalar_tensor_tensor(xs, part, gs, xs, ALU.mult, ALU.add)
                    if last:
                        ins.then_inc(x_added, 1)
                    else:
                        ins.then_inc(x_part, 1)
                vec.wait_ge(x_added, count + (1 + SPARE))
                vec.wait_ge(x_part, count * 2 + 2)
                xs = x[:, bass.ds(d, 1), :].rearrange("p o n -> p (o n)")
                vec.tensor_tensor(tmp_b[:, b, :], xs, xs, ALU.mult).then_inc(square_made, 1)
                vec.wait_ge(square_made, count + 1)
                vec.wait_ge(sumsq_ready, count + KD)
                vec.tensor_tensor(sumsq[:, :], sumsq[:, :], tmp_b[:, b, :], ALU.add).then_inc(sumsq_ready, 1)

            def zero_sumsq():
                settle(vec.memset(sumsq[:, :], 0.0))

            def ffn(n, added):
                down_first = DOWN1 if n == 1 else DOWN2
                done = NF * (n - 1)
                def hidden(f):
                    if n == 1:
                        pair(f)
                    vec.wait_ge(silu_ready, f + (done + 1) + SPARE)
                    vec.wait_ge(used, f * 2 + ((FFN1 if n == 1 else FFN2) + 2 + CREDIT))
                    vec.wait_ge(g_ready, f + done + SPARE)
                    vec.tensor_tensor(halves(tmp_a[:, 1, :]), halves(tmp_a[:, 0, :]), accumulator(1), ALU.mult).then_inc(g_full, 1)
                    vec.wait_ge(g_full, f + (done + 1) + SPARE)
                    hi = g_hi[:, bass.ds(f, 1), :].rearrange("p o n -> p (o n)")
                    lo = g_lo[:, bass.ds(f, 1), :].rearrange("p o n -> p (o n)")
                    vec.tensor_copy(hi, tmp_a[:, 1, :]).then_inc(g_rounded, 1)
                    vec.wait_ge(g_rounded, f + (done + 1))
                    vec.tensor_tensor(lo, tmp_a[:, 1, :], hi.bitcast(F32), ALU.subtract).then_inc(g_ready, 1)
                    if n == 1:
                        keep_pair(f)

                with vec.Fori(0, NF // 2) as i:
                    for s in range(2):
                        hidden(i * 2 + s)
                if n == 1:
                    vec.wait_ge(ada_kept, NF + SPARE)
                out_gate(2 * KD if n == 1 else 8 * KD, 0.5)
                zero_sumsq()
                with vec.Fori(0, KD // 2) as i:
                    if n == 1:
                        pair(i + NF)
                    for j in range(2):
                        add_out(i * 2 + j, j, i * 2 + (added + j), i * 8 + (down_first + 4 * j + 4 + CREDIT))
                    if n == 1:
                        keep_pair(i + NF)

            def start_pair(p):
                vec.wait_ge(start_in[2 + p // 2], 16)
                for k in range(KD):
                    for s in range(2):
                        if k == 0:
                            ins = vec.tensor_scalar(start_acc[:, p, s, :], ada_pairs[:, p, k, :], scond[:, k, s:s + 1], None, ALU.mult)
                        else:
                            vec.wait_ge(start_step, 16 * p + 2 * k + s - 1)
                            ins = vec.scalar_tensor_tensor(start_acc[:, p, s, :], ada_pairs[:, p, k, :], scond[:, k, s:s + 1],
                                                           start_acc[:, p, s, :], ALU.mult, ALU.add)
                        ins.then_inc(start_step, 1)
                vec.wait_ge(start_step, 16 * p + 16)
                vec.sem_inc(start_pair_made, 1)

            vec.wait_ge(cond_ready, 1)
            start_pair(0)
            start_pair(1)
            vec.wait_ge(x_in, 16)
            settle(vec.memset(sumsq[:, :], 0.0))
            for k in range(KD):
                vec.wait_ge(sq_ready, k + 1)
                if k:
                    vec.wait_ge(sumsq_ready, k)
                vec.tensor_tensor(sumsq[:, :], sumsq[:, :], tmp_b[:, k % 2, :], ALU.add).then_inc(sumsq_ready, 1)
            start_pair(2)
            start_pair(3)
            vec.wait_ge(start_sum, 1)
            vec.wait_ge(start_pair_sum, 1)
            vec.wait_ge(small_in, 48)
            settle(vec.tensor_tensor(mod[:, 0:2 * KD, :], aux[:, 2, 0:4 * KD].rearrange("p (u s) -> p u s", s=2),
                                     b_ada[:, 0:2 * KD].rearrange("p (u o) -> p u o", o=1).to_broadcast([P, 2 * KD, 2]), ALU.add))
            modulate(0, KD, None)
            norm(0)
            ffn(1, 0)
            vec.wait_ge(ada_kept, NF + KD // 2 + SPARE)
            modulate(1, 4 * KD, None)
            norm(1)
            with vec.Fori(0, 2) as i:
                pair(i + (NF + KD // 2))
                keep_pair(i + (NF + KD // 2))

            vec.wait_ge(mixer_in, MIXER_LOADS)
            vec.wait_ge(z_ready, 4 + SPARE)
            mark(vec.tensor_copy(ikT_sample[:, PAST:LSAMPLE], z[:, IK, NPROMPT:T]))
            vec.wait_ge(vec_step, steps[0])
            vec.wait_ge(iw_ready, 1)
            for m in range(4 * IDX_HEADS):
                n, h = m // IDX_HEADS, m % IDX_HEADS
                _, nq, nk, _ = TILES[1 + n]
                vec.wait_ge(relu_ready, m + 1)
                weight = iw[0:nq, n, LOWRANK + h:LOWRANK + h + 1]
                if h == 0:
                    ins = vec.tensor_scalar(score[0:nq, n, 0:nk], tmp_a[0:nq, m % 2, 0:nk], weight, None, ALU.mult)
                else:
                    vec.wait_ge(logit_used, m)
                    ins = vec.scalar_tensor_tensor(score[0:nq, n, 0:nk], tmp_a[0:nq, m % 2, 0:nk], weight,
                                                   score[0:nq, n, 0:nk], ALU.mult, ALU.add)
                ins.then_inc(logit_used, 1)
            vec.wait_ge(logit_used, 4 * IDX_HEADS)
            for n in range(3):
                nk = TILES[1 + n][2]
                mark(vec.memset(score[0:64, n, nk - 64:nk], INADMISSIBLE))
            mark(vec.memset(bias0[:, :], 0.0))
            vec.wait_ge(vec_step, steps[0])
            settle(vec.memset(bias0[0:64, 64:P], DROPPED))

            def top_rounds(start, stop, tiles, before):
                each = len(tiles)
                with vec.Fori(start, stop) as i:
                    for q, n in enumerate(tiles):
                        _, nq, nk, _ = TILES[1 + n]
                        vec.wait_ge(top_taken, i * each + (before - start * each + q) + SPARE)
                        vec.sem_inc(tick, 1)
                        vec.max(top[0:nq, q, :], score[0:nq, n, 0:nk]).then_inc(top_found, 1)
                        vec.wait_ge(top_found, i * each + (before - start * each + q + 1))
                        vec.sem_inc(tick, 1)
                        vec.match_replace(score[0:nq, n, 0:nk], top[0:nq, q, :], score[0:nq, n, 0:nk], TAKEN).then_inc(top_taken, 1)

            rounds_s, rounds_p = TILES[SAMPLE][3], TILES[1][3]
            together = (3, 0, 1, 2)
            top_rounds(0, 3, together, 0)
            vec.wait_ge(log_ready, 1)
            settle(vec.tensor_scalar(exp_q[:, :, :], exp_q[:, :, :], 0.0, None, ALU.min))
            settle(vec.tensor_tensor(exp_q[:, :, :], exp_q[:, :, :], exp_k[:, :, :], ALU.subtract))
            for j in range(2):
                settle(vec.tensor_tensor_scan(decay[:, j, :], c("carry"), exp_q[:, j, :], 0.0, ALU.mult, ALU.add))
            vec.sem_inc(decay_ready, 1)
            blocks = decay[:, :, :].rearrange("p j (b n) -> p j b n", n=GBLOCK)
            for j in range(2):
                ins = vec.tensor_tensor(exp_end[:, j, :].rearrange("p (b n) -> p b n", n=GBLOCK),
                                        blocks[:, j, :, GBLOCK - 1:GBLOCK].to_broadcast([P, T // GBLOCK, GBLOCK]),
                                        blocks[:, j, :, :], ALU.subtract)
                settle(ins)
            vec.sem_inc(decay_ready, 1)
            top_rounds(3, 6, together, 4 * 3)
            vec.wait_ge(z_ready, AQ + 4 + SPARE)
            tiles = [AK, AQ, AQ + 1, AQ + 2, AQ + 3]
            for j, n in enumerate(tiles):
                if j == 4:
                    vec.wait_ge(qk_ss, 1)
                vec.tensor_tensor((tmp_a if j % 4 < 2 else tmp_b)[:, j % 2, :], z[:, n, :], z[:, n, :], ALU.mult).then_inc(qk_sq, 1)
            top_rounds(6, rounds_s, together, 4 * 6)
            vec.wait_ge(qk_rms, 1)
            settle(vec.reciprocal(rstd[0:10, :], rstd[0:10, :]))
            vec.sem_inc(qk_rstd, 1)
            top_rounds(rounds_s, rounds_s + 3, (0, 1, 2), 4 * rounds_s)
            settle(vec.tensor_scalar(gain_q8, gain_q, HD ** -0.5, None, ALU.mult))
            for j, n in enumerate(tiles):
                vec.wait_ge(qk_wide, j + 1)
                vec.scalar_tensor_tensor(halves(z[:, n, :]), halves(z[:, n, :]), gain_k if j == 0 else gain_q8,
                                         wide(j % 2), ALU.mult, ALU.mult).then_inc(qk_ready, 1)
            vec.wait_ge(qk_ready, 5)
            mark(vec.tensor_copy(kT_sample[:, PAST:LSAMPLE], z[:, AK, NPROMPT:T]))
            vec.wait_ge(exp_ready, 4)
            vec.wait_ge(z_ready, GV + SPARE)
            for j in range(2):
                mark(vec.scalar_tensor_tensor(z[:, GQ + j, :], z[:, GQ + j, :], GLA_DK ** -0.5, exp_q[:, j, :], ALU.mult, ALU.mult))
                mark(vec.tensor_tensor(k_dec[:, j, :], z[:, GK + j, :], exp_k[:, j, :], ALU.mult))
                vec.wait_ge(vec_step, steps[0])
                vec.tensor_tensor(z[:, GK + j, :], z[:, GK + j, :], exp_end[:, j, :], ALU.mult).then_inc(gla_in_ready, 1)
            vec.wait_ge(gla_in_ready, 2)
            mark(vec.memset(state[:, :, 0, :], 0.0))
            vec.wait_ge(vec_step, steps[0])
            vec.sem_inc(s_first, 1)

            top_rounds(rounds_s + 3, rounds_p, (0, 1, 2), 4 * rounds_s + 9)
            vec.wait_ge(top_taken, 4 * rounds_s + 3 * (rounds_p - rounds_s) + SPARE)
            for n in range(4):
                _, nq, nk, _ = TILES[1 + n]
                mark(vec.tensor_scalar(score[0:nq, n, 0:nk], score[0:nq, n, 0:nk], 0.5 * (INADMISSIBLE + TAKEN), DROPPED,
                                       ALU.is_gt, ALU.mult))
            vec.wait_ge(vec_step, steps[0])


            def tile_mask(i):
                _, nt, _, _ = TILES[i]
                vec.wait_ge(attn_made, i + 1)
                if i >= 2:
                    vec.wait_ge(inter_made, 8 * (i - 1))
                mask = c("causal", nt)[:, 0:nt].bitcast(I32).rearrange("p (o n) -> p o n", o=1).to_broadcast([nt, 2, nt])
                for r in range(2):
                    ins = vec.copy_predicated(attn[0:nt, i % 2, r:4:2, 0:nt], mask,
                                              acc[0:nt, r, 0:2 * P].rearrange("p (h n) -> p h n", h=2)[:, :, 0:nt])
                ins.then_inc(attn_ready, 1)

            def new_state(n):
                if n == NPROMPT // GBLOCK:
                    vec.wait_ge(inter_made, first_free(n))
                    for r in range(2):
                        rows = slice(GLA_DK * r, GLA_DK * (r + 1))
                        mark(vec.tensor_copy(state[rows, :, state_slot(n), GLA_DV * r:GLA_DV * (r + 1)], state_in[rows, :, :]))
                    vec.wait_ge(vec_step, steps[0])
                    vec.sem_inc(s_first, 1)
                elif n:
                    vec.wait_ge(s_ready, n)
                vec.wait_ge(u_made, n + 1)
                if first_free(n) > 0:
                    vec.wait_ge(inter_made, first_free(n))
                old, new = state_slot(n), (state_slot(n) + 1) % 9
                for j in range(2):
                    ins = vec.scalar_tensor_tensor(state[:, j, new, :], state[:, j, old, :], etot[:, j, n:n + 1],
                                                   aux[:, 3, 256 * j:256 * j + 256], ALU.mult, ALU.add)
                ins.then_inc(s_ready, 1)

            def gla_step(n):
                if n < STEPS:
                    new_state(n)
                if n % 8 == 7 and n // 8 < SAMPLE:
                    tile_mask(n // 8 + 1)

            def gla_squares():
                vec.wait_ge(o_ready, len(TILES))
                for h in range(GLA_HEADS):
                    vec.tensor_tensor(gla_square[:, h, :], z[:, GV + h, :], z[:, GV + h, :], ALU.mult).then_inc(gla_sq, 1)

            def gla_finish(h):
                vec.wait_ge(gla_wide, h + 1)
                vec.wait_ge(gla_silu, 1)
                vec.scalar_tensor_tensor(halves(z[:, GV + h, :]), halves(z[:, GV + h, :]), gain_gla,
                                         accumulator(h % 2), ALU.mult, ALU.mult).then_inc(gla_in_ready, 1)
                vec.wait_ge(gla_in_ready, 2 + 2 * h + 1)
                vec.tensor_tensor(z[:, GV + h, :], z[:, GV + h, :], z[:, GR + h, :], ALU.mult).then_inc(gla_in_ready, 1)

            def scaled_probs(m):
                _, nq, _, _ = TILES[m // HEADS]
                nk = TILES[m // HEADS][2]
                vec.wait_ge(p_exp, m + 1)
                settle(vec.reciprocal(stats[0:nq, m % 2, 3:4], stats[0:nq, m % 2, 2:3]))
                vec.tensor_scalar(tmp_a[0:nq, m % 2, 0:nk], tmp_a[0:nq, m % 2, 0:nk], stats[0:nq, m % 2, 3:4], None,
                                  ALU.mult).then_inc(p_ready, 1)

            vec.wait_ge(z_ready, NZ + SPARE)
            settle(vec.memset(attn[:, :, :, :], 0.0))
            tile_mask(0)
            for m in range(SLOTS + 1):
                if m < SLOTS:
                    ti = m // HEADS
                    _, nq, nk, _ = TILES[ti]
                    first_dist = 384 - (P * ti if ti != SAMPLE else PAST)
                    dist = c("dist", nq)[:, first_dist:first_dist + nk]
                    dropped = bias0[0:nq, 0:nk] if ti == 0 else score[0:nq, ti - 1, 0:nk]
                    slant = tmp_b[0:nq, m % 2, 0:nk]
                    slanted = mark(vec.scalar_tensor_tensor(slant, dist, -(2.0 ** -(m % HEADS + 1)), dropped,
                                                            ALU.mult, ALU.add))
                for n in gla_steps(m):
                    gla_step(n)
                if m < SLOTS:
                    vec.wait_ge(vec_step, slanted)
                    vec.wait_ge(s_made, m + 1)
                    if m >= 2:
                        vec.wait_ge(pT_made, m - 1)
                    settle(vec.tensor_tensor_reduce(tmp_a[0:nq, m % 2, 0:nk], aux[0:nq, 0, 0:nk], slant,
                                                    1.0, TAKEN, ALU.add, ALU.max, stats[0:nq, m % 2, 0:1]))
                    vec.tensor_scalar(stats[0:nq, m % 2, 1:2], stats[0:nq, m % 2, 0:1], -1.0, None, ALU.mult).then_inc(s_biased, 1)
                if m == SLOTS - 5:
                    gla_squares()
                if m == SLOTS - 3:
                    vec.wait_ge(gla_rms, 1)
                    settle(vec.reciprocal(rstd[0:4, :], rstd[0:4, :]))
                    vec.sem_inc(gla_rstd, 1)
                if m:
                    scaled_probs(m - 1)
                if m == SLOTS - 1:
                    gla_finish(0)
                    gla_finish(1)
            gla_finish(2)
            gla_finish(3)

            for k in range(KD):
                source = z[:, GV + k, :] if k < 4 else z[:, AQ + k - 4, :]
                vec.wait_ge(mix_rounded, k + 1)
                vec.tensor_tensor(h_lo[:, k, :], source, h_hi[:, k, :].bitcast(F32), ALU.subtract).then_inc(mix_ready, 1)
            out_gate(5 * KD, 1.0)
            zero_sumsq()
            with vec.Fori(0, KD // 2) as i:
                for j in range(2):
                    add_out(i * 2 + j, j, i * 2 + (KD + j), i * 2 + (WOUT + j + 1 + CREDIT))
            modulate(2, 7 * KD, None)
            norm(2)
            vec.wait_ge(stored, 16 * 7)
            ffn(2, 2 * KD)
            vec.wait_ge(rms_ready, 4)
            settle(vec.reciprocal(rstd[:, :], rstd[:, :]))
            for k in range(KD):
                if k >= 4:
                    vec.wait_ge(y_stored[k % 4], 16 * (k // 4))
                y = (tmp_a if k % 4 < 2 else tmp_b)[:, k % 2, :]
                vec.scalar_tensor_tensor(y, x[:, k, :], gains[:, 3, k:k + 1], rstd[:, :], ALU.mult, ALU.mult).then_inc(y_ready, 1)


def constants():
    p = np.arange(P)
    out = np.zeros((P, NCONST), np.float32)

    def put(name, value, rows=P):
        a, w = CONST_AT[name]
        out[0:rows, a:a + w] = np.asarray(value, np.float32).reshape(rows, w)

    put("ident", np.eye(P))
    put("causal", (p[:, None] // GBLOCK == p[None, :] // GBLOCK) & (p[:, None] <= p[None, :]))
    put("block", p[:, None] // GBLOCK == np.arange(8)[None, :])
    put("carry", np.tile(np.arange(T) % GBLOCK != 0, (P, 1)))
    put("dist", np.abs(np.arange(512)[None, :] - 384 - p[:, None]))
    row = np.arange(10)
    tile = np.arange(5)
    belongs = row[None, None, :] == 2 * tile[None, :, None] + p[:, None, None] // HD
    put("qk_sum", belongs)
    put("qk_spread", belongs.transpose(2, 1, 0), 10)
    head = np.arange(4)
    own = np.broadcast_to(head[None, :, None] == head[None, None, :], (P, 4, 4))
    put("gla_sum", own)
    put("gla_spread", own.transpose(2, 1, 0), 4)
    return out


INPUTS = {
    "x": (P, KD, T), "cond": (P, KD, 2), "b_ada": (P, 9 * KD), "gains": (P, 4, KD), "small": (P, 6), "const": (P, NCONST),
    "w_ada_units": (P, KD, D), "w_ada_pairs": (NPAIR, P, 2 * D), "w_in": (NZ, P, D), "w_a2": (LOWRANK, 2 * P),
    "w_out": (KD, P, D), "w1_gate": (NF, P, D), "w1_up": (NF, P, D), "w1_down": (KD, P, DFF),
    "w2_gate": (NF, P, D), "w2_up": (NF, P, D), "w2_down": (KD, P, DFF),
    "cache_kT": (P, PAST), "cache_ikT": (P, PAST), "cache_v": (P, 2, P), "state": (P, 2, GLA_DV),
}
OUTPUTS = {"yT": (P, KD, T), "kT": (P, T), "vT": (P, T), "ikT": (HD, T), "state_prompt": (P, 2, GLA_DV),
           "state_sample": (P, 2, GLA_DV)}


def laid_out(v):
    v = {n: np.asarray(a) for n, a in v.items()}

    def units(w):
        k, n = w.shape
        return w.reshape(k // P, P, n // P, P).transpose(2, 1, 0, 3).reshape(n // P, P, k)

    def by_partition(a):
        return a.reshape(-1, P).T

    out = {}
    x = np.concatenate([v["x_prompt"][0], v["x_sample"][0]])
    out["x"] = x.T.reshape(KD, P, T).transpose(1, 0, 2)
    c = np.stack([v["c_prompt"][0], v["c_sample"][0]])
    out["cond"] = c.T.reshape(KD, P, 2).transpose(1, 0, 2)
    out["b_ada"] = by_partition(v["b_ada"][0])
    out["gains"] = np.stack([by_partition(v[n][0]) for n in ("g_ffn1", "g_mix", "g_ffn2", "g_out")], axis=1)
    b_a = by_partition(v["b_a"][0])
    out["small"] = np.stack([np.tile(v["g_q"][0], 2), np.tile(v["g_k"][0], 2), v["g_gla"][0],
                             np.zeros(P, np.float32), b_a[:, 0], b_a[:, 1]], axis=1)
    out["const"] = constants()
    ada = units(v["w_ada"][0])
    out["w_ada_units"] = ada[:KD].transpose(1, 0, 2)
    pairs = ada[KD:].reshape(NPAIR, 2, P, KD, P)
    out["w_ada_pairs"] = pairs.transpose(0, 2, 3, 1, 4).reshape(NPAIR, P, 2 * D)
    sizes = (256, 256, 512, LOWRANK, 512, 512, 128, 128, 256, 64, 4)
    gq, gk, gv, ga, gr, aq, ak, av, iq, ik, iw = np.split(v["w_in"][0], np.cumsum(sizes)[:-1], axis=1)
    paired = aq.reshape(D, KV_HEADS, PER_KV, HD).transpose(0, 2, 1, 3).reshape(D, HEADS * HD)
    padding = np.zeros((D, P - LOWRANK - IDX_HEADS), np.float32)
    out["w_in"] = units(np.concatenate([iq, ik, ik, ga, iw, padding, ak, av, paired, gq, gk, gv, gr], axis=1))
    out["w_a2"] = v["w_a2"][0]
    w_out = v["w_out"][0]
    att = w_out[512:].reshape(KV_HEADS, PER_KV, HD, D).transpose(1, 0, 2, 3).reshape(512, D)
    out["w_out"] = units(np.concatenate([w_out[:512], att]))
    for n in ("w1_gate", "w1_up", "w1_down", "w2_gate", "w2_up", "w2_down"):
        out[n] = units(v[n][0])
    out["cache_kT"] = v["cache_k"][0, 0].reshape(PAST, P).T
    ik_past = v["cache_idx_k"][0, 0].T
    out["cache_ikT"] = np.concatenate([ik_past, ik_past])
    out["cache_v"] = v["cache_v"][0, 0].reshape(2, P, P).transpose(1, 0, 2)
    out["state"] = v["state_gla"][0, 0].reshape(2, P, GLA_DV).transpose(1, 0, 2)
    return {n: np.ascontiguousarray(out[n]) for n in INPUTS}


def kernel(**inputs):
    import concourse.bacc as bacc
    from concourse.bass_utils import run_bass_kernel_spmd

    nc = bacc.Bacc("TRN2", target_bir_lowering=False, num_devices=1)
    given = {n: nc.dram_tensor(f"{n}_in", shape, F32, kind="ExternalInput").ap() for n, shape in INPUTS.items()}
    made = {n: nc.dram_tensor(f"{n}_out", shape, F32, kind="ExternalOutput").ap() for n, shape in OUTPUTS.items()}
    program(nc, given, made)
    r = run_bass_kernel_spmd(nc, [{f"{n}_in": a for n, a in laid_out(inputs).items()}], core_ids=[0]).results[0]

    y = r["yT_out"].transpose(2, 1, 0).reshape(T, D)
    k, v = (r[n].T.reshape(T, KV_HEADS, HD) for n in ("kT_out", "vT_out"))
    ik = r["ikT_out"].T
    first, second = (r[n].transpose(1, 0, 2).reshape(1, 1, GLA_HEADS, GLA_DK, GLA_DV)
                     for n in ("state_prompt_out", "state_sample_out"))
    a, b = slice(0, NPROMPT), slice(NPROMPT, T)
    return (y[a][None], y[b][None], k[a][None, None], v[a][None, None], ik[a][None, None], first,
            k[b][None, None], v[b][None, None], ik[b][None, None], second)
```

```python
from contextlib import ExitStack

import numpy as np

import concourse.bass as bass
from concourse import mybir

ALU = mybir.AluOpType
ACT = mybir.ActivationFunctionType
F32 = mybir.dt.float32
F32R = mybir.dt.float32r
I32 = mybir.dt.int32

P = 128
D = 1024
KD = D // P
DFF = 2816
NF = DFF // P
NPROMPT = 512
NSAMPLE = 64
T = NPROMPT + NSAMPLE
HALF = T // 2
PAST = 256
LSAMPLE = PAST + NSAMPLE
CREDIT = 2
LAG = 5
SPARE = 2

GLA_HEADS, GLA_DK, GLA_DV, LOWRANK, GBLOCK = 4, 64, 128, 16, 16
TAU = 16.0
HEADS, KV_HEADS, HD = 8, 2, 64
PER_KV = HEADS // KV_HEADS
IDX_HEADS = 4
EPS = 1e-6
TOPK_PROMPT = min(256, NPROMPT // 4)
TOPK_SAMPLE = min(256, LSAMPLE // 4)
INADMISSIBLE = -3.0e38
TAKEN = -3.4e38
DROPPED = -1.0e30

IQ, IK, GA, AK, AV, AQ, GQ, GK, GV, GR = 0, 2, 3, 4, 5, 6, 10, 12, 14, 18
NZ = 22

BESIDE = (9 * KD - 2 * KD) // 2
MIXER_LOADS = 16 * 7
DOWN_PARTS = ((0, 6), (6, 5), (11, 6), (17, 5))

TILES = [(P * i, P, P * (i + 1), TOPK_PROMPT // 8) for i in range(4)] + [(NPROMPT, NSAMPLE, LSAMPLE, TOPK_SAMPLE // 8)]
SAMPLE = 4

CONST_AT = {}
for _name, _width in (("ident", P), ("causal", P), ("block", 8), ("carry", T), ("dist", 512), ("qk_sum", 50),
                      ("qk_spread", 5 * P), ("gla_sum", 16), ("gla_spread", 4 * P)):
    CONST_AT[_name] = (sum(w for _, w in CONST_AT.values()), _width)
NCONST = sum(w for _, w in CONST_AT.values())


def program(nc, I, O):
    with ExitStack() as ctx:
        at = [-(-nc.sbuf_base // 64) * 64]

        def place(name, shape, dt=F32, offset=None):
            size = 4 * int(np.prod(shape[1:]))
            if offset is None:
                offset = at[0]
                at[0] += -(-size // 32) * 32
            return nc.alloc_sbuf_tensor_at(name, list(shape), dt, offset=offset)

        x = place("x", [P, KD, T])
        mod = place("mod", [P, 9 * KD, 2])
        gains = place("gains", [P, 4, KD])
        scale = place("scale", [P, KD, 2])
        gate = place("gate", [P, KD, 2])
        scalars = place("scalars", [P, 8])
        eps, ada_part = scalars[:, 0:1], scalars[:, 4:8]
        ones = place("ones", [P, P])
        sumsq = place("sumsq", [P, T])
        rstd = place("rstd", [P, T])
        tmp_a = place("tmp_a", [P, 2, T])
        tmp_b = place("tmp_b", [P, 2, T])
        cond_at = at[0]
        cond_all = place("cond_all", [P, 2, D])
        raw = place("raw", [P, 2, KD, P])
        w_hi = place("w_hi", [P, 2, KD, P], F32R)
        w_lo = place("w_lo", [P, 2, KD, P], F32R)
        ada_at = at[0]
        ada = place("ada", [P, 2, D])
        h_at = at[0]
        h_hi = place("h_hi", [P, KD, T], F32R)
        h_lo = place("h_lo", [P, KD, T], F32R)
        g_at = at[0]
        g_hi = place("g_hi", [P, NF, T], F32R)
        g_lo = place("g_lo", [P, NF, T], F32R)
        end = at[0]
        assert end <= nc.sbuf_usable_end
        at[0] = g_at
        ada_units = place("ada_units", [P, KD, KD, P])
        ada_rows = place("ada_rows", [P, KD, D])
        start_part = place("start_part", [P, KD, 2])
        cond = place("cond", [P, KD, 2])
        scond = place("scond", [P, KD, 2])
        assert at[0] <= end
        at[0] = g_at
        z = place("z", [P, NZ, T])
        const = place("const", [P, NCONST])
        score = place("score", [P, 4, 512])
        bias0 = place("bias0", [P, P])
        v_prompt = place("v_prompt", [P, 4, P])
        v_sample = place("v_sample", [P, 3, P])
        kT_sample = place("kT_sample", [P, LSAMPLE])
        ikT_sample = place("ikT_sample", [P, LSAMPLE])
        iw = place("iw", [P, 4, 32])
        w_a2 = place("w_a2", [LOWRANK, 2 * P])
        small = place("small", [P, 8])
        etot = place("etot", [P, 2, T // GBLOCK])
        state_at = at[0]
        state = place("state", [P, 2, 9, GLA_DV])
        gate_parts = place("gate_parts", [P, 8 * T - 2 * 9 * GLA_DV])
        stats = place("stats", [P, 2, 4])
        top = place("top", [P, 4, 8])
        state_in = place("state_in", [P, 2, GLA_DV])
        assert at[0] <= nc.sbuf_usable_end
        after = at[0]
        at[0] = state_at
        decay = place("decay", [P, 2, T])
        exp_q = place("exp_q", [P, 2, T])
        exp_k = place("exp_k", [P, 2, T])
        exp_end = place("exp_end", [P, 2, T])
        assert at[0] <= after
        at[0] = h_at
        q_half = place("q_half", [P, 2, 2, T])
        v_tok = place("v_tok", [P, 2, 4 * GLA_DV])
        k_tok = place("k_tok", [P, 2 * P])
        k_block = place("k_block", [P, 8, 2 * P])
        attn = place("attn", [P, 2, GLA_HEADS, P])
        assert at[0] <= g_at
        k_dec = place("k_dec", [P, 2, T], F32, offset=cond_at)
        y = place("y", [P, KD, T], F32, offset=h_at)
        probs_t = place("probs_t", [P, 4, PER_KV, P], F32, offset=ada_at)

        def c(name, rows=P):
            a, w = CONST_AT[name]
            return const[0:rows, a:a + w]

        ident = c("ident")
        qk_sum = c("qk_sum").rearrange("p (j r) -> p j r", j=5)
        qk_spread = c("qk_spread").rearrange("p (j r) -> p j r", j=5)
        gla_sum = c("gla_sum").rearrange("p (j r) -> p j r", j=4)
        gla_spread = c("gla_spread").rearrange("p (j r) -> p j r", j=4)
        gain_q, gain_k, gain_gla, gain_q8 = (small[:, n:n + 1] for n in range(4))
        b_a = small[:, 4:6]

        acc = ctx.enter_context(nc.psum_tensor("acc", [P, 4, 512], F32))
        aux = ctx.enter_context(nc.psum_tensor("aux", [P, 4, 512], F32))

        def sem(name):
            return ctx.enter_context(nc.semaphore(name))

        def accumulator(b):
            return acc[:, 2 * b:2 * b + 2, 0:HALF]

        def wide(b):
            return aux[:, 2 * b:2 * b + 2, 0:HALF]

        unused_products = aux[:, 2:4, :]
        scaled_x = tmp_a[:, 0, :], tmp_a[:, 1, :], sumsq[:, :]

        def halves(ap):
            return ap.rearrange("p (a n) -> p a n", a=2)

        small_in, x_in, mixer_in = sem("small_in"), sem("x_in"), sem("mixer_in")
        units_in = [sem(f"units_in{n}") for n in range(KD // 2)]
        rows_in = [sem(f"rows_in{n}") for n in range(KD // 2)]
        cond_in, start_step, sumsq_zero = sem("cond_in"), sem("start_step"), sem("sumsq_zero")
        raw_in = [sem(f"raw_in{n}") for n in range(2)]
        ada_in = [sem(f"ada_in{n}") for n in range(2)]
        rounded, split, used = sem("rounded"), sem("split"), sem("used")
        cond_ready, cond_all_ready, start_sum, ada_step, ada_kept = (
            sem(n) for n in ("cond_ready", "cond_all_ready", "start_sum", "ada_step", "ada_kept"))
        mod_ready, shift_ready = sem("mod_ready"), sem("shift_ready")
        consts_ready, sq_ready, sumsq_ready, ss_ready, rms_ready, rstd_ready, scaled_first, scaled, shifted, h_ready = (
            sem(n) for n in ("consts_ready", "sq_ready", "sumsq_ready", "ss_ready", "rms_ready", "rstd_ready",
                             "scaled_first", "scaled", "shifted", "h_ready"))
        silu_ready, g_full, g_rounded, g_ready, x_part, x_added, square_made = (
            sem(n) for n in ("silu_ready", "g_full", "g_rounded", "g_ready", "x_part", "x_added", "square_made"))
        z_ready, mix_rounded, mix_ready = sem("z_ready"), sem("mix_rounded"), sem("mix_ready")
        iw_made, iw_ready, logit_made, relu_ready, logit_used = (
            sem(n) for n in ("iw_made", "iw_ready", "logit_made", "relu_ready", "logit_used"))
        top_found, top_taken, tick = sem("top_found"), sem("top_taken"), sem("tick")
        za_made, log_ready, decay_ready, exp_ready, gla_in_ready = (
            sem(n) for n in ("za_made", "log_ready", "decay_ready", "exp_ready", "gla_in_ready"))
        qk_sq, qk_ss, qk_rms, qk_rstd, qk_wide, qk_ready = (
            sem(n) for n in ("qk_sq", "qk_ss", "qk_rms", "qk_rstd", "qk_wide", "qk_ready"))
        v_turned, v_ready = sem("v_turned"), sem("v_ready")
        tok_made, tok_ready, block_ready, attn_made, attn_ready, u_made, s_ready, inter_made, o_ready, s_first = (
            sem(n) for n in ("tok_made", "tok_ready", "block_ready", "attn_made", "attn_ready", "u_made",
                             "s_ready", "inter_made", "o_ready", "s_first"))
        o_within, attn_zero, q_zero, q_apart = sem("o_within"), sem("attn_zero"), sem("q_zero"), sem("q_apart")
        gla_sq, gla_ss, gla_ss_kept, gla_rms, gla_rstd, gla_wide = (
            sem(n) for n in ("gla_sq", "gla_ss", "gla_ss_kept", "gla_rms", "gla_rstd", "gla_wide"))
        s_made, s_biased, p_exp, p_ready, pT_made, pT_ready, pv_made, att_ready = (
            sem(n) for n in ("s_made", "s_biased", "p_exp", "p_ready", "pT_made", "pT_ready", "pv_made",
                             "att_ready"))
        y_ready, y_gained, y_pool_ready = sem("y_ready"), sem("y_gained"), sem("y_pool_ready")
        Y_POOL, Y_VECTOR = (1, 3, 6), (0, 2, 4, 5, 7)
        stored, y_stored = sem("stored"), sem("y_stored")
        act_step, vec_step = sem("act_step"), sem("vec_step")

        FFN1, DOWN1, Z0, WOUT, FFN2, DOWN2 = np.cumsum([0, 2 * NF, 4 * KD, NZ, KD, 2 * NF]).tolist()

        SLOTS = len(TILES) * HEADS
        STEPS = T // GBLOCK
        DOUBLED = 4
        NORM_SLOT = STEPS + 4 - DOUBLED

        def gla_steps(m):
            return [2 * m, 2 * m + 1] if m < DOUBLED else [m + DOUBLED] if m < NORM_SLOT else []

        def tile_of(m):
            return m // HEADS

        def state_slot(n):
            return (n + n // (NPROMPT // GBLOCK)) % 9

        def first_free(n):
            return n - 7 + n // (NPROMPT // GBLOCK)

        block = ctx.enter_context(nc.Block())

        @block.sync
        def _(sp):
            def load(u, slot, source, nk=KD):
                sp.wait_ge(split, u + 1)
                sp.dma_start(raw[:, slot, 0:nk, :], source.rearrange("p (k n) -> p k n", k=nk)).then_inc(raw_in[slot], 16)

            def load_pair(p):
                for j in range(2):
                    sp.wait_ge(ada_step, p * 4 + (2 * j - 2 + SPARE))
                    sp.dma_start(ada[:, j, :], I["w_ada_rows"][p * 2 + (KD + j)]).then_inc(ada_in[j], 16)

            def load_ffn(n, first, down_first):
                w_gate, w_up, w_down = I[f"w{n}_gate"], I[f"w{n}_up"], I[f"w{n}_down"]
                with sp.Fori(0, NF) as f:
                    load(f * 2 + first, 0, w_gate[f])
                    load(f * 2 + (first + 1), 1, w_up[f])
                    if n == 1:
                        load_pair(f)
                with sp.Fori(0, KD // 2) as i:
                    for j in range(2):
                        for q, (k0, nk) in enumerate(DOWN_PARTS):
                            load(i * 8 + (down_first + 4 * j + q), q % 2, w_down[i * 2 + j][:, k0 * P:(k0 + nk) * P], nk)
                    if n == 1:
                        load_pair(i + NF)

            sp.dma_start(cond[:, :, :], I["cond"]).then_inc(cond_in, 16)
            sp.dma_start(cond_all[:, :, :].rearrange("p s k -> p (s k)"), I["cond_row"].to_broadcast([P, 2 * D])).then_inc(cond_in, 16)
            sp.dma_start(mod[:, :, :], I["b_ada"]).then_inc(small_in, 16)
            sp.dma_start(gains[:, :, :], I["gains"]).then_inc(small_in, 16)

            for n in range(KD // 2):
                sp.dma_start(ada_units[:, 2 * n:2 * n + 2, :, :],
                             I["w_ada_units"][:, 2 * n:2 * n + 2, :].rearrange("p m (k n) -> p m k n", k=KD)
                             ).then_inc(units_in[n], 16)
                sp.dma_start(ada_rows[:, 2 * n:2 * n + 2, :], I["w_ada_rows"][2 * n:2 * n + 2].rearrange("m p k -> p m k")
                             ).then_inc(rows_in[n], 16)
                if n == 1:
                    sp.dma_start(x[:, :, :], I["x"]).then_inc(x_in, 16)
            load_ffn(1, FFN1, DOWN1)
            with sp.Fori(0, 2) as i:
                for j in range(2):
                    load(i * 2 + (Z0 + j), j, I["w_in"][i * 2 + j])
                load_pair(i + (NF + KD // 2))
            sp.wait_ge(used, Z0 + CREDIT)
            for dst, name in ((const[:, :], "const"), (small[:, 0:6], "small"), (w_a2[:, :], "w_a2"),
                              (kT_sample[:, 0:PAST], "cache_kT"), (ikT_sample[:, 0:PAST], "cache_ikT"),
                              (v_sample[:, 0:2, :], "cache_v"), (state_in[:, :, :], "state")):
                sp.dma_start(dst, I[name]).then_inc(mixer_in, 16)
            with sp.Fori(2, NZ // 2) as i:
                for j in range(2):
                    load(i * 2 + (Z0 + j), j, I["w_in"][i * 2 + j])
            for j in range(2):
                load(WOUT + j, j, I["w_out"][j])
            sp.wait_ge(v_ready, 2)
            sp.dma_start(O["ikT"], z[0:HD, IK, :]).then_inc(stored, 16)
            sp.dma_start(O["vT"], z[:, AV, :]).then_inc(stored, 16)
            sp.wait_ge(qk_ready, 5)
            sp.dma_start(O["kT"], z[:, AK, :]).then_inc(stored, 16)
            sp.wait_ge(s_ready, NPROMPT // GBLOCK)
            sp.dma_start(O["state_prompt"], state[:, :, (NPROMPT // GBLOCK) % 9, :]).then_inc(stored, 16)
            sp.wait_ge(s_ready, STEPS)
            sp.dma_start(O["state_sample"], state[:, :, (STEPS + 1) % 9, :]).then_inc(stored, 16)
            with sp.Fori(1, KD // 2) as i:
                for j in range(2):
                    load(i * 2 + (WOUT + j), j, I["w_out"][i * 2 + j])
            load_ffn(2, FFN2, DOWN2)
            for k in range(KD):
                if k in Y_POOL:
                    sp.wait_ge(y_pool_ready, Y_POOL.index(k) + 1)
                else:
                    sp.wait_ge(y_ready, Y_VECTOR.index(k) + 1)
                sp.dma_start(O["yT"][:, k, :], y[:, k, :]).then_inc(y_stored, 16)
            sp.wait_ge(y_stored, 16 * KD)
            sp.wait_ge(stored, 16 * 5)

        @block.gpsimd
        def _(pool):
            pool.sem_inc(split, CREDIT)
            pool.memset(ones[:, :], 1.0).then_inc(consts_ready, 1)
            pool.memset(eps, EPS).then_inc(consts_ready, 1)

            def low_half(u, slot, nk=KD):
                pool.wait_ge(rounded, u + 1)
                pool.tensor_tensor(w_lo[:, slot, 0:nk, :], raw[:, slot, 0:nk, :], w_hi[:, slot, 0:nk, :].bitcast(F32),
                                   ALU.subtract).then_inc(split, 1)

            def ahead(first, down_first, next_size):
                with pool.Fori(0, NF // 2 - 1) as i:
                    for s in range(4):
                        low_half(i * 4 + (first + 2 + s), s % 2)
                for s in range(4):
                    low_half(down_first - 2 + s, s % 2, KD if s < 2 else DOWN_PARTS[s % 2][1])
                with pool.Fori(0, KD // 2 - 1) as i:
                    for q in range(8):
                        low_half(i * 8 + (down_first + 2 + q), q % 2, DOWN_PARTS[q % 2][1])
                for q in range(6):
                    low_half(down_first + 4 * KD - 6 + q, q % 2, DOWN_PARTS[q % 2][1])
                for s in range(2 if next_size else 0):
                    low_half(down_first + 4 * KD + s, s, next_size)

            def paired(first, count):
                with pool.Fori(0, count // 2) as i:
                    for s in range(2):
                        low_half(i * 2 + (first + s), s)

            def scale_tiles(n):
                pool.wait_ge(rstd_ready, 2 * n + 2)
                for k in range(1, KD):
                    if k > 2:
                        pool.wait_ge(shifted, KD * n + k - 2)
                    pool.tensor_tensor(scaled_x[k % 3], x[:, k, :], rstd[:, :], ALU.mult).then_inc(scaled, 1)

            pool.memset(sumsq[:, :], 0.0).then_inc(sumsq_zero, 1)
            pool.wait_ge(sumsq_zero, 1)
            for k in range(KD):
                pool.wait_ge(sq_ready, k + 1)
                if k:
                    pool.wait_ge(sumsq_ready, k)
                pool.tensor_tensor(sumsq[:, :], sumsq[:, :], tmp_b[:, k % 2, :], ALU.add).then_inc(sumsq_ready, 1)
            pool.wait_ge(sumsq_ready, KD)
            for s in range(2):
                low_half(s, s)
            scale_tiles(0)
            ahead(FFN1, DOWN1, KD)
            scale_tiles(1)
            paired(Z0 + 2, NZ)
            pool.wait_ge(z_ready, NZ + SPARE)
            pool.wait_ge(split, WOUT + 2 + CREDIT)
            pool.memset(attn[:, :, :, :], 0.0).then_inc(attn_zero, 1)
            pool.wait_ge(attn_zero, 1)
            pool.wait_ge(mixer_in, MIXER_LOADS)
            for i, (t0, nt, _, _) in enumerate(TILES):
                for half in range(nt // (4 * GBLOCK)):
                    blocks = slice(4 * half, 4 * half + 4)
                    pool.wait_ge(tok_ready, i + 1)
                    if i:
                        pool.wait_ge(u_made, 8 * i - 4 + 4 * half)
                    pool.tensor_tensor(
                        k_block[0:nt, blocks, :],
                        k_tok[0:nt, :].rearrange("p (o n) -> p o n", o=1).to_broadcast([nt, 4, 2 * P]),
                        c("block", nt)[:, blocks].rearrange("p (n o) -> p n o", o=1).to_broadcast([nt, 4, 2 * P]),
                        ALU.mult).then_inc(block_ready, 1)
                    if i == 0 and half == 0:
                        pool.wait_ge(block_ready, 1)
                        for r in range(2):
                            if r:
                                pool.wait_ge(q_zero, 1)
                            rows = slice(GLA_DK * (1 - r), GLA_DK * (2 - r))
                            pool.memset(q_half[rows, :, r, :], 0.0).then_inc(q_zero, 1)
                        pool.wait_ge(q_zero, 2)
            paired(WOUT + 2, KD)
            scale_tiles(2)
            ahead(FFN2, DOWN2, 0)
            pool.wait_ge(rstd_ready, 8)
            for n, k in enumerate(Y_POOL):
                pool.wait_ge(y_gained, n + 1)
                pool.tensor_tensor(y[:, k, :], y[:, k, :], rstd[:, :], ALU.mult).then_inc(y_pool_ready, 1)

        @block.scalar
        def _(act):
            steps = [0]
            for s in (z_ready, silu_ready):
                act.sem_inc(s, SPARE)

            def settle(ins):
                steps[0] += 1
                ins.then_inc(act_step, 1)
                act.wait_ge(act_step, steps[0])

            def round_unit(n, u, slot, nk=KD):
                act.wait_ge(raw_in[slot], n)
                act.wait_ge(used, u + 1)
                act.activation(w_hi[:, slot, 0:nk, :], raw[:, slot, 0:nk, :], ACT.Copy).then_inc(rounded, 1)

            def round_next(u, slot, nk=KD):
                round_unit(16 * (u // 2 + 1), u, slot, nk)

            def rms(n):
                for half in range(2):
                    act.wait_ge(ss_ready, 2 * n + half + 1)
                    act.activation(rstd[:, HALF * half:HALF * (half + 1)], aux[:, half, 0:HALF], ACT.Sqrt, bias=eps,
                                   scale=1.0 / D).then_inc(rms_ready, 1)

            def norm(n, shift_at):
                act.preload_act_table(ACT.Sqrt)
                rms(n)
                if n == 0:
                    for s in range(2):
                        round_next(s, s)
                    act.wait_ge(shift_ready, 1)
                act.wait_ge(mod_ready, 1 + n)
                for k in range(KD):
                    act.wait_ge(scaled if k else scaled_first, (KD - 1) * n + k if k else n + 1)
                    if KD * n + k >= 2:
                        act.wait_ge(h_ready, KD * n + k - 1)
                    source = scaled_x[k % 3]
                    for s, cols in enumerate((slice(0, NPROMPT), slice(NPROMPT, T))):
                        ins = act.activation(tmp_b[:, k % 2, cols], source[:, cols], ACT.Identity,
                                             bias=mod[:, shift_at + k, s:s + 1], scale=scale[:, k, s:s + 1])
                    ins.then_inc(shifted, 1)

            def ffn(n, first, down_first, next_size):
                done = NF * (n - 1)

                def silu(f):
                    act.wait_ge(used, f * 2 + (first + 1 + CREDIT))
                    act.wait_ge(g_full, f + (done + SPARE))
                    act.activation(halves(tmp_a[:, 0, :]), accumulator(0), ACT.Silu).then_inc(silu_ready, 1)

                act.preload_act_table(ACT.Silu)
                with act.Fori(0, NF // 2 - 1) as i:
                    for s in range(4):
                        round_unit(i * 32 + (8 * first + 16 * (s // 2) + 32), i * 4 + (first + 2 + s), s % 2)
                        if s % 2 == 0:
                            silu(i * 2 + s // 2)
                for s in range(4):
                    round_next(down_first - 2 + s, s % 2, KD if s < 2 else DOWN_PARTS[s % 2][1])
                    if s % 2 == 0:
                        silu(NF - 2 + s // 2)
                with act.Fori(0, KD // 2 - 1) as i:
                    for q in range(8):
                        round_unit(i * 64 + (8 * down_first + 16 * (q // 2) + 32), i * 8 + (down_first + 2 + q), q % 2,
                                   DOWN_PARTS[q % 2][1])
                for q in range(6):
                    round_next(down_first + 4 * KD - 6 + q, q % 2, DOWN_PARTS[q % 2][1])
                for s in range(2 if next_size else 0):
                    round_next(down_first + 4 * KD + s, s, next_size)

            act.wait_ge(cond_in, 32)
            act.activation(scond[:, :, :], cond[:, :, :], ACT.Silu).then_inc(cond_ready, 1)
            act.activation(cond_all[:, :, :], cond_all[:, :, :], ACT.Silu).then_inc(cond_all_ready, 1)
            act.wait_ge(consts_ready, 2)
            for k in range(KD):
                act.wait_ge(x_in, 16)
                if k >= 2:
                    act.wait_ge(sumsq_ready, k - 1)
                act.activation(tmp_b[:, k % 2, :], x[:, k, :], ACT.Square).then_inc(sq_ready, 1)
            norm(0, 0)
            ffn(1, FFN1, DOWN1, KD)
            norm(1, 3 * KD)

            def z_pair(i, function=ACT.Copy):
                for j in range(2):
                    round_unit(i * 16 + (8 * Z0 + 32), i * 2 + (Z0 + 2 + j), j)
                    act.wait_ge(used, i * 2 + (Z0 + j + 1 + CREDIT))
                    act.activation(halves(z[:, bass.ds(i * 2 + j, 1), :].rearrange("p o n -> p (o n)")), accumulator(j),
                                   function).then_inc(z_ready, 1)

            with act.Fori(0, 2) as i:
                z_pair(i)
            act.wait_ge(iw_made, 1)
            act.activation(iw[:, 0:3, :], aux[:, 0, 0:96].rearrange("p (i n) -> p i n", i=3), ACT.Copy,
                           scale=(IDX_HEADS * HD) ** -0.5)
            act.activation(iw[0:NSAMPLE, 3, :], aux[0:NSAMPLE, 0, 96:128], ACT.Copy,
                           scale=(IDX_HEADS * HD) ** -0.5).then_inc(iw_ready, 1)
            for m in range(4 * IDX_HEADS):
                _, nq, nk, _ = TILES[1 + m // IDX_HEADS]
                act.wait_ge(logit_made, m + 1)
                if m >= 2:
                    act.wait_ge(logit_used, m - 1)
                act.activation(tmp_a[0:nq, m % 2, 0:nk], aux[0:nq, 1 + m % 3, 0:nk], ACT.Relu).then_inc(relu_ready, 1)
            z_pair(2)
            for j in range(2):
                act.wait_ge(za_made, j + 1)
                ins = act.activation(halves(exp_q[:, j, :]), wide(j), ACT.Identity, bias=b_a[:, j:j + 1])
                if j == 0:
                    ins.then_inc(act_step, 1)
                    steps[0] += 1
            settle(ins)
            for f, scaling, shift in ((ACT.Abs, 1.0, 0.0), (ACT.Exp, -1.0, 0.0), (ACT.Ln, 1.0, 1.0)):
                source = exp_q if f == ACT.Abs else exp_k
                settle(act.activation(exp_k[:, :, :], source[:, :, :], f, bias=shift, scale=scaling))
            act.sem_inc(log_ready, 1)
            z_pair(3)
            act.wait_ge(decay_ready, 1)
            act.activation(exp_q[:, :, :], decay[:, :, :], ACT.Exp, scale=1.0 / TAU).then_inc(exp_ready, 1)
            act.activation(exp_k[:, :, :], decay[:, :, :], ACT.Exp, scale=-1.0 / TAU).then_inc(exp_ready, 1)
            act.activation(etot[:, :, :], decay[:, :, GBLOCK - 1:T:GBLOCK], ACT.Exp, scale=1.0 / TAU).then_inc(exp_ready, 1)
            z_pair(4)
            act.wait_ge(decay_ready, 2)
            settle(act.activation(exp_end[:, :, :], exp_end[:, :, :], ACT.Exp, scale=1.0 / TAU))
            act.sem_inc(exp_ready, 1)
            act.wait_ge(v_turned, 1)
            act.activation(v_prompt[:, :, :], aux[:, 0, :].rearrange("p (i n) -> p i n", i=4), ACT.Copy).then_inc(v_ready, 1)
            act.activation(v_sample[0:NSAMPLE, 2, :], aux[0:NSAMPLE, 1, 0:P], ACT.Copy).then_inc(v_ready, 1)
            z_pair(5)
            act.wait_ge(qk_ss, 5)
            act.activation(halves(rstd[0:10, :]), aux[0:10, 2:4, 0:HALF], ACT.Sqrt, bias=eps[0:10, :],
                           scale=1.0 / HD).then_inc(qk_rms, 1)
            with act.Fori(6, GR // 2) as i:
                z_pair(i)
            act.preload_act_table(ACT.Silu)
            with act.Fori(GR // 2, NZ // 2) as i:
                z_pair(i, ACT.Silu)

            def turned_tile(i):
                _, nt, _, _ = TILES[i]
                act.wait_ge(tok_made, i + 1)
                if i >= 2:
                    act.wait_ge(inter_made, 8 * (i - 1))
                if i:
                    act.wait_ge(block_ready, 2 * i)
                act.activation(v_tok[0:nt, i % 2, :], acc[0:nt, 0, :], ACT.Copy)
                act.activation(k_tok[0:nt, :], acc[0:nt, 1, 0:2 * P], ACT.Copy).then_inc(tok_ready, 1)

            def gla_out(i):
                t0, nt, _, _ = TILES[i]
                act.wait_ge(inter_made, min(8 * (i + 1), STEPS))
                for j in range(2):
                    ins = act.activation(z[:, GV + 2 * j:GV + 2 * j + 2, t0:t0 + nt],
                                         acc[:, 2 + j, 0:2 * P].rearrange("p (h n) -> p h n", h=2)[:, :, 0:nt], ACT.Copy)
                ins.then_inc(o_ready, 1)

            def gla_step(n):
                i, b = n // 8, n % 8
                if b == 2 and 1 <= i <= SAMPLE:
                    gla_out(i - 1)
                if b == 4 and i < SAMPLE:
                    turned_tile(i + 1)
                if n == STEPS + 2:
                    gla_out(SAMPLE)
                if (b == 6 and i) or n == STEPS + 3:
                    t = i - 1 if n < STEPS + 3 else SAMPLE
                    t0, nt, _, _ = TILES[t]
                    act.wait_ge(gla_ss, t + 1)
                    act.activation(rstd[0:4, t0:t0 + nt], acc[0:4, 1, 2 * P:2 * P + nt], ACT.Copy).then_inc(gla_ss_kept, 1)

            def turned(m):
                ti, r = tile_of(m), m % PER_KV
                _, nq, nk, _ = TILES[ti]
                act.wait_ge(pT_made, m + 1)
                if m >= PER_KV:
                    act.wait_ge(pv_made, m // PER_KV)
                full, rest = nk // P, nk % P
                src = aux[:, 1, :].rearrange("p (n q) -> p n q", n=4)
                if rest:
                    act.activation(probs_t[0:rest, full, r, 0:nq], src[0:rest, full, 0:nq], ACT.Copy)
                act.activation(probs_t[:, 0:full, r, 0:nq], src[:, 0:full, 0:nq], ACT.Copy).then_inc(pT_ready, 1)

            def gathered(g):
                ti, kv = tile_of(PER_KV * g), g % KV_HEADS
                t0, nq, _, _ = TILES[ti]
                rows = slice(HD * kv, HD * kv + HD)
                act.wait_ge(pv_made, g + 1)
                act.activation(z[rows, AQ:AQ + 4, t0:t0 + nq],
                               aux[rows, 2, :].rearrange("p (r q) -> p r q", r=4)[:, :, 0:nq], ACT.Copy).then_inc(att_ready, 1)

            turned_tile(0)
            act.preload_act_table(ACT.Exp)
            for r in range(2):
                rows = slice(GLA_DK * r, GLA_DK * (r + 1))
                act.activation(q_half[rows, :, r, :], z[rows, GQ:GQ + 2, :], ACT.Copy).then_inc(q_apart, 1)
            for m in range(SLOTS + 1):
                for n in gla_steps(m):
                    gla_step(n)
                if m == NORM_SLOT:
                    act.wait_ge(gla_ss_kept, len(TILES))
                    act.activation(rstd[0:4, :], rstd[0:4, :], ACT.Sqrt, bias=eps[0:4, :],
                                   scale=1.0 / GLA_DV).then_inc(gla_rms, 1)
                if m < SLOTS:
                    _, nq, nk, _ = TILES[tile_of(m)]
                    act.wait_ge(s_biased, m + 1)
                    act.activation(tmp_a[0:nq, m % 2, 0:nk], tmp_a[0:nq, m % 2, 0:nk], ACT.Exp,
                                   bias=stats[0:nq, m % 2, 1:2], accum_out=stats[0:nq, m % 2, 2:3]).then_inc(p_exp, 1)
                if m >= 1:
                    turned(m - 1)
                    if m % PER_KV == 0:
                        gathered(m // PER_KV - 1)
                if m == SLOTS:
                    for k in range(GLA_HEADS):
                        act.wait_ge(gla_in_ready, 2 + 2 * (k + 1))
                        act.activation(h_hi[:, k, :], z[:, GV + k, :], ACT.Copy).then_inc(mix_rounded, 1)

            act.wait_ge(att_ready, len(TILES) * KV_HEADS)
            for k in range(4, KD):
                act.activation(h_hi[:, k, :], z[:, AQ + k - 4, :], ACT.Copy).then_inc(mix_rounded, 1)

            with act.Fori(0, KD // 2) as i:
                for s in range(2):
                    round_unit(i * 16 + (8 * WOUT + 32), i * 2 + (WOUT + 2 + s), s)
            norm(2, 6 * KD)
            ffn(2, FFN2, DOWN2, 0)
            act.preload_act_table(ACT.Sqrt)
            rms(3)
            for k in Y_POOL:
                act.activation(y[:, k, :], x[:, k, :], ACT.Copy, scale=gains[:, 3, k:k + 1]).then_inc(y_gained, 1)

        @block.tensor
        def _(pe):
            pe.sem_inc(used, CREDIT)

            def product(u, slot, b, operand_hi, operand_lo, ks, first=True, last=True):
                pe.wait_ge(split, u + (1 + CREDIT))
                for n, k in enumerate(ks):
                    for m, (w, a) in enumerate(((w_hi, operand_hi), (w_hi, operand_lo), (w_lo, operand_hi))):
                        for half in range(2):
                            ins = pe.matmul(acc[:, 2 * b + half, 0:HALF], w[:, slot, n, :],
                                            a[:, k, HALF * half:HALF * (half + 1)],
                                            start=first and n == 0 and m == 0, stop=last and n == len(ks) - 1 and m == 2)
                ins.then_inc(used, 1)

            def product_pair(u, arrived, before):
                pe.wait_ge(split, u + 2 + CREDIT)
                for step in range(KD + LAG):
                    for b, k in ((0, step), (1, step - LAG)):
                        if not 0 <= k < KD:
                            continue
                        if b == 0:
                            pe.wait_ge(arrived, before + k + 1)
                        for m, (w, a) in enumerate(((w_hi, h_hi), (w_hi, h_lo), (w_lo, h_hi))):
                            for half in range(2):
                                ins = pe.matmul(acc[:, 2 * b + half, 0:HALF], w[:, b, k, :], a[:, k, HALF * half:HALF * (half + 1)],
                                                start=k == 0 and m == 0, stop=k == KD - 1 and m == 2)
                        if k == KD - 1:
                            ins.then_inc(used, 1)

            def mean_square(n):
                pe.wait_ge(sumsq_ready, [8, 16, 24, 32][n])
                for half in range(2):
                    pe.matmul(aux[:, half, 0:HALF], ones[:, :], sumsq[:, HALF * half:HALF * (half + 1)],
                              start=True, stop=True).then_inc(ss_ready, 1)

            def ffn(n, first, down_first):
                done = NF * (n - 1)

                def hidden(f):
                    pe.wait_ge(silu_ready, f + (done + SPARE))
                    product(f * 2 + first, 0, 0, h_hi, h_lo, range(KD))
                    pe.wait_ge(g_full, f + (done + SPARE))
                    product(f * 2 + (first + 1), 1, 1, h_hi, h_lo, range(KD))

                pe.wait_ge(silu_ready, done + SPARE)
                pe.wait_ge(g_full, done + SPARE)
                product_pair(first, h_ready, 2 * KD * (n - 1))
                hidden(1)
                with pe.Fori(1, NF // 2) as i:
                    for s in range(2):
                        hidden(i * 2 + s)
                for j in range(2):
                    pe.wait_ge(g_full if j else silu_ready, NF * n + SPARE)
                    for q, (k0, nk) in enumerate(DOWN_PARTS):
                        if j == 0:
                            pe.wait_ge(g_ready, NF * (n - 1) + k0 + nk + SPARE)
                        product(down_first + 4 * j + q, q % 2, j, g_hi, g_lo, range(k0, k0 + nk), q == 0, q == 3)
                with pe.Fori(1, KD // 2) as i:
                    for j in range(2):
                        pe.wait_ge(x_added, i * 2 + (2 * KD * (n - 1) + j - 1 + SPARE))
                        for q, (k0, nk) in enumerate(DOWN_PARTS):
                            product(i * 8 + (down_first + 4 * j + q), q % 2, j, g_hi, g_lo, range(k0, k0 + nk),
                                    q == 0, q == 3)
                mean_square(2 * n - 1)

            pe.wait_ge(cond_ready, 1)
            pe.wait_ge(consts_ready, 2)
            for u in range(KD):
                pe.wait_ge(units_in[u // 2], 16)
                for k in range(KD):
                    ins = pe.matmul(aux[:, 2, 2 * u:2 * u + 2], ada_units[:, u, k, :], scond[:, k, :],
                                    start=(k == 0), stop=(k == KD - 1))
                if u == KD - 1:
                    ins.then_inc(start_sum, 1)
                if u == KD - 2:
                    mean_square(0)
            ffn(1, FFN1, DOWN1)

            def z_pair(i):
                for j in range(2):
                    pe.wait_ge(z_ready, i * 2 + (j - 1 + SPARE))
                    product(i * 2 + (Z0 + j), j, j, h_hi, h_lo, range(KD))

            pe.wait_ge(x_added, KD + SPARE)
            product_pair(Z0, h_ready, KD)
            z_pair(1)
            pe.wait_ge(z_ready, 4 + SPARE)
            pe.wait_ge(mixer_in, MIXER_LOADS)
            pe.wait_ge(ada_kept, BESIDE + SPARE)
            for n, (t0, nq, _, _) in enumerate(TILES[1:]):
                ins = pe.transpose(aux[0:nq, 0, 32 * n:32 * n + 32], z[0:32, GA, t0:t0 + nq], ident[0:32, 0:32])
            ins.then_inc(iw_made, 1)
            for m in range(4 * IDX_HEADS):
                t0, nq, nk, _ = TILES[1 + m // IDX_HEADS]
                h = m % IDX_HEADS
                rows = slice(HD * (h % 2), HD * (h % 2) + HD)
                if m >= 3:
                    pe.wait_ge(relu_ready, m - 2)
                if m // IDX_HEADS == 3:
                    pe.wait_ge(logit_used, 3 * IDX_HEADS)
                keys = ikT_sample[rows, :] if m // IDX_HEADS == 3 else z[rows, IK, 0:nk]
                pe.matmul(aux[0:nq, 1 + m % 3, 0:nk], z[rows, IQ + h // 2, t0:t0 + nq], keys,
                          start=True, stop=True).then_inc(logit_made, 1)
            pe.wait_ge(relu_ready, 4 * IDX_HEADS)
            for j in range(2):
                for half in range(2):
                    ins = pe.matmul(aux[:, 2 * j + half, 0:HALF], w_a2[:, P * j:P * j + P],
                                    z[0:LOWRANK, GA, HALF * half:HALF * (half + 1)], start=True, stop=True)
                ins.then_inc(za_made, 1)
            with pe.Fori(2, 5) as i:
                z_pair(i)
            pe.wait_ge(z_ready, AV + 1 + SPARE)
            pe.wait_ge(log_ready, 1)
            for i in range(4):
                pe.transpose(aux[:, 0, P * i:P * i + P], z[:, AV, P * i:P * i + P], ident)
            pe.transpose(aux[0:NSAMPLE, 1, 0:P], z[:, AV, NPROMPT:T], ident).then_inc(v_turned, 1)
            z_pair(5)
            for j in range(5):
                pe.wait_ge(qk_sq, j + 1)
                for half in range(2):
                    ins = pe.matmul(aux[0:10, 2 + half, 0:HALF], qk_sum[:, j, :],
                                    (tmp_a if j % 4 < 2 else tmp_b)[:, j % 2, HALF * half:HALF * (half + 1)],
                                    start=(j == 0), stop=(j == 4))
                ins.then_inc(qk_ss, 1)
            z_pair(6)
            z_pair(7)
            pe.wait_ge(qk_rstd, 1)
            pe.wait_ge(v_ready, 2)
            for j in range(5):
                if j >= 2:
                    pe.wait_ge(qk_ready, j - 1)
                for half in range(2):
                    ins = pe.matmul(aux[:, 2 * (j % 2) + half, 0:HALF], qk_spread[0:10, j, :],
                                    rstd[0:10, HALF * half:HALF * (half + 1)], start=True, stop=True)
                ins.then_inc(qk_wide, 1)
                if j == 1 or j == 3:
                    z_pair(8 + j // 2)
            z_pair(10)

            def turn_tile(i):
                t0, nt, _, _ = TILES[i]
                if i:
                    pe.wait_ge(attn_ready, i)
                for h in range(GLA_HEADS):
                    pe.transpose(acc[0:nt, 0, P * h:P * h + P], z[:, GV + h, t0:t0 + nt], ident)
                for j in range(2):
                    ins = pe.transpose(acc[0:nt, 1, P * j:P * j + P], z[:, GK + j, t0:t0 + nt], ident)
                ins.then_inc(tok_made, 1)

            def tile_scores(i):
                t0, nt, _, _ = TILES[i]
                pe.wait_ge(tok_ready, i + 1)
                for h in range(GLA_HEADS):
                    rows = slice(GLA_DK * (h % 2), GLA_DK * (h % 2) + GLA_DK)
                    ins = pe.matmul(acc[0:nt, h % 2, P * (h // 2):P * (h // 2) + nt], k_dec[rows, h // 2, t0:t0 + nt],
                                    z[rows, GQ + h // 2, t0:t0 + nt], start=True, stop=True)
                ins.then_inc(attn_made, 1)

            def addition(n):
                i, b = n // 8, n % 8
                _, nt, _, _ = TILES[i]
                pe.wait_ge(block_ready, 2 * i + b // 4 + 1)
                if n:
                    pe.wait_ge(s_ready, n)
                for h in range(GLA_HEADS):
                    rows = slice(GLA_DK * (h % 2), GLA_DK * (h % 2) + GLA_DK)
                    ins = pe.matmul(aux[rows, 3, P * (h // 2):P * (h // 2) + P], k_block[0:nt, b, GLA_DK * h:GLA_DK * (h + 1)],
                                    v_tok[0:nt, i % 2, P * h:P * h + P], start=True, stop=True)
                ins.then_inc(u_made, 1)

            def within(i):
                _, nt, _, _ = TILES[i]
                pe.wait_ge(attn_ready, i + 1)
                if i:
                    pe.wait_ge(o_ready, i)
                for h in range(GLA_HEADS):
                    at_h = P * (h % 2)
                    ins = pe.matmul(acc[:, 2 + h // 2, at_h:at_h + nt], v_tok[0:nt, i % 2, P * h:P * h + P],
                                    attn[0:nt, i % 2, h, 0:nt], start=(h % 2 == 0), stop=False, skip_group_check=True)
                if nt < P:
                    ins.then_inc(o_within, 1)
                    pe.wait_ge(o_within, 1)

            def from_state(n):
                i, b = n // 8, n % 8
                t0 = TILES[i][0] + GBLOCK * b
                if n % (NPROMPT // GBLOCK) == 0:
                    pe.wait_ge(s_first, 1 + n // (NPROMPT // GBLOCK))
                else:
                    pe.wait_ge(s_ready, n)
                pe.wait_ge(q_zero, 2)
                pe.wait_ge(q_apart, 2)
                for j in range(2):
                    out = acc[:, 2 + j, 0:2 * P].rearrange("p (r t) -> p r t", r=2)[:, :, GBLOCK * b:GBLOCK * (b + 1)]
                    ins = pe.matmul(out, state[:, j, state_slot(n), :], q_half[:, j, :, t0:t0 + GBLOCK],
                                    start=False, stop=(b == 7 or n == STEPS - 1), skip_group_check=True)
                ins.then_inc(inter_made, 1)

            def gla_addition(n):
                if n < STEPS:
                    addition(n)

            def tile_mean_square(i):
                t0, nt, _, _ = TILES[i]
                pe.wait_ge(gla_sq, i + 1)
                if i + 2 < len(TILES):
                    pe.wait_ge(tok_ready, i + 3)
                else:
                    pe.wait_ge(attn_ready, len(TILES))
                    pe.wait_ge(gla_ss_kept, i)
                for h in range(GLA_HEADS):
                    ins = pe.matmul(acc[0:4, 1, 2 * P:2 * P + nt], gla_sum[:, h, :], q_half[:, h // 2, h % 2, t0:t0 + nt],
                                    start=(h == 0), stop=(h == GLA_HEADS - 1))
                ins.then_inc(gla_ss, 1)

            def gla_step(n):
                i, b = n // 8, n % 8
                if b == 2 and n < STEPS:
                    within(i)
                if 2 <= n < STEPS + 2:
                    from_state(n - 2)
                if b == 3 and i < SAMPLE:
                    turn_tile(i + 1)
                if (b == 5 and i) or n == STEPS + 3:
                    tile_mean_square(i - 1 if n < STEPS + 3 else SAMPLE)
                if b == 6 and i < SAMPLE:
                    if i:
                        pe.wait_ge(gla_ss_kept, i)
                    tile_scores(i + 1)

            def gla_spread_out(h):
                pe.wait_ge(gla_rstd, 1)
                if h >= 2:
                    pe.wait_ge(gla_in_ready, 2 + 2 * (h - 2) + 1)
                for half in range(2):
                    ins = pe.matmul(acc[:, 2 * (h % 2) + half, 0:HALF], gla_spread[0:4, h, :],
                                    rstd[0:4, HALF * half:HALF * (half + 1)], start=True, stop=True)
                ins.then_inc(gla_wide, 1)

            def turn(m):
                _, nq, nk, _ = TILES[tile_of(m)]
                pe.wait_ge(p_ready, m + 1)
                if m:
                    pe.wait_ge(pT_ready, m)
                for n in range(-(-nk // P)):
                    w = min(P, nk - P * n)
                    ins = pe.transpose(aux[0:w, 1, P * n:P * n + nq], tmp_a[0:nq, m % 2, P * n:P * n + w],
                                       ident[0:nq, 0:nq])
                ins.then_inc(pT_made, 1)

            def weigh(g):
                ti, kv = tile_of(PER_KV * g), g % KV_HEADS
                _, nq, nk, _ = TILES[ti]
                v = v_sample if ti == SAMPLE else v_prompt
                pe.wait_ge(pT_ready, PER_KV * (g + 1))
                if g:
                    pe.wait_ge(att_ready, g)
                last = -(-nk // P) - 1
                for n in range(last + 1):
                    w = min(P, nk - P * n)
                    if nq == P:
                        out, rhs = aux[HD * kv:HD * kv + HD, 2, :], probs_t[0:w, n, :, :].rearrange("p r q -> p (r q)")
                    else:
                        out = aux[HD * kv:HD * kv + HD, 2, :].rearrange("p (r q) -> p r q", r=4)[:, :, 0:nq]
                        rhs = probs_t[0:w, n, :, 0:nq]
                    ins = pe.matmul(out, v[0:w, n, HD * kv:HD * kv + HD], rhs, start=(n == 0), stop=(n == last))
                ins.then_inc(pv_made, 1)

            pe.wait_ge(gla_in_ready, 2)
            pe.wait_ge(z_ready, NZ + SPARE)
            turn_tile(0)
            tile_scores(0)
            pe.wait_ge(qk_ready, 5)

            def head_scores(m):
                ti, kv, r = tile_of(m), m % HEADS // PER_KV, m % PER_KV
                t0, nq, nk, _ = TILES[ti]
                rows = slice(HD * kv, HD * kv + HD)
                if m:
                    pe.wait_ge(s_biased, m)
                keys = kT_sample[rows, :] if ti == SAMPLE else z[rows, AK, 0:nk]
                pe.matmul(aux[0:nq, 0, 0:nk], z[rows, AQ + r, t0:t0 + nq], keys, start=True, stop=True).then_inc(s_made, 1)

            head_scores(0)
            for m in range(SLOTS + 1):
                for n in gla_steps(m)[:1]:
                    gla_addition(n)
                if m:
                    turn(m - 1)
                if m + 1 < SLOTS:
                    head_scores(m + 1)
                for n in gla_steps(m):
                    if n > gla_steps(m)[0]:
                        gla_addition(n)
                    gla_step(n)
                if m == NORM_SLOT + 2:
                    gla_spread_out(0)
                    gla_spread_out(1)
                if m and m % PER_KV == 0:
                    weigh(m // PER_KV - 1)
                if m == NORM_SLOT + 3:
                    gla_spread_out(2)
                    gla_spread_out(3)

            product_pair(WOUT, mix_ready, 0)
            with pe.Fori(1, KD // 2) as i:
                for j in range(2):
                    pe.wait_ge(x_added, i * 2 + (KD + j - 1 + SPARE))
                    product(i * 2 + (WOUT + j), j, j, h_hi, h_lo, range(KD))
            mean_square(2)
            ffn(2, FFN2, DOWN2)

        @block.vector
        def _(vec):
            steps = [0]
            for s in (x_added, g_full, g_ready, ada_step, ada_kept, top_taken):
                vec.sem_inc(s, SPARE)

            def mark(ins):
                steps[0] += 1
                ins.then_inc(vec_step, 1)
                return steps[0]

            def settle(ins):
                vec.wait_ge(vec_step, mark(ins))

            def modulate(n, scale_at):
                gain = gains[:, n, :].rearrange("p (k o) -> p k o", o=1).to_broadcast([P, KD, 2])
                settle(vec.tensor_scalar(scale[:, :, :], mod[:, scale_at:scale_at + KD, :], 1.0, None, ALU.add))
                vec.tensor_tensor(scale[:, :, :], scale[:, :, :], gain, ALU.mult).then_inc(mod_ready, 1)

            def out_gate(gate_at, factor):
                settle(vec.tensor_scalar(gate[:, :, :], mod[:, gate_at:gate_at + KD, :], factor, None, ALU.mult))

            def norm_rstd(n):
                for half in range(2):
                    vec.wait_ge(rms_ready, 2 * n + half + 1)
                    part = rstd[:, HALF * half:HALF * (half + 1)]
                    vec.reciprocal(part, part).then_inc(rstd_ready, 1)

            def norm(n):
                vec.wait_ge(rstd_ready, 2 * n + 2)
                vec.tensor_tensor(scaled_x[0], x[:, 0, :], rstd[:, :], ALU.mult).then_inc(scaled_first, 1)
                for k in range(KD):
                    vec.wait_ge(shifted, KD * n + k + 1)
                    rounded_h = mark(vec.tensor_copy(h_hi[:, k, :], tmp_b[:, k % 2, :]))
                    vec.wait_ge(vec_step, rounded_h)
                    vec.tensor_tensor(h_lo[:, k, :], tmp_b[:, k % 2, :], h_hi[:, k, :].bitcast(F32),
                                      ALU.subtract).then_inc(h_ready, 1)

            def pair(p):
                vec.wait_ge(ada_kept, p + SPARE)
                for j in range(2):
                    vec.wait_ge(ada_in[j], p * 16 + 16)
                    for s in range(2):
                        vec.wait_ge(ada_step, p * 4 + (2 * j + s + SPARE))
                        vec.tensor_tensor_reduce(unused_products, halves(ada[:, j, :]), halves(cond_all[:, s, :]), 1.0, 0.0,
                                                 ALU.mult, ALU.add, ada_part[:, 2 * j + s:2 * j + s + 1]).then_inc(ada_step, 1)
                vec.wait_ge(ada_step, p * 4 + (4 + SPARE))
                units = mod[:, bass.ds(p * 2 + 2 * KD, 2), :].rearrange("p u s -> p (u s)")
                vec.tensor_tensor(units, units, ada_part, ALU.add).then_inc(ada_kept, 1)

            def add_out(d, b, count, made):
                vec.wait_ge(used, made)
                a = accumulator(b)
                for lo, hi, s, last in ((0, HALF, 0, 0), (HALF, NPROMPT, 0, 0), (NPROMPT, T, 1, 1)):
                    part = a[:, lo // HALF, lo % HALF:lo % HALF + hi - lo]
                    xs = x[:, bass.ds(d, 1), lo:hi].rearrange("p o n -> p (o n)")
                    gs = gate[:, bass.ds(d, 1), s:s + 1].rearrange("p o n -> p (o n)")
                    ins = vec.scalar_tensor_tensor(xs, part, gs, xs, ALU.mult, ALU.add)
                    if last:
                        ins.then_inc(x_added, 1)
                    else:
                        ins.then_inc(x_part, 1)
                vec.wait_ge(x_added, count + (1 + SPARE))
                vec.wait_ge(x_part, count * 2 + 2)
                xs = x[:, bass.ds(d, 1), :].rearrange("p o n -> p (o n)")
                vec.tensor_tensor(tmp_b[:, b, :], xs, xs, ALU.mult).then_inc(square_made, 1)
                vec.wait_ge(square_made, count + 1)
                vec.wait_ge(sumsq_ready, count + KD)
                vec.tensor_tensor(sumsq[:, :], sumsq[:, :], tmp_b[:, b, :], ALU.add).then_inc(sumsq_ready, 1)

            def zero_sumsq():
                settle(vec.memset(sumsq[:, :], 0.0))

            def ffn(n, added):
                down_first = DOWN1 if n == 1 else DOWN2
                done = NF * (n - 1)
                def hidden(f):
                    if n == 1:
                        pair(f)
                    vec.wait_ge(silu_ready, f + (done + 1) + SPARE)
                    vec.wait_ge(used, f * 2 + ((FFN1 if n == 1 else FFN2) + 2 + CREDIT))
                    vec.wait_ge(g_ready, f + done + SPARE)
                    vec.tensor_tensor(halves(tmp_a[:, 1, :]), halves(tmp_a[:, 0, :]), accumulator(1), ALU.mult).then_inc(g_full, 1)
                    vec.wait_ge(g_full, f + (done + 1) + SPARE)
                    hi = g_hi[:, bass.ds(f, 1), :].rearrange("p o n -> p (o n)")
                    lo = g_lo[:, bass.ds(f, 1), :].rearrange("p o n -> p (o n)")
                    vec.tensor_copy(hi, tmp_a[:, 1, :]).then_inc(g_rounded, 1)
                    vec.wait_ge(g_rounded, f + (done + 1))
                    vec.tensor_tensor(lo, tmp_a[:, 1, :], hi.bitcast(F32), ALU.subtract).then_inc(g_ready, 1)

                with vec.Fori(0, NF // 2) as i:
                    for s in range(2):
                        hidden(i * 2 + s)
                if n == 1:
                    vec.wait_ge(ada_kept, NF + SPARE)
                out_gate(2 * KD if n == 1 else 8 * KD, 0.5)
                zero_sumsq()
                with vec.Fori(0, KD // 2) as i:
                    if n == 1:
                        pair(i + NF)
                    for j in range(2):
                        add_out(i * 2 + j, j, i * 2 + (added + j), i * 8 + (down_first + 4 * j + 4 + CREDIT))

            def start_unit(u):
                vec.wait_ge(rows_in[u // 2], 16)
                for s in range(2):
                    if u:
                        vec.wait_ge(start_step, 2 * u + s - 1)
                    vec.tensor_tensor_reduce(acc[:, 2 * s:2 * s + 2, :], halves(ada_rows[:, u, :]), halves(cond_all[:, s, :]),
                                             1.0, 0.0, ALU.mult, ALU.add, start_part[:, u, s:s + 1]).then_inc(start_step, 1)

            vec.wait_ge(cond_all_ready, 1)
            for u in range(KD):
                start_unit(u)
            vec.wait_ge(start_step, 2 * KD)
            vec.wait_ge(small_in, 32)
            settle(vec.tensor_tensor(mod[:, KD:2 * KD, :], mod[:, KD:2 * KD, :], start_part[:, :, :], ALU.add))
            modulate(0, KD)
            norm_rstd(0)
            vec.wait_ge(start_sum, 1)
            vec.tensor_tensor(mod[:, 0:KD, :], mod[:, 0:KD, :], aux[:, 2, 0:2 * KD].rearrange("p (u s) -> p u s", s=2),
                              ALU.add).then_inc(shift_ready, 1)
            norm(0)
            ffn(1, 0)
            vec.wait_ge(ada_kept, NF + KD // 2 + SPARE)
            modulate(1, 4 * KD)
            norm_rstd(1)
            norm(1)
            with vec.Fori(0, 2) as i:
                pair(i + (NF + KD // 2))

            vec.wait_ge(mixer_in, MIXER_LOADS)
            vec.wait_ge(z_ready, 4 + SPARE)
            mark(vec.tensor_copy(ikT_sample[:, PAST:LSAMPLE], z[:, IK, NPROMPT:T]))
            vec.wait_ge(vec_step, steps[0])
            vec.wait_ge(iw_ready, 1)
            for m in range(4 * IDX_HEADS):
                n, h = m // IDX_HEADS, m % IDX_HEADS
                _, nq, nk, _ = TILES[1 + n]
                vec.wait_ge(relu_ready, m + 1)
                weight = iw[0:nq, n, LOWRANK + h:LOWRANK + h + 1]
                if h == 0:
                    ins = vec.tensor_scalar(score[0:nq, n, 0:nk], tmp_a[0:nq, m % 2, 0:nk], weight, None, ALU.mult)
                else:
                    vec.wait_ge(logit_used, m)
                    ins = vec.scalar_tensor_tensor(score[0:nq, n, 0:nk], tmp_a[0:nq, m % 2, 0:nk], weight,
                                                   score[0:nq, n, 0:nk], ALU.mult, ALU.add)
                ins.then_inc(logit_used, 1)
            vec.wait_ge(logit_used, 4 * IDX_HEADS)
            for n in range(3):
                nk = TILES[1 + n][2]
                mark(vec.memset(score[0:64, n, nk - 64:nk], INADMISSIBLE))
            mark(vec.memset(bias0[:, :], 0.0))
            vec.wait_ge(vec_step, steps[0])
            settle(vec.memset(bias0[0:64, 64:P], DROPPED))

            def top_rounds(start, stop, tiles, before):
                each = len(tiles)
                with vec.Fori(start, stop) as i:
                    for q, n in enumerate(tiles):
                        _, nq, nk, _ = TILES[1 + n]
                        vec.wait_ge(top_taken, i * each + (before - start * each + q) + SPARE)
                        vec.sem_inc(tick, 1)
                        vec.max(top[0:nq, q, :], score[0:nq, n, 0:nk]).then_inc(top_found, 1)
                        vec.wait_ge(top_found, i * each + (before - start * each + q + 1))
                        vec.sem_inc(tick, 1)
                        vec.match_replace(score[0:nq, n, 0:nk], top[0:nq, q, :], score[0:nq, n, 0:nk], TAKEN).then_inc(top_taken, 1)

            rounds_s, rounds_p = TILES[SAMPLE][3], TILES[1][3]
            together = (3, 0, 1, 2)
            top_rounds(0, 3, together, 0)
            vec.wait_ge(log_ready, 1)
            settle(vec.tensor_scalar(exp_q[:, :, :], exp_q[:, :, :], 0.0, None, ALU.min))
            settle(vec.tensor_tensor(exp_q[:, :, :], exp_q[:, :, :], exp_k[:, :, :], ALU.subtract))
            for j in range(2):
                settle(vec.tensor_tensor_scan(decay[:, j, :], c("carry"), exp_q[:, j, :], 0.0, ALU.mult, ALU.add))
            vec.sem_inc(decay_ready, 1)
            blocks = decay[:, :, :].rearrange("p j (b n) -> p j b n", n=GBLOCK)
            for j in range(2):
                ins = vec.tensor_tensor(exp_end[:, j, :].rearrange("p (b n) -> p b n", n=GBLOCK),
                                        blocks[:, j, :, GBLOCK - 1:GBLOCK].to_broadcast([P, T // GBLOCK, GBLOCK]),
                                        blocks[:, j, :, :], ALU.subtract)
                settle(ins)
            vec.sem_inc(decay_ready, 1)
            top_rounds(3, 6, together, 4 * 3)
            vec.wait_ge(z_ready, AQ + 4 + SPARE)
            tiles = [AK, AQ, AQ + 1, AQ + 2, AQ + 3]
            for j, n in enumerate(tiles):
                if j == 4:
                    vec.wait_ge(qk_ss, 1)
                vec.tensor_tensor((tmp_a if j % 4 < 2 else tmp_b)[:, j % 2, :], z[:, n, :], z[:, n, :], ALU.mult).then_inc(qk_sq, 1)
            top_rounds(6, rounds_s, together, 4 * 6)
            vec.wait_ge(qk_rms, 1)
            settle(vec.reciprocal(rstd[0:10, :], rstd[0:10, :]))
            vec.sem_inc(qk_rstd, 1)
            top_rounds(rounds_s, rounds_s + 3, (0, 1, 2), 4 * rounds_s)
            settle(vec.tensor_scalar(gain_q8, gain_q, HD ** -0.5, None, ALU.mult))
            for j, n in enumerate(tiles):
                if j == 2:
                    top_rounds(rounds_s + 3, rounds_p, (0, 1, 2), 4 * rounds_s + 9)
                vec.wait_ge(qk_wide, j + 1)
                vec.scalar_tensor_tensor(halves(z[:, n, :]), halves(z[:, n, :]), gain_k if j == 0 else gain_q8,
                                         wide(j % 2), ALU.mult, ALU.mult).then_inc(qk_ready, 1)
            vec.wait_ge(qk_ready, 5)
            mark(vec.tensor_copy(kT_sample[:, PAST:LSAMPLE], z[:, AK, NPROMPT:T]))
            vec.wait_ge(exp_ready, 4)
            vec.wait_ge(z_ready, GV + SPARE)
            for j in range(2):
                mark(vec.scalar_tensor_tensor(z[:, GQ + j, :], z[:, GQ + j, :], GLA_DK ** -0.5, exp_q[:, j, :], ALU.mult, ALU.mult))
                mark(vec.tensor_tensor(k_dec[:, j, :], z[:, GK + j, :], exp_k[:, j, :], ALU.mult))
                vec.wait_ge(vec_step, steps[0])
                vec.tensor_tensor(z[:, GK + j, :], z[:, GK + j, :], exp_end[:, j, :], ALU.mult).then_inc(gla_in_ready, 1)
            vec.wait_ge(gla_in_ready, 2)
            mark(vec.memset(state[:, :, 0, :], 0.0))
            vec.wait_ge(vec_step, steps[0])
            vec.sem_inc(s_first, 1)

            vec.wait_ge(top_taken, 4 * rounds_s + 3 * (rounds_p - rounds_s) + SPARE)

            def selection(i):
                _, nq, nk, _ = TILES[i]
                settle(vec.tensor_scalar(score[0:nq, i - 1, 0:nk], score[0:nq, i - 1, 0:nk], 0.5 * (INADMISSIBLE + TAKEN), DROPPED,
                                         ALU.is_gt, ALU.mult))

            def tile_mask(i):
                _, nt, _, _ = TILES[i]
                vec.wait_ge(attn_made, i + 1)
                if i >= 2:
                    vec.wait_ge(inter_made, 8 * (i - 1))
                mask = c("causal", nt)[:, 0:nt].bitcast(I32).rearrange("p (o n) -> p o n", o=1).to_broadcast([nt, 2, nt])
                for r in range(2):
                    ins = vec.copy_predicated(attn[0:nt, i % 2, r:4:2, 0:nt], mask,
                                              acc[0:nt, r, 0:2 * P].rearrange("p (h n) -> p h n", h=2)[:, :, 0:nt])
                ins.then_inc(attn_ready, 1)

            def new_state(n):
                if n == NPROMPT // GBLOCK:
                    vec.wait_ge(inter_made, first_free(n))
                    settle(vec.tensor_copy(state[:, :, state_slot(n), :], state_in[:, :, :]))
                    vec.sem_inc(s_first, 1)
                elif n:
                    vec.wait_ge(s_ready, n)
                vec.wait_ge(u_made, n + 1)
                if first_free(n) > 0:
                    vec.wait_ge(inter_made, first_free(n))
                old, new = state_slot(n), (state_slot(n) + 1) % 9
                for j in range(2):
                    ins = vec.scalar_tensor_tensor(state[:, j, new, :], state[:, j, old, :], etot[:, j, n:n + 1],
                                                   aux[:, 3, P * j:P * j + P], ALU.mult, ALU.add)
                ins.then_inc(s_ready, 1)

            def gla_step(n):
                if n < STEPS:
                    new_state(n)
                if (n % 8 == 4 and n >= 8) or n == STEPS + 3:
                    tile_squares(n // 8 - 1 if n < STEPS + 3 else SAMPLE)
                if n % 8 == 7 and n // 8 < SAMPLE:
                    tile_mask(n // 8 + 1)

            def tile_squares(i):
                t0, nt, _, _ = TILES[i]
                vec.wait_ge(o_ready, i + 1)
                vec.tensor_tensor(q_half[:, :, :, t0:t0 + nt].rearrange("p j r n -> p (j r) n"), z[:, GV:GV + 4, t0:t0 + nt],
                                  z[:, GV:GV + 4, t0:t0 + nt], ALU.mult).then_inc(gla_sq, 1)

            def gla_finish(h):
                vec.wait_ge(gla_wide, h + 1)
                vec.wait_ge(z_ready, NZ + SPARE)
                vec.scalar_tensor_tensor(halves(z[:, GV + h, :]), halves(z[:, GV + h, :]), gain_gla,
                                         accumulator(h % 2), ALU.mult, ALU.mult).then_inc(gla_in_ready, 1)
                vec.wait_ge(gla_in_ready, 2 + 2 * h + 1)
                vec.tensor_tensor(z[:, GV + h, :], z[:, GV + h, :], z[:, GR + h, :], ALU.mult).then_inc(gla_in_ready, 1)

            def scaled_probs(m):
                _, nq, _, _ = TILES[tile_of(m)]
                nk = TILES[tile_of(m)][2]
                vec.wait_ge(p_exp, m + 1)
                settle(vec.reciprocal(stats[0:nq, m % 2, 3:4], stats[0:nq, m % 2, 2:3]))
                vec.tensor_scalar(tmp_a[0:nq, m % 2, 0:nk], tmp_a[0:nq, m % 2, 0:nk], stats[0:nq, m % 2, 3:4], None,
                                  ALU.mult).then_inc(p_ready, 1)

            vec.wait_ge(attn_zero, 1)
            tile_mask(0)

            def slanted_bias(m):
                ti = tile_of(m)
                if m % HEADS == 0 and ti:
                    selection(ti)
                _, nq, nk, _ = TILES[ti]
                first_dist = 384 - (P * ti if ti != SAMPLE else PAST)
                dist = c("dist", nq)[:, first_dist:first_dist + nk]
                dropped = bias0[0:nq, 0:nk] if ti == 0 else score[0:nq, ti - 1, 0:nk]
                return mark(vec.scalar_tensor_tensor(tmp_b[0:nq, m % 2, 0:nk], dist, -(2.0 ** -(m % HEADS + 1)), dropped,
                                                     ALU.mult, ALU.add))

            slanted = slanted_bias(0)
            for m in range(SLOTS + 1):
                if m:
                    scaled_probs(m - 1)
                if m < SLOTS:
                    _, nq, nk, _ = TILES[tile_of(m)]
                    vec.wait_ge(vec_step, slanted)
                    vec.wait_ge(s_made, m + 1)
                    if m >= 2:
                        vec.wait_ge(pT_made, m - 1)
                    settle(vec.tensor_tensor_reduce(tmp_a[0:nq, m % 2, 0:nk], aux[0:nq, 0, 0:nk], tmp_b[0:nq, m % 2, 0:nk],
                                                    1.0, TAKEN, ALU.add, ALU.max, stats[0:nq, m % 2, 0:1]))
                    vec.tensor_scalar(stats[0:nq, m % 2, 1:2], stats[0:nq, m % 2, 0:1], -1.0, None, ALU.mult).then_inc(s_biased, 1)
                if m + 1 < SLOTS:
                    slanted = slanted_bias(m + 1)
                for n in gla_steps(m):
                    gla_step(n)
                if m == NORM_SLOT + 1:
                    vec.wait_ge(gla_rms, 1)
                    settle(vec.reciprocal(rstd[0:4, :], rstd[0:4, :]))
                    vec.sem_inc(gla_rstd, 1)
                if m in (NORM_SLOT + 3, NORM_SLOT + 4):
                    for h in range(2):
                        gla_finish(h + (0 if m == NORM_SLOT + 3 else 2))

            for k in range(KD):
                source = z[:, GV + k, :] if k < 4 else z[:, AQ + k - 4, :]
                vec.wait_ge(mix_rounded, k + 1)
                vec.tensor_tensor(h_lo[:, k, :], source, h_hi[:, k, :].bitcast(F32), ALU.subtract).then_inc(mix_ready, 1)
            out_gate(5 * KD, 1.0)
            zero_sumsq()
            with vec.Fori(0, KD // 2) as i:
                for j in range(2):
                    add_out(i * 2 + j, j, i * 2 + (KD + j), i * 2 + (WOUT + j + 1 + CREDIT))
            modulate(2, 7 * KD)
            norm_rstd(2)
            norm(2)
            vec.wait_ge(stored, 16 * 5)
            ffn(2, 2 * KD)
            norm_rstd(3)
            vec.wait_ge(rstd_ready, 8)
            for k in Y_VECTOR:
                vec.scalar_tensor_tensor(y[:, k, :], x[:, k, :], gains[:, 3, k:k + 1], rstd[:, :], ALU.mult, ALU.mult).then_inc(y_ready, 1)


def constants():
    p = np.arange(P)
    out = np.zeros((P, NCONST), np.float32)

    def put(name, value, rows=P):
        a, w = CONST_AT[name]
        out[0:rows, a:a + w] = np.asarray(value, np.float32).reshape(rows, w)

    put("ident", np.eye(P))
    put("causal", (p[:, None] // GBLOCK == p[None, :] // GBLOCK) & (p[:, None] <= p[None, :]))
    put("block", p[:, None] // GBLOCK == np.arange(8)[None, :])
    put("carry", np.tile(np.arange(T) % GBLOCK != 0, (P, 1)))
    put("dist", np.abs(np.arange(512)[None, :] - 384 - p[:, None]))
    row = np.arange(10)
    tile = np.arange(5)
    belongs = row[None, None, :] == 2 * tile[None, :, None] + p[:, None, None] // HD
    put("qk_sum", belongs)
    put("qk_spread", belongs.transpose(2, 1, 0), 10)
    head = np.arange(4)
    own = np.broadcast_to(head[None, :, None] == head[None, None, :], (P, 4, 4))
    put("gla_sum", own)
    put("gla_spread", own.transpose(2, 1, 0), 4)
    return out


INPUTS = {
    "x": (P, KD, T), "cond": (P, KD, 2), "cond_row": (1, 2 * D), "b_ada": (P, 9 * KD, 2), "gains": (P, 4, KD), "small": (P, 6), "const": (P, NCONST),
    "w_ada_units": (P, KD, D), "w_ada_rows": (8 * KD, P, D), "w_in": (NZ, P, D), "w_a2": (LOWRANK, 2 * P),
    "w_out": (KD, P, D), "w1_gate": (NF, P, D), "w1_up": (NF, P, D), "w1_down": (KD, P, DFF),
    "w2_gate": (NF, P, D), "w2_up": (NF, P, D), "w2_down": (KD, P, DFF),
    "cache_kT": (P, PAST), "cache_ikT": (P, PAST), "cache_v": (P, 2, P), "state": (P, 2, GLA_DV),
}
OUTPUTS = {"yT": (P, KD, T), "kT": (P, T), "vT": (P, T), "ikT": (HD, T), "state_prompt": (P, 2, GLA_DV),
           "state_sample": (P, 2, GLA_DV)}


def laid_out(v):
    v = {n: np.asarray(a) for n, a in v.items()}

    def units(w):
        k, n = w.shape
        return w.reshape(k // P, P, n // P, P).transpose(2, 1, 0, 3).reshape(n // P, P, k)

    def by_partition(a):
        return a.reshape(-1, P).T

    out = {}
    x = np.concatenate([v["x_prompt"][0], v["x_sample"][0]])
    out["x"] = x.T.reshape(KD, P, T).transpose(1, 0, 2)
    c = np.stack([v["c_prompt"][0], v["c_sample"][0]])
    out["cond"] = c.T.reshape(KD, P, 2).transpose(1, 0, 2)
    out["cond_row"] = c.reshape(1, 2 * D)
    out["b_ada"] = np.repeat(by_partition(v["b_ada"][0])[:, :, None], 2, axis=2)
    out["gains"] = np.stack([by_partition(v[n][0]) for n in ("g_ffn1", "g_mix", "g_ffn2", "g_out")], axis=1)
    b_a = by_partition(v["b_a"][0])
    out["small"] = np.stack([np.tile(v["g_q"][0], 2), np.tile(v["g_k"][0], 2), v["g_gla"][0],
                             np.zeros(P, np.float32), b_a[:, 0], b_a[:, 1]], axis=1)
    out["const"] = constants()
    out["w_ada_units"] = units(v["w_ada"][0][:, :KD * P]).transpose(1, 0, 2)
    out["w_ada_rows"] = v["w_ada"][0].T.reshape(9 * KD, P, D)[KD:]
    sizes = (256, 256, 512, LOWRANK, 512, 512, 128, 128, 256, 64, 4)
    gq, gk, gv, ga, gr, aq, ak, av, iq, ik, iw = np.split(v["w_in"][0], np.cumsum(sizes)[:-1], axis=1)
    paired = aq.reshape(D, KV_HEADS, PER_KV, HD).transpose(0, 2, 1, 3).reshape(D, HEADS * HD)
    padding = np.zeros((D, P - LOWRANK - IDX_HEADS), np.float32)
    out["w_in"] = units(np.concatenate([iq, ik, ik, ga, iw, padding, ak, av, paired, gq, gk, gv, gr], axis=1))
    out["w_a2"] = v["w_a2"][0]
    w_out = v["w_out"][0]
    att = w_out[512:].reshape(KV_HEADS, PER_KV, HD, D).transpose(1, 0, 2, 3).reshape(512, D)
    out["w_out"] = units(np.concatenate([w_out[:512], att]))
    for n in ("w1_gate", "w1_up", "w1_down", "w2_gate", "w2_up", "w2_down"):
        out[n] = units(v[n][0])
    out["cache_kT"] = v["cache_k"][0, 0].reshape(PAST, P).T
    ik_past = v["cache_idx_k"][0, 0].T
    out["cache_ikT"] = np.concatenate([ik_past, ik_past])
    out["cache_v"] = v["cache_v"][0, 0].reshape(2, P, P).transpose(1, 0, 2)
    out["state"] = v["state_gla"][0, 0].reshape(2, P, GLA_DV).transpose(1, 0, 2)
    return {n: np.ascontiguousarray(out[n]) for n in INPUTS}


def kernel(**inputs):
    import concourse.bacc as bacc
    from concourse.bass_utils import run_bass_kernel_spmd

    nc = bacc.Bacc("TRN2", target_bir_lowering=False, num_devices=1)
    given = {n: nc.dram_tensor(f"{n}_in", shape, F32, kind="ExternalInput").ap() for n, shape in INPUTS.items()}
    made = {n: nc.dram_tensor(f"{n}_out", shape, F32, kind="ExternalOutput").ap() for n, shape in OUTPUTS.items()}
    program(nc, given, made)
    r = run_bass_kernel_spmd(nc, [{f"{n}_in": a for n, a in laid_out(inputs).items()}], core_ids=[0]).results[0]

    y = r["yT_out"].transpose(2, 1, 0).reshape(T, D)
    k, v = (r[n].T.reshape(T, KV_HEADS, HD) for n in ("kT_out", "vT_out"))
    ik = r["ikT_out"].T
    first, second = (r[n].transpose(1, 0, 2).reshape(1, 1, GLA_HEADS, GLA_DK, GLA_DV)
                     for n in ("state_prompt_out", "state_sample_out"))
    a, b = slice(0, NPROMPT), slice(NPROMPT, T)
    return (y[a][None], y[b][None], k[a][None, None], v[a][None, None], ik[a][None, None], first,
            k[b][None, None], v[b][None, None], ik[b][None, None], second)
```
